# Optimizing a Trainium2 kernel written in Bass

```python
import jax, jax.numpy as jnp
from jax import lax
import numpy as np

D_MODEL = 1024
BATCH = 1
SEQ = 1024
DEPTH = 2
DEC_BATCH = 8
DEC_SEQ = 16
PAST_LEN = 256

CHUNK = 64
N_EVEN = (DEPTH + 1) // 2
N_ODD = DEPTH // 2
EPS = 1e-6
F32 = jnp.float32

FOX_HEADS = 8
FOX_HEAD_DIM = 64
FOX_WIDTH = FOX_HEADS * FOX_HEAD_DIM
FOX_QBLOCK = 128
FOX_F_BIAS = 4.0
ML_HEADS = 4
ML_HEAD_DIM = 128
ML_WIDTH = ML_HEADS * ML_HEAD_DIM
ML_CONV = 4
ML_F_BIAS = 3.0
GLA_HEADS = 4
GLA_DK = 128
GLA_DV = 256
GLA_KW = GLA_HEADS * GLA_DK
GLA_VW = GLA_HEADS * GLA_DV
GLA_RANK = 16
GLA_TAU = 16.0
D_FF = 4 * D_MODEL

EVEN_SPLITS = (FOX_WIDTH, FOX_WIDTH, FOX_WIDTH, FOX_HEADS,
               2 * ML_WIDTH, ML_WIDTH, ML_WIDTH, ML_HEADS, ML_HEADS)
EVEN_IN = 3 * FOX_WIDTH + FOX_HEADS + 4 * ML_WIDTH + 2 * ML_HEADS
ODD_SPLITS = (GLA_KW, GLA_KW, GLA_VW, GLA_VW, GLA_RANK)
ODD_IN = 2 * GLA_KW + 2 * GLA_VW + GLA_RANK

kernel_name = "fox_mlstm_gla_streaming_step"

def _rmsnorm(x, g):
    xf = x.astype(F32)
    y = xf * lax.rsqrt(jnp.mean(xf * xf, axis=-1, keepdims=True) + EPS)
    return (y * g.astype(F32)).astype(x.dtype)

def _head_rmsnorm(h, g):
    B, T, H, Dh = h.shape
    hf = h.astype(F32)
    y = hf * lax.rsqrt(jnp.mean(hf * hf, axis=-1, keepdims=True) + EPS)
    return (y * g.reshape(H, Dh).astype(F32)).reshape(B, T, H * Dh)

def _split(z, sizes):
    return jnp.split(z, np.cumsum(sizes)[:-1].tolist(), axis=-1)

def _heads(a, n):
    return a.reshape(a.shape[0], a.shape[1], n, -1)

def _to_chunks(a, L):
    B, T = a.shape[:2]
    return jnp.moveaxis(a.reshape(B, T // L, L, *a.shape[2:]), 1, 0)

def _from_chunks(a):
    nc, B, L = a.shape[:3]
    return jnp.moveaxis(a, 0, 1).reshape(B, nc * L, *a.shape[3:])

def _causal_dwconv(u, buf, w, b):
    full = jnp.concatenate([buf.astype(u.dtype), u], axis=1)
    y = lax.conv_general_dilated(full, w[:, None, :].astype(u.dtype), window_strides=(1,),
                                 padding='VALID', dimension_numbers=('NWC', 'WIO', 'NWC'),
                                 feature_group_count=u.shape[-1])
    return y + b.astype(u.dtype), full[:, -(ML_CONV - 1):]

def _fox(q, k, v, logf, past_k, past_v, past_logf):
    B, T, H, Dh = q.shape
    P = past_k.shape[1]
    k_all = jnp.concatenate([past_k.astype(k.dtype), k], axis=1)
    v_all = jnp.concatenate([past_v.astype(v.dtype), v], axis=1)
    lf_all = jnp.concatenate([past_logf.astype(F32), logf], axis=1)
    Fk = jnp.cumsum(lf_all, axis=1).transpose(0, 2, 1)
    kpos = jnp.arange(P + T)
    qb = min(FOX_QBLOCK, T)
    nb = T // qb
    q_blocks = q.reshape(B, nb, qb, H, Dh).swapaxes(0, 1)
    Fq_blocks = Fk[:, :, P:].reshape(B, H, nb, qb).transpose(2, 0, 1, 3)
    qpos_blocks = (P + jnp.arange(T)).reshape(nb, qb)
    scale = FOX_HEAD_DIM ** -0.5

    def attend(args):
        qblk, Fq, qpos = args
        s = jnp.einsum('bqhd,bkhd->bhqk', qblk, k_all).astype(F32) * scale
        s = s + Fq[..., :, None] - Fk[..., None, :]
        s = jnp.where(kpos[None, :] <= qpos[:, None], s, -jnp.inf)
        p = jax.nn.softmax(s, axis=-1).astype(v_all.dtype)
        return jnp.einsum('bhqk,bkhd->bqhd', p, v_all)

    o = lax.map(attend, (q_blocks, Fq_blocks, qpos_blocks))
    return o.swapaxes(0, 1).reshape(B, T, H * Dh)

def _mlstm(q, k, v, i_pre, f_pre, C0, n0, m0):
    B, T, H, Dh = q.shape
    L = min(CHUNK, T)
    q, k, v = q.astype(F32), k.astype(F32), v.astype(F32)
    log_f = jax.nn.log_sigmoid(f_pre.astype(F32))
    i_pre = i_pre.astype(F32)
    causal = jnp.tril(jnp.ones((L, L), dtype=bool))

    def step(carry, inp):
        C, n, m = carry
        qc, kc, vc, ic, lfc = inp
        b = jnp.cumsum(lfc, axis=1).transpose(0, 2, 1)
        ic = ic.transpose(0, 2, 1)
        dmat = jnp.where(causal, b[..., :, None] - b[..., None, :] + ic[..., None, :], -jnp.inf)
        inter = b + m[..., None]
        m_t = jnp.maximum(inter, jnp.max(dmat, axis=-1))
        w = jnp.exp(dmat - m_t[..., None])
        g = jnp.exp(inter - m_t)
        a = w * jnp.einsum('bthd,bshd->bhts', qc, kc)
        num = g[..., None] * jnp.einsum('bhed,bthd->bhte', C, qc) + jnp.einsum('bhts,bshe->bhte', a, vc)
        den = g * jnp.einsum('bhd,bthd->bht', n, qc) + jnp.sum(a, axis=-1)
        h = num / jnp.maximum(jnp.abs(den), jnp.exp(-m_t))[..., None]
        w_end, g_end = w[..., -1, :], g[..., -1]
        C_new = g_end[..., None, None] * C + jnp.einsum('bhs,bshe,bshd->bhed', w_end, vc, kc)
        n_new = g_end[..., None] * n + jnp.einsum('bhs,bshd->bhd', w_end, kc)
        return (C_new, n_new, m_t[..., -1]), h.transpose(0, 2, 1, 3)

    xs = tuple(_to_chunks(a, L) for a in (q, k, v, i_pre, log_f))
    (C, n, m), h = lax.scan(step, (C0.astype(F32), n0.astype(F32), m0.astype(F32)), xs)
    return _from_chunks(h), C, n, m

def _gla(q, k, v, log_a, S0):
    B, T, H, DK = q.shape
    L = min(CHUNK, T)
    causal = jnp.tril(jnp.ones((L, L), dtype=bool))[None, :, :, None, None]

    def step(S, inp):
        qc, kc, vc, lac = inp
        cb = jnp.cumsum(lac, axis=1)
        decay = jnp.exp(jnp.where(causal, cb[:, :, None] - cb[:, None, :], -jnp.inf))
        a = jnp.einsum('btshk,bshk->bhts', qc[:, :, None] * decay, kc)
        o = jnp.einsum('bthk,bhkv->bthv', qc * jnp.exp(cb), S) + jnp.einsum('bhts,bshv->bthv', a, vc)
        cl = cb[:, -1]
        S_new = jnp.exp(cl)[..., None] * S + jnp.einsum('bshk,bshv->bhkv', kc * jnp.exp(cl[:, None] - cb), vc)
        return S_new, o

    xs = tuple(_to_chunks(a, L) for a in (q, k, v, log_a))
    S, o = lax.scan(step, S0.astype(F32), xs)
    return _from_chunks(o), S

def _even_mixer(h, w_in, b_fox_f, conv_w, conv_b, b_i, b_f, g_ml,
                fk_past, fv_past, flf_past, C0, n0, m0, buf):
    z = h @ w_in
    fq, fk, fv, ff, mqk, mv, mo, mi, mf = _split(z, EVEN_SPLITS)
    f_logf = jax.nn.log_sigmoid(ff.astype(F32) + b_fox_f.astype(F32))
    k_f, v_f = _heads(fk, FOX_HEADS), _heads(fv, FOX_HEADS)
    attn = _fox(_heads(fq, FOX_HEADS), k_f, v_f, f_logf, fk_past, fv_past, flf_past)
    qk, new_buf = _causal_dwconv(mqk, buf, conv_w, conv_b)
    mq, mk = jnp.split(jax.nn.silu(qk), 2, axis=-1)
    h_ml, C, n, m = _mlstm(_heads(mq, ML_HEADS), _heads(mk, ML_HEADS) * (ML_HEAD_DIM ** -0.5),
                           _heads(mv, ML_HEADS), mi + b_i, mf + b_f, C0, n0, m0)
    h_ml = _head_rmsnorm(h_ml, g_ml) * jax.nn.sigmoid(mo.astype(F32))
    mix = jnp.concatenate([attn, h_ml.astype(h.dtype)], axis=-1)
    return mix, (k_f, v_f, f_logf, C, n, m, new_buf)

def _odd_mixer(h, w_in, w_a2, b_a, g_gla, S0):
    z = h @ w_in
    gq, gk, gv, gg, ga = _split(z, ODD_SPLITS)
    log_a = jax.nn.log_sigmoid((ga @ w_a2 + b_a).astype(F32)) / GLA_TAU
    q = _heads(gq, GLA_HEADS).astype(F32) * (GLA_DK ** -0.5)
    o, S = _gla(q, _heads(gk, GLA_HEADS).astype(F32), _heads(gv, GLA_HEADS).astype(F32),
                _heads(log_a, GLA_HEADS), S0)
    o = _head_rmsnorm(o, g_gla) * jax.nn.silu(gg.astype(F32))
    return o.astype(h.dtype), S

def _trunk(x, fox_k, fox_v, fox_lf, ml_c, ml_n, ml_m, ml_buf, gla_s,
           norm_mix, norm_ffn, norm_final, w_in_even, b_fox_f, conv_w_ml, conv_b_ml,
           b_ml_i, b_ml_f, g_ml, w_in_odd, w_gla_a2, b_gla_a, g_gla, w_out, w_ff1, w_ff2):
    even_states, odd_states = [], []
    for layer in range(DEPTH):
        h = _rmsnorm(x, norm_mix[layer])
        j = layer // 2
        if layer % 2 == 0:
            mix, st = _even_mixer(h, w_in_even[j], b_fox_f[j], conv_w_ml[j], conv_b_ml[j],
                                  b_ml_i[j], b_ml_f[j], g_ml[j], fox_k[j], fox_v[j], fox_lf[j],
                                  ml_c[j], ml_n[j], ml_m[j], ml_buf[j])
            even_states.append(st)
        else:
            mix, S = _odd_mixer(h, w_in_odd[j], w_gla_a2[j], b_gla_a[j], g_gla[j], gla_s[j])
            odd_states.append(S)
        x = x + mix @ w_out[layer]
        h = _rmsnorm(x, norm_ffn[layer])
        x = x + jnp.square(jax.nn.relu(h @ w_ff1[layer])) @ w_ff2[layer]
    y = _rmsnorm(x, norm_final)
    dt = x.dtype
    ev = [jnp.stack([s[i] for s in even_states]).astype(dt) for i in range(7)]
    return y, ev, jnp.stack(odd_states).astype(dt)

def setup_inputs(seed: int = 0) -> dict:
    key = jax.random.key(seed)
    ks = iter(jax.random.split(key, 32))

    def nrm(shape, scale=1.0):
        return jax.random.normal(next(ks), shape, F32) * scale

    D = D_MODEL
    return {
        "x_prompt": nrm((BATCH, SEQ, D)),
        "x_sample": nrm((DEC_BATCH, DEC_SEQ, D)),
        "cache_fox_k": nrm((N_EVEN, DEC_BATCH, PAST_LEN, FOX_HEADS, FOX_HEAD_DIM)),
        "cache_fox_v": nrm((N_EVEN, DEC_BATCH, PAST_LEN, FOX_HEADS, FOX_HEAD_DIM)),
        "cache_fox_logf": jax.nn.log_sigmoid(FOX_F_BIAS + nrm((N_EVEN, DEC_BATCH, PAST_LEN, FOX_HEADS))),
        "state_mlstm_c": nrm((N_EVEN, DEC_BATCH, ML_HEADS, ML_HEAD_DIM, ML_HEAD_DIM), 0.5),
        "state_mlstm_n": nrm((N_EVEN, DEC_BATCH, ML_HEADS, ML_HEAD_DIM), 0.5),
        "state_mlstm_m": nrm((N_EVEN, DEC_BATCH, ML_HEADS)),
        "state_mlstm_conv": nrm((N_EVEN, DEC_BATCH, ML_CONV - 1, 2 * ML_WIDTH)),
        "state_gla_s": nrm((N_ODD, DEC_BATCH, GLA_HEADS, GLA_DK, GLA_DV)),
        "norm_mix": 1.0 + nrm((DEPTH, D), 0.05),
        "norm_ffn": 1.0 + nrm((DEPTH, D), 0.05),
        "norm_final": 1.0 + nrm((D,), 0.05),
        "w_in_even": nrm((N_EVEN, D, EVEN_IN), D ** -0.5),
        "b_fox_f": FOX_F_BIAS + nrm((N_EVEN, FOX_HEADS), 0.5),
        "conv_w_ml": nrm((N_EVEN, ML_CONV, 2 * ML_WIDTH), ML_CONV ** -0.5),
        "conv_b_ml": nrm((N_EVEN, 2 * ML_WIDTH), 0.02),
        "b_ml_i": nrm((N_EVEN, ML_HEADS), 0.1),
        "b_ml_f": ML_F_BIAS + nrm((N_EVEN, ML_HEADS), 0.5),
        "g_ml": 1.0 + nrm((N_EVEN, ML_WIDTH), 0.05),
        "w_in_odd": nrm((N_ODD, D, ODD_IN), D ** -0.5),
        "w_gla_a2": nrm((N_ODD, GLA_RANK, GLA_KW), GLA_RANK ** -0.5),
        "b_gla_a": nrm((N_ODD, GLA_KW), 0.02),
        "g_gla": 1.0 + nrm((N_ODD, GLA_VW), 0.05),
        "w_out": nrm((DEPTH, D, D), D ** -0.5),
        "w_ff1": nrm((DEPTH, D, D_FF), D ** -0.5),
        "w_ff2": nrm((DEPTH, D_FF, D), D_FF ** -0.5),
    }

def reference(x_prompt, x_sample, cache_fox_k, cache_fox_v, cache_fox_logf, state_mlstm_c,
              state_mlstm_n, state_mlstm_m, state_mlstm_conv, state_gla_s,
              norm_mix, norm_ffn, norm_final, w_in_even, b_fox_f, conv_w_ml, conv_b_ml,
              b_ml_i, b_ml_f, g_ml, w_in_odd, w_gla_a2, b_gla_a, g_gla, w_out, w_ff1, w_ff2):
    params = (norm_mix, norm_ffn, norm_final, w_in_even, b_fox_f, conv_w_ml, conv_b_ml,
              b_ml_i, b_ml_f, g_ml, w_in_odd, w_gla_a2, b_gla_a, g_gla, w_out, w_ff1, w_ff2)
    B, dt = x_prompt.shape[0], x_prompt.dtype
    z_fk = jnp.zeros((N_EVEN, B, 0, FOX_HEADS, FOX_HEAD_DIM), dt)
    z_flf = jnp.zeros((N_EVEN, B, 0, FOX_HEADS), dt)
    z_c = jnp.zeros((N_EVEN, B, ML_HEADS, ML_HEAD_DIM, ML_HEAD_DIM), dt)
    z_n = jnp.zeros((N_EVEN, B, ML_HEADS, ML_HEAD_DIM), dt)
    z_m = jnp.zeros((N_EVEN, B, ML_HEADS), dt)
    z_buf = jnp.zeros((N_EVEN, B, ML_CONV - 1, 2 * ML_WIDTH), dt)
    z_s = jnp.zeros((N_ODD, B, GLA_HEADS, GLA_DK, GLA_DV), dt)
    y_prompt, p_ev, p_gla_s = _trunk(x_prompt, z_fk, z_fk, z_flf, z_c, z_n, z_m, z_buf, z_s, *params)
    p_fox_k, p_fox_v, p_fox_logf, p_mlstm_c, p_mlstm_n, p_mlstm_m, p_mlstm_conv = p_ev
    y_sample, s_ev, s_gla_s = _trunk(x_sample, cache_fox_k, cache_fox_v, cache_fox_logf, state_mlstm_c,
                                     state_mlstm_n, state_mlstm_m, state_mlstm_conv, state_gla_s, *params)
    s_fox_k, s_fox_v, s_fox_logf, s_mlstm_c, s_mlstm_n, s_mlstm_m, s_mlstm_conv = s_ev
    return (y_prompt, y_sample,
            p_fox_k, p_fox_v, p_fox_logf, p_mlstm_c, p_mlstm_n, p_mlstm_m, p_mlstm_conv, p_gla_s,
            s_fox_k, s_fox_v, s_fox_logf, s_mlstm_c, s_mlstm_n, s_mlstm_m, s_mlstm_conv, s_gla_s)


_drawn_inputs = setup_inputs


def setup_inputs(seed=0):
    import zlib

    import numpy as np

    out = dict(_drawn_inputs(seed))
    spreads = {}
    factors = {'cache_fox_logf': 2.783, 'b_gla_a': 5.824, 'g_gla': 3.23}
    for name, (base, spread) in spreads.items():
        noise = np.random.default_rng([zlib.crc32(name.encode()), seed]).standard_normal(out[name].shape)
        drawn = base * np.exp(spread * noise) if base else spread * noise
        out[name] = __import__('jax').numpy.asarray(drawn.astype(out[name].dtype))
    for name, factor in factors.items():
        out[name] = (out[name] * factor).astype(out[name].dtype)
    return out
```

```python
from contextlib import ExitStack

import numpy as np

import concourse.bass as bass
from concourse import mybir

F32 = mybir.dt.float32
ALU = mybir.AluOpType
ACT = mybir.ActivationFunctionType
AX = mybir.AxisListType

P = 128
D = 1024
KC = D // P
SEQ, NSEQ, STEP, PAST = 1024, 8, 16, 256
T = SEQ + NSEQ * STEP
NT = T // P
PT = SEQ // P
GN = T // 3
FH, FD = 8, 64
MH, MD = 4, 128
GH, GK, GV = 4, 128, 256
TAPS = 4
FF = 4 * D
SLAB = 512
EPS = 1e-6
BIG = 1e30
TAU = 16.0
LEVELS = [64, 32, 16, 8, 4, 2, 1]
UNIT = 4672
UPAD = 3 + SEQ + NSEQ * (STEP + 3)

E_FQ, E_FK, E_FV, E_FF, E_MQK, E_MV, E_MO, E_MI, E_MF = 0, 512, 1024, 1536, 1544, 2568, 3080, 3592, 3596
O_GQ, O_GK, O_GV, O_GG, O_GA = 0, 512, 1024, 2048, 3072

C_ID, C_MQ, C_MC, C_MB, C_ONE, C_MW, C_IND, C_C16 = 0, 128, 256, 384, 512, 640, 880, 888
C_N = 904


def constants():
    a, b = np.arange(P)[:, None], np.arange(P)[None, :]
    same = (a // STEP) == (b // STEP)
    c = np.zeros((P, C_N), np.float32)
    c[:, C_ID:C_ID + P] = np.eye(P)
    c[:, C_MQ:C_MQ + P] = np.where(b <= a, 0, -BIG)
    c[:, C_MC:C_MC + P] = np.where(a <= b, 0, -BIG)
    c[:, C_MB:C_MB + P] = np.where((a <= b) & same, 0, -BIG)
    c[:, C_ONE:C_ONE + P] = 1
    wide = np.full((P, 240), -BIG, np.float32)
    wide[:, 112:128] = np.where(np.arange(STEP)[None, :] <= (np.arange(P) % STEP)[:, None], 0, -BIG)
    c[:, C_MW:C_MW + 240] = wide
    c[:, C_IND:C_IND + 8] = (a // STEP) == np.arange(NSEQ)[None, :]
    c[:, C_C16:C_C16 + 16] = (a % STEP) <= np.arange(STEP)[None, :]
    sel = np.zeros((P, 8, P), np.float32)
    for h in range(8):
        sel[h, h, :] = 1
    gmask = np.zeros((P, 8, P), np.float32)
    for i, w in enumerate(LEVELS):
        gmask[:, i] = (a // (2 * w) == b // (2 * w)) & (a % (2 * w) < w) & (b % (2 * w) >= w)
    gmask[:, 7] = np.eye(P)
    later = np.zeros((P, 3, 384), np.float32)
    strict = (b < a).astype(np.float32)
    later[:, 0, 0:128] = strict
    later[:, 1, 0:128] = 1
    later[:, 1, 128:256] = strict
    later[:, 2, 0:256] = 1
    later[:, 2, 256:384] = strict * same
    return {"c_masks": c, "c_sel": sel.reshape(P, 1024), "c_levels": gmask.reshape(P, 1024),
            "c_later": later.reshape(P, 1152)}


def link(eng, sem, count, instruction):
    count[0] += 1
    instruction.then_inc(sem, 1)
    eng.wait_ge(sem, count[0])


def streaming_step(nc, i, o, scratch):
    ctx = ExitStack()
    with ctx:
        def sb(name, shape):
            return ctx.enter_context(nc.sbuf_tensor(name, shape, F32))

        def sem(name):
            return ctx.enter_context(nc.semaphore(name))

        units = sb("units", [P, 9 * UNIT])
        slabs = sb("slabs", [P, 2, KC, SLAB])
        masks = sb("masks", [P, C_N])
        sel = sb("sel", [P, 8, P])
        spare = sb("spare", [P, 2048])
        glrow = sb("glrow", [P, T])
        small = sb("small", [P, 880])
        junk256 = sb("junk256", [P, GV])[:, :]
        ps = ctx.enter_context(nc.psum_tensor("ps", [P, 8, 512], F32))

        used = [0]

        def few(n):
            used[0] += n
            assert used[0] <= 880
            return small[:, used[0] - n:used[0]]

        def unit(k, n=4608, at=0):
            return units[:, k * UNIT + at:k * UNIT + at + n]

        def fm(k, chunks=4):
            return unit(k, chunks * T).rearrange("p (c t) -> p c t", c=chunks)

        def tm(k, width):
            return unit(k, NT * width).rearrange("p (n w) -> p n w", n=NT)

        def mask(c, n=P):
            return masks[:, c:c + n]

        ident = mask(C_ID)
        wg = few(KC * 16).rearrange("p (k n) -> p k n", k=KC)
        convstate = few(KC * 27).rearrange("p (c n) -> p c n", c=KC)
        history = few(KC * 24).rearrange("p (c n) -> p c n", c=KC)
        params = few(56)
        gbias = few(3)
        lfT = few(NT * 8).rearrange("p (n h) -> p n h", n=NT)
        ssum, rstd = few(NT), few(NT)
        stat = few(32)
        conv_w = params[:, 0:32].rearrange("p (j c) -> p j c", j=TAPS)
        conv_b, g_ml, b_gla, g_gla = params[:, 32:40], params[:, 40:44], params[:, 44:48], params[:, 48:56]

        pe_stage, act_stage, dve_stage, pool_stage = (sem(n) for n in ("pe_stage", "act_stage", "dve_stage", "pool_stage"))
        dve_own, act_own, pool_own = sem("dve_own"), sem("act_own"), sem("pool_own")
        slab_in = [sem("slab_in0"), sem("slab_in1")]
        slab_used = sem("slab_used")
        const_in, x_in, param_in, gate_in, later_in, level_in, ga_in = (
            sem(n) for n in ("const_in", "x_in", "param_in", "gate_in", "later_in", "level_in", "ga_in"))
        xb_in = sem("xb_in")
        gain_in = sem("gain_in")
        out_done = sem("out_done")
        spill_done, respill_in = sem("spill_done"), sem("respill_in")
        par_tr, par_ev = sem("par_tr"), sem("par_ev")
        sq_done, xs_ready, tr_ready, tr_taken, root_ready, root_in = (
            sem(n) for n in ("sq_done", "xs_ready", "tr_ready", "tr_taken", "root_ready", "root_in"))
        fm_ready, fm_taken, tmj_ready, tmj_taken, gate_ready = (
            sem(n) for n in ("fm_ready", "fm_taken", "tmj_ready", "tmj_taken", "gate_ready"))
        conv_ready, conv_done, silu_done, ones_set = (sem(n) for n in ("conv_ready", "conv_done", "silu_done", "ones_set"))
        g_a, g_b, g_rows, g_tr, g_cols, m0_in = (sem(n) for n in ("g_a", "g_b", "g_rows", "g_tr", "g_cols", "m0_in"))
        fkT_ready, fkT_taken = sem("fkT_ready"), sem("fkT_taken")
        fk_out = [sem("fk_out0"), sem("fk_out1")]
        f_qz, f_s, f_mx, f_p, f_pt, f_pts, f_o, f_oev, f_ot = (
            sem(n) for n in ("f_qz", "f_s", "f_mx", "f_p", "f_pt", "f_pts", "f_o", "f_oev", "f_ot"))
        s_kin, s_kt, s_kts, s_q, s_s, s_mx, s_p, s_pn, s_pt, s_pts, s_o, s_oev = (
            sem("s_" + n) for n in ("kin", "kt", "kts", "q", "s", "mx", "p", "pn", "pt", "pts", "o", "oev"))
        cache_in = [sem("cache_in0"), sem("cache_in1")]
        pastlf_in = sem("pastlf_in")
        m_in, m_dm, m_w, m_g, m_a, m_kw, m_o, m_num, m_u, m_cn = (
            sem("m_" + n) for n in ("in", "dm", "w", "g", "a", "kw", "o", "num", "u", "cn"))
        c_in, n_in, c_tr, c_ev, c_qg, c_kw, c_u, c_cn, c_ct, c_ctev, c_o, c_out = (
            sem("c_" + n) for n in ("in", "nin", "tr", "ev", "qg", "kw", "u", "cn", "ct", "ctev", "o", "out"))
        h_sq, h_root, h_rt, h_hs, h_tr, h_mix = (sem("h_" + n) for n in ("sq", "root", "rt", "hs", "tr", "mix"))
        w_y, w_add = sem("w_y"), sem("w_add")
        ff_h, ff_relu, ff_sq, ff_y, ff_add = (sem("ff_" + n) for n in ("h", "relu", "sq", "y", "add"))
        a_e, a_l, a_cb, a_pre = (sem("a_" + n) for n in ("e", "l", "cb", "pre"))
        l_d, l_e, l_m, l_ks, l_kt, l_ktev, l_eb, l_qe = (sem("l_" + n) for n in ("d", "e", "m", "ks", "kt", "ktev", "eb", "qe"))
        l_free, l_keb = sem("l_free"), sem("l_keb")
        l_a, l_at, l_o, l_u, l_sn, l_osq, l_oln, l_osc, l_otr, l_mix = (
            sem("l_" + n) for n in ("a", "at", "o", "u", "sn", "osq", "oln", "osc", "otr", "mix"))
        l_v = sem("l_v")
        st_in, st_out = [sem("st_in0"), sem("st_in1")], [sem("st_out0"), sem("st_out1")]
        y_ready, y_out = sem("y_ready"), [sem(f"y_out{r}") for r in range(4)]

        def columns(w, at):
            return w[:, at:at + SLAB].rearrange("(k p) n -> p k n", p=P)

        we, wo_ = i["w_in_even"][0], i["w_in_odd"][0]
        first_slabs = [columns(we, c) for c in (E_MQK, E_MQK + SLAB, E_FQ, E_FK, E_MO, E_FV, E_MV)]
        first_slabs += [columns(i["w_out"][0], c) for c in (0, SLAB)]
        odd_slabs = [columns(wo_, c) for c in (O_GQ, O_GK, O_GG, O_GG + SLAB, O_GV, O_GV + SLAB)]
        odd_slabs += [columns(i["w_out"][1], c) for c in (0, SLAB)]
        MLP0 = len(first_slabs)
        ODD = MLP0 + 16
        MLP1 = ODD + len(odd_slabs)

        def slab_wait(eng, n, i4=None):
            if i4 is None:
                eng.wait_ge(slab_in[n % 2], 16 * (n // 2 + 1))
            else:
                eng.wait_ge(slab_in[n % 2], i4 * 32 + 16 * (n // 2 + 1))

        def enter(eng, stage):
            for s in (pe_stage, act_stage, dve_stage, pool_stage):
                eng.wait_ge(s, stage)

        def leave(eng, s):
            eng.drain().then_inc(s, 1)

        block = ctx.enter_context(nc.Block())

        (S_LOAD, S_NORM0, S_PROJ0, S_GATES, S_FOX, S_FOXS, S_ML, S_MLS, S_MLH, S_OUT0, S_NORM1, S_FF0,
         S_NORM2, S_PROJ1, S_CB, S_GLA, S_GLAS, S_OUT1, S_NORM3, S_FF1, S_FINAL) = range(21)

        def wide(k):
            return units[:, k * UNIT:k * UNIT + NT * D]

        def tokens(k):
            return wide(k).rearrange("p (n d) -> p n d", n=NT)

        def features(k):
            return wide(k).rearrange("p (c t) -> p c t", c=KC)

        FQ, FK, FV = fm(0), fm(1), tm(4, 512)
        MQ, MK, MO = fm(5), fm(6), fm(8)
        MV = unit(7, NT * MH * 129).rearrange("p (n h d) -> p n h d", n=NT, h=MH)
        HT0 = features(2)
        norms = [
            (tokens(0), features(2), 4, i["norm_mix"][0]),
            (tokens(2), features(4), 6, i["norm_ffn"][0]),
            (tokens(2), features(4), 6, i["norm_mix"][1]),
            (tokens(4), features(0), 6, i["norm_ffn"][1]),
        ]
        GQ, GKT, GG, GVT, CB = fm(0), fm(1), features(2), tokens(6), fm(8)

        def norm_parts(k):
            s = norms[k][2]
            return (unit(s, 2048).rearrange("p (b d) -> p b d", b=2), unit(s, 1024, 2048), unit(s, 1024, 3072))

        stage_of_norm = [S_NORM0, S_NORM1, S_NORM2, S_NORM3]

        def norm_act(act, k, own):
            x, h, _, _ = norms[k]
            _, junk, _ = norm_parts(k)
            if k == 0:
                act.wait_ge(x_in, 16 * NT)
            for n in range(NT):
                link(act, act_own, own, act.activation(junk, x[:, n], ACT.Square, accum_out=ssum[:, n:n + 1]))
            act.sem_inc(sq_done, 1)
            act.wait_ge(root_in, k + 1)
            act.activation(rstd, ssum, ACT.Sqrt).then_inc(root_ready, 1)
            for n in range(NT):
                act.wait_ge(tr_ready, NT * k + n + 1)
                b = 2 * (n % 4)
                act.activation(h[:, :, n * P:(n + 1) * P], ps[:, b:b + 2, :].rearrange("p b (c t) -> p (b c) t", c=4),
                               ACT.Copy).then_inc(tr_taken, 1)

        def norm_dve(dve, k, own):
            x, _, _, _ = norms[k]
            xs, _, gain = norm_parts(k)
            dve.wait_ge(sq_done, k + 1)
            dve.tensor_scalar(ssum, ssum, 1.0 / D, EPS, ALU.mult, ALU.add).then_inc(root_in, 1)
            dve.wait_ge(root_ready, k + 1)
            link(dve, dve_own, own, dve.reciprocal(ssum, rstd))
            dve.wait_ge(gain_in, 16 * (k + 1))
            for n in range(NT):
                if n >= 2:
                    dve.wait_ge(tr_ready, NT * k + n - 1)
                dve.scalar_tensor_tensor(out=xs[:, n % 2], in0=x[:, n], scalar=ssum[:, n:n + 1], in1=gain,
                                         op0=ALU.mult, op1=ALU.mult).then_inc(xs_ready, 1)

        def norm_pe(pe, k):
            xs, _, _ = norm_parts(k)
            for n in range(NT):
                pe.wait_ge(xs_ready, NT * k + n + 1)
                if n >= 4:
                    pe.wait_ge(tr_taken, NT * k + n - 3)
                for c in range(KC):
                    last = pe.transpose(ps[:, 2 * (n % 4) + c // 4, (c % 4) * P:(c % 4 + 1) * P],
                                        xs[:, n % 2, c * P:(c + 1) * P], ident)
                last.then_inc(tr_ready, 1)

        def proj_fm(pe, job, slab, m, h):
            g = 3 * (job % 2)
            for k in range(KC):
                for n in range(3):
                    last = pe.matmul(ps[:, g + n, 0:GN], slabs[:, slab % 2, k, m * P:(m + 1) * P],
                                     h[:, k, n * GN:(n + 1) * GN], start=(k == 0), stop=(k == KC - 1))
            return last

        def group(job):
            g = 3 * (job % 2)
            return ps[:, g:g + 3, 0:GN]

        def as_groups(row):
            return row.rearrange("p (g t) -> p g t", g=3)

        def out_pe(pe, layer, mix):
            for half in range(2):
                s = (MLP0 if layer == 0 else MLP1) - 2 + half
                slab_wait(pe, s)
                for n in range(NT):
                    j = half * NT + n
                    if j >= 4:
                        pe.wait_ge(w_add, 2 * NT * layer + j - 3)
                    for k in range(KC):
                        last = pe.matmul(ps[:, j % 4, :], mix(k)[:, n * P:(n + 1) * P], slabs[:, s % 2, k, :],
                                         start=(k == 0), stop=(k == KC - 1))
                    last.then_inc(w_y, 1)
                pe.drain().then_inc(slab_used, 1)

        def out_dve(dve, layer, x):
            for half in range(2):
                for n in range(NT):
                    j = half * NT + n
                    dve.wait_ge(w_y, 2 * NT * layer + j + 1)
                    xx = x[:, n, half * SLAB:(half + 1) * SLAB]
                    dve.tensor_tensor(xx, xx, ps[:, j % 4, :], ALU.add).then_inc(w_add, 1)

        BLOCKS = FF // D

        def mlp_pe(pe, layer, base, h, hid):
            with pe.Fori(0, BLOCKS) as blk:
                for half in range(2):
                    slab_wait(pe, base + half, blk)
                    for m in range(4):
                        j = half * 4 + m
                        if j >= 2:
                            pe.wait_ge(ff_relu, blk * KC + (layer * FF // P + j - 1))
                        proj_fm(pe, j, base + half, m, h).then_inc(ff_h, 1)
                    pe.drain().then_inc(slab_used, 1)
                pe.wait_ge(ff_sq, blk * KC + (layer * FF // P + KC))
                for half in range(2):
                    slab_wait(pe, base + 2 + half, blk)
                    for n in range(NT):
                        j = half * NT + n
                        if j >= 2:
                            pe.wait_ge(ff_add, blk * (2 * NT) + (layer * 2 * NT * BLOCKS + j - 1))
                        for k in range(KC):
                            last = pe.matmul(ps[:, 6 + j % 2, :], hid[:, k, n * P:(n + 1) * P],
                                             slabs[:, (base + half) % 2, k, :], start=(k == 0), stop=(k == KC - 1))
                        last.then_inc(ff_y, 1)
                    pe.drain().then_inc(slab_used, 1)

        def mlp_act(act, layer, hid):
            with act.Fori(0, BLOCKS) as blk:
                for j in range(KC):
                    act.wait_ge(ff_h, blk * KC + (layer * FF // P + j + 1))
                    act.activation(as_groups(hid[:, j]), group(j), ACT.Relu).then_inc(ff_relu, 1)

        def mlp_dve(dve, layer, x, hid):
            with dve.Fori(0, BLOCKS) as blk:
                for j in range(KC):
                    dve.wait_ge(ff_relu, blk * KC + (layer * FF // P + j + 1))
                    dve.tensor_tensor(hid[:, j], hid[:, j], hid[:, j], ALU.mult).then_inc(ff_sq, 1)
                for half in range(2):
                    for n in range(NT):
                        dve.wait_ge(ff_y, blk * (2 * NT) + (layer * 2 * NT * BLOCKS + half * NT + n + 1))
                        xx = x[:, n, half * SLAB:(half + 1) * SLAB]
                        dve.tensor_tensor(xx, xx, ps[:, 6 + (half * NT + n) % 2, :], ALU.add).then_inc(ff_add, 1)

        base2 = 2 * UNIT

        def scratch_row(n):
            return units[:, base2 + n * T:base2 + (n + 1) * T]

        RF, RI, RM, LF, LM, TF, TM_ = (scratch_row(n) for n in range(7))
        FN = units[:, base2 + 2 * UNIT - T:base2 + 2 * UNIT]
        slab_rows = slabs[:, 0].rearrange("p k n -> p (k n)")
        BM, IB, MM = (slab_rows[:, n * T:(n + 1) * T] for n in range(3))
        GL, RESET = glrow[:, :], glrow[:, :]
        ONES = spare[:, 0:SEQ]
        mbefore = few(9)
        enmT = few(NT * MH).rearrange("p (n h) -> p n h", n=NT)
        ibT = few(NT * MH).rearrange("p (n h) -> p n h", n=NT)
        ecl = few(2 * 32).rearrange("p (r h b) -> p r h b", r=2, h=GH)
        osum = few(8)

        otok = units[:, base2:base2 + 4096].rearrange("p (b f) -> p b f", b=PT)
        QZ = [units[:, base2 + 4096 + 1024 * r:base2 + 5120 + 1024 * r] for r in range(2)]
        PR = [units[:, base2 + 6144 + 1024 * r:base2 + 7168 + 1024 * r] for r in range(2)]
        PTS = [spare[:, 1024 * r:1024 * (r + 1)] for r in range(2)]
        FKST = [spare[:, 1024 * r:1024 * r + 512] for r in range(2)]
        fox_jobs = [(h, q) for h in range(FH) for q in range(PT)]
        NJ = len(fox_jobs)

        place = [base2]

        def take(n):
            place[0] += n
            return units[:, place[0] - n:place[0]]

        KIN = [take(1024).rearrange("p (j f) -> p j f", j=2) for _ in range(2)]
        VIN = [take(1024).rearrange("p (j f) -> p j f", j=2) for _ in range(2)]
        KT = take(1536).rearrange("p (c k) -> p c k", c=4)
        QB = [take(640) for _ in range(2)]
        LP = take(384).rearrange("p (j r) -> p j r", j=3)
        LNEW, SP, SPT_, PLF = take(128), take(384), take(384), take(128)
        SPT = SPT_.rearrange("p (j r) -> p j r", j=3)
        assert place[0] <= base2 + 2 * UNIT
        LATER = spare[:, 0:1152].rearrange("p (j k) -> p j k", j=3)

        place[0] = base2
        WT, GB, AT, QG, KW = (take(512).rearrange("p (h t) -> p h t", h=MH) for _ in range(5))
        CN = take(MH * 129).rearrange("p (h d) -> p h d", h=MH)
        CRAW = take(1024).rearrange("p (b d) -> p b d", b=NSEQ)
        CNS = take(NSEQ * 129).rearrange("p (b d) -> p b d", b=NSEQ)
        QGB = take(NSEQ * 144)
        KWB = take(1024).rearrange("p (b d) -> p b d", b=NSEQ)
        NROW, NOUT = take(128), take(128)
        NCOL, NNEW = take(32), take(36)
        assert place[0] <= base2 + 2 * UNIT
        NUM = unit(4, NT * MH * 129).rearrange("p (n h d) -> p n h d", n=NT, h=MH)
        HST = unit(1, 1024).rearrange("p (b d) -> p b d", b=2)
        HJUNK = unit(1, 128, 1024)
        RD, SSQ, HSC, HTMP = (unit(1, 36, 1152 + 36 * r) for r in range(4))

        EL = [units[:, 4 * UNIT + 3584 * r:4 * UNIT + 3584 * (r + 1)].rearrange("p (l h t) -> p l h t", l=7, h=GH)
              for r in range(2)]
        place[0] = 4 * UNIT + 7168
        LT = take(1024).rearrange("p (l t) -> p l t", l=8)
        LA = take(512).rearrange("p (h t) -> p h t", h=GH)
        QE = take(512).rearrange("p (h t) -> p h t", h=GH)
        assert place[0] <= 6 * UNIT
        KS = glrow[:, 0:512].rearrange("p (h t) -> p h t", h=GH)
        KST = glrow[:, 512:1024].rearrange("p (h t) -> p h t", h=GH)
        SS = spare[:, 0:1024].rearrange("p (h v) -> p h v", h=GH)
        OO = spare[:, 1024:2048].rearrange("p (h v) -> p h v", h=GH)
        GAT, WA2 = spare[:, 0:1152], spare[:, 1152:1664]
        SIN = [GQ[:, 2 * r:2 * r + 2, 0:SEQ].rearrange("p c (b v) -> p c b v", v=GV) for r in range(2)]
        SNEW = [GKT[:, 2 * r:2 * r + 2, 0:SEQ].rearrange("p c (b v) -> p c b v", v=GV) for r in range(2)]
        QEB = units[:, 4 * UNIT + 3584:4 * UNIT + 3584 + NSEQ * 144]
        KEB = units[:, 4 * UNIT + 3584 + 1152:4 * UNIT + 3584 + 2176].rearrange("p (b k) -> p b k", b=NSEQ)

        def sample(row):
            return row[:, SEQ:T].rearrange("p (b t) -> p b t", b=NSEQ)

        def starts(n):
            return slice(SEQ, T, STEP) if n else slice(0, SEQ, P)

        def conv_in(j):
            return unit(4, UPAD, (j % 3) * UPAD)

        def conv_seq(j):
            return conv_in(j)[:, 3 + SEQ:].rearrange("p (b t) -> p b t", b=NSEQ)

        def conv_out(j):
            return (MQ if j < 4 else MK)[:, j % 4]

        @block.sync
        def _(sp):
            def load(n, src):
                if n >= 2:
                    sp.wait_ge(slab_used, n - 1)
                sp.dma_start(slabs[:, n % 2], src).then_inc(slab_in[n % 2], 16)

            for n, src in enumerate(first_slabs):
                if n == 8:
                    for s in (pe_stage, dve_stage, act_stage, pool_stage):
                        sp.wait_ge(s, S_OUT0)
                load(n, src)

            def mlp(layer, base):
                w1 = i["w_ff1"][layer].rearrange("(k p) (b n) -> b p k n", p=P, n=SLAB)
                w2 = i["w_ff2"][layer].rearrange("(b k p) n -> b p k n", p=P, k=KC)
                with sp.Fori(0, BLOCKS) as blk:
                    for j, w in ((0, w1), (1, w1), (2, w2), (3, w2)):
                        n = base + j
                        sp.wait_ge(slab_used, blk * 4 + (n - 1))
                        src = w[bass.ds(blk * 2 + j, 1)] if j < 2 else w[bass.ds(blk, 1), :, :, (j - 2) * SLAB:(j - 1) * SLAB]
                        src = src.rearrange("o p k n -> (o p) k n")
                        sp.dma_start(slabs[:, n % 2], src).then_inc(slab_in[n % 2], 16)

            mlp(0, MLP0)
            for n, src in enumerate(odd_slabs):
                load(ODD + n, src)
            mlp(1, MLP1)

        @block.gpsimd
        def _(pool):
            outs, pown = [0], [0]

            def put(dst, src):
                outs[0] += 16
                pool.dma_start(dst, src).then_inc(out_done, 16)

            pool.dma_start(masks[:, :], i["c_masks"]).then_inc(const_in, 16)
            pool.dma_start(sel.rearrange("p h t -> p (h t)"), i["c_sel"]).then_inc(const_in, 16)
            rows = unit(4, P, 0)
            for r, src in ((0, i["conv_w_ml"][0].rearrange("j (c p) -> (j c) p", p=P)),
                           (32, i["conv_b_ml"][0].rearrange("(c p) -> c p", p=P)),
                           (40, i["g_ml"][0].rearrange("(c p) -> c p", p=P)),
                           (44, i["b_gla_a"][0].rearrange("(c p) -> c p", p=P)),
                           (48, i["g_gla"][0].rearrange("(c p) -> c p", p=P))):
                pool.dma_start(rows[r:r + src.shape[0], :], src).then_inc(param_in, 16)
            pool.dma_start(unit(4, D, P)[0:24, :], i["state_mlstm_conv"][0].rearrange("b j f -> (b j) f")).then_inc(param_in, 16)
            pool.dma_start(gbias[0:8, 0:1], i["b_fox_f"].rearrange("o h -> h o")).then_inc(gate_in, 16)
            pool.dma_start(gbias[0:4, 1:2], i["b_ml_i"].rearrange("o h -> h o")).then_inc(gate_in, 16)
            pool.dma_start(gbias[0:4, 2:3], i["b_ml_f"].rearrange("o h -> h o")).then_inc(gate_in, 16)
            with nc.allow_non_contiguous_dma(reason="32 values"):
                pool.dma_start(mbefore[0:4, 1:9], i["state_mlstm_m"][0].rearrange("b h -> h b")).then_inc(gate_in, 16)
            pool.dma_start(wg[:, :, 0:8], we[:, E_FF:E_FF + 8].rearrange("(k p) n -> p k n", p=P)).then_inc(gate_in, 16)
            pool.dma_start(wg[:, :, 8:16], we[:, E_MI:E_MI + 8].rearrange("(k p) n -> p k n", p=P)).then_inc(gate_in, 16)
            x = tokens(0)
            for n in range(PT):
                pool.dma_start(x[:, n], i["x_prompt"][0, n * P:(n + 1) * P, :]).then_inc(x_in, 16)
            pool.dma_start(x[:, PT], i["x_sample"].rearrange("b t d -> (b t) d")).then_inc(x_in, 16)
            pool.memset(mbefore[0:4, 0:1], 0.0)
            leave(pool, pool_stage)

            def gain(k):
                pool.dma_start(norm_parts(k)[2], norms[k][3].partition_broadcast(P)).then_inc(gain_in, 16)

            enter(pool, S_NORM0)
            gain(0)
            leave(pool, pool_stage)

            enter(pool, S_PROJ0)
            pool.memset(MV[:, :, :, 128:129], 1.0)
            for r in range(3):
                pool.memset(conv_in(r)[:, 0:3], 0.0)
            for j in range(KC):
                if j >= 3:
                    pool.wait_ge(conv_done, j - 2)
                pool.tensor_copy(conv_seq(j)[:, :, 0:3],
                                 history[:, j].rearrange("p (b t) -> p b t", b=NSEQ)).then_inc(conv_ready, 1)
            for j in range(4, KC):
                pool.wait_ge(silu_done, j + 1)
                pool.tensor_scalar(conv_out(j), conv_out(j), MD ** -0.5, None, ALU.mult)
            leave(pool, pool_stage)

            enter(pool, S_GATES)
            put(o["p_fox_v"][0, 0].rearrange("(n p) h d -> p n (h d)", p=P), FV[:, 0:PT])
            put(o["s_fox_v"][0].rearrange("b t h d -> (b t) (h d)"), FV[:, PT])
            pool.wait_ge(g_cols, 1)
            put(o["p_fox_logf"][0, 0].rearrange("(n p) h -> p n h", p=P), lfT[:, 0:PT])
            put(o["s_fox_logf"][0].rearrange("b t h -> (b t) h"), lfT[:, PT])
            pool.wait_ge(g_rows, 1)
            with nc.allow_non_contiguous_dma(reason="36 values"):
                put(o["p_mlstm_m"][0].rearrange("o h -> h o"), MM[0:4, SEQ - 1:SEQ])
                put(o["s_mlstm_m"][0].rearrange("b h -> h b"), MM[0:4, SEQ + STEP - 1:T:STEP])
            leave(pool, pool_stage)

            enter(pool, S_FOX)
            pool.memset(QZ[0][64:128, :], 0.0)
            pool.memset(QZ[1][0:64, :], 0.0).then_inc(f_qz, 1)
            for n in range(NT):
                pool.wait_ge(fkT_taken, n + 1)
                dst = o["p_fox_k"][0, 0, n * P:(n + 1) * P].rearrange("t h d -> t (h d)") if n < PT \
                    else o["s_fox_k"][0].rearrange("b t h d -> (b t) (h d)")
                pool.dma_start(dst, FKST[n % 2]).then_inc(fk_out[n % 2], 16)
            pool.wait_ge(fk_out[0], 16 * 5)
            pool.wait_ge(fk_out[1], 16 * 4)
            leave(pool, pool_stage)

            enter(pool, S_FOXS)
            pool.memset(QB[0], 0.0)
            pool.memset(QB[1], 0.0).then_inc(s_q, 1)
            pool.dma_start(LATER.rearrange("p j k -> p (j k)"), i["c_later"]).then_inc(later_in, 16)
            for jt in range(2):
                pool.dma_start(PLF.rearrange("p (b j h) -> p b j h", b=NSEQ, j=2)[:, :, jt],
                               i["cache_fox_logf"][0, :, jt * P:(jt + 1) * P].rearrange("b p h -> p b h")).then_inc(pastlf_in, 16)
            for b in range(NSEQ):
                if b >= 2:
                    pool.wait_ge(s_o, b - 1)
                for buf, src in ((KIN, i["cache_fox_k"]), (VIN, i["cache_fox_v"])):
                    pool.dma_start(buf[b % 2], src[0, b].rearrange("(j p) h d -> p j (h d)", p=P)).then_inc(cache_in[b % 2], 16)
            leave(pool, pool_stage)

            enter(pool, S_ML)
            pool.memset(CN.rearrange("p h d -> p (h d)"), 0.0).then_inc(m_cn, 1)
            pool.memset(QGB, 0.0)
            pool.dma_start(NROW[0:32, :], i["state_mlstm_n"][0].rearrange("b h d -> (b h) d")).then_inc(n_in, 16)
            pool.dma_start(CRAW, i["state_mlstm_c"][0, :, 0].rearrange("b e d -> e b d")).then_inc(c_in, 16)
            leave(pool, pool_stage)

            enter(pool, S_MLS)
            put(o["p_mlstm_c"][0, 0].rearrange("h e d -> e h d"), QG)
            put(o["p_mlstm_n"][0, 0], NOUT[0:4, :])
            for h in range(MH):
                pool.wait_ge(c_ctev, h + 1)
                pool.dma_start(o["s_mlstm_c"][0, :, h].rearrange("b e d -> e b d"), CRAW).then_inc(c_out, 16)
                if h < MH - 1:
                    pool.wait_ge(c_out, 16 * (h + 1))
                    pool.dma_start(CRAW, i["state_mlstm_c"][0, :, h + 1].rearrange("b e d -> e b d")).then_inc(c_in, 16)
            pool.wait_ge(c_out, 16 * MH)
            pool.wait_ge(c_o, 1)
            put(o["s_mlstm_n"][0].rearrange("b h d -> (b h) d"), NROW[0:32, :])
            leave(pool, pool_stage)

            enter(pool, S_MLH)
            cs = KWB.rearrange("p b d -> p (b d)")
            put(o["p_mlstm_conv"][0, 0], cs[0:3, :])
            put(o["s_mlstm_conv"][0].rearrange("b j f -> (b j) f"), cs[3:27, :])
            pool.wait_ge(out_done, outs[0])
            leave(pool, pool_stage)

            enter(pool, S_OUT0)
            x = tokens(2)
            for n in range(PT):
                pool.dma_start(x[:, n], i["x_prompt"][0, n * P:(n + 1) * P, :]).then_inc(xb_in, 16)
            pool.dma_start(x[:, PT], i["x_sample"].rearrange("b t d -> (b t) d")).then_inc(xb_in, 16)
            gain(1)
            leave(pool, pool_stage)
            for s in (S_NORM1, S_FF0):
                enter(pool, s)
                leave(pool, pool_stage)

            enter(pool, S_NORM2)
            gain(2)
            pool.dma_start(wg[:, :, :], wo_[:, O_GA:O_GA + 16].rearrange("(k p) n -> p k n", p=P)).then_inc(ga_in, 16)
            pool.dma_start(sel.rearrange("p h t -> p (h t)"), i["c_levels"]).then_inc(level_in, 16)
            pool.dma_start(scratch, wide(2)).then_inc(spill_done, 16)
            pool.dma_start(WA2[0:16, :], i["w_gla_a2"][0]).then_inc(ga_in, 16)
            pool.wait_ge(spill_done, 16)
            leave(pool, pool_stage)

            enter(pool, S_PROJ1)
            leave(pool, pool_stage)

            enter(pool, S_CB)
            link(pool, pool_own, pown, pool.memset(RESET, 1.0))
            pool.memset(RESET[:, starts(0)], 0.0)
            pool.memset(RESET[:, starts(1)], 0.0).then_inc(a_pre, 1)
            leave(pool, pool_stage)

            enter(pool, S_GLA)
            pool.memset(SS.rearrange("p h v -> p (h v)"), 0.0).then_inc(l_sn, 1)

            def exponents(n):
                cb = CB[:, :, n * P:(n + 1) * P]
                if n >= 2:
                    pool.wait_ge(l_a, 4 * (n - 1))
                for l, w in enumerate(LEVELS):
                    if n == PT and w > 8:
                        continue
                    np_ = P // (2 * w)
                    pairs = cb.rearrange("p h (n w) -> p h n w", w=2 * w)
                    e = EL[n % 2][:, l].rearrange("p h (n w) -> p h n w", w=2 * w)
                    edge = pairs[:, :, :, w - 1:w].broadcast_to([P, GH, np_, w])
                    pool.tensor_tensor(e[:, :, :, 0:w], edge, pairs[:, :, :, 0:w], ALU.subtract)
                    last = pool.tensor_tensor(e[:, :, :, w:2 * w], pairs[:, :, :, w:2 * w], edge, ALU.subtract)
                last.then_inc(l_d, 1)
                if n >= 1:
                    pool.wait_ge(l_kt, n)
                seg = P if n < PT else STEP
                ends = cb.rearrange("p h (b t) -> p h b t", t=seg)
                pool.tensor_tensor(KS.rearrange("p h (b t) -> p h b t", t=seg),
                                   ends[:, :, :, seg - 1:seg].broadcast_to([P, GH, P // seg, seg]), ends,
                                   ALU.subtract).then_inc(l_d, 1)

            for n in range(PT):
                exponents(n)
            leave(pool, pool_stage)

            enter(pool, S_GLAS)
            put(o["p_gla_s"][0, 0].rearrange("h k v -> k h v"), SS)
            pool.memset(QEB, 0.0).then_inc(l_v, 1)
            exponents(PT)

            def state_in(h):
                for c in range(2):
                    pool.dma_start(SIN[h % 2][:, c],
                                   i["state_gla_s"][0, 4 * c:4 * c + 4, h].rearrange("b k v -> k b v")).then_inc(st_in[h % 2], 16)

            state_in(0)
            state_in(1)
            for h in range(GH):
                pool.wait_ge(l_sn, 1 + 4 * PT + NSEQ * (h + 1))
                for c in range(2):
                    pool.dma_start(o["s_gla_s"][0, 4 * c:4 * c + 4, h].rearrange("b k v -> k b v"),
                                   SNEW[h % 2][:, c]).then_inc(st_out[h % 2], 16)
                if h + 2 < GH:
                    state_in(h + 2)
            pool.wait_ge(st_out[0], 64)
            pool.wait_ge(st_out[1], 64)
            pool.wait_ge(out_done, outs[0])
            leave(pool, pool_stage)

            enter(pool, S_OUT1)
            pool.dma_start(wide(4), scratch).then_inc(respill_in, 16)
            gain(3)
            leave(pool, pool_stage)
            for s in (S_NORM3, S_FF1):
                enter(pool, s)
                leave(pool, pool_stage)

            enter(pool, S_FINAL)
            pool.dma_start(unit(6, D), i["norm_final"].partition_broadcast(P)).then_inc(gain_in, 16)
            for n in range(NT):
                pool.wait_ge(y_ready, n + 1)
                dst = o["y_prompt"][0, n * P:(n + 1) * P] if n < PT else o["y_sample"].rearrange("b t d -> (b t) d")
                pool.dma_start(dst, unit(0, D, (n % 4) * D)).then_inc(y_out[n % 4], 16)
            for r in range(4):
                pool.wait_ge(y_out[r], 16 * len(range(r, NT, 4)))

        @block.tensor
        def _(pe):
            pe.wait_ge(const_in, 32)
            pe.wait_ge(param_in, 16 * 6)
            pe.transpose(ps[:, 0, 0:56], unit(4, P)[0:56, :], ident[0:56, 0:56]).then_inc(par_tr, 1)
            for c in range(KC):
                last = pe.transpose(ps[:, 1, c * 24:(c + 1) * 24], unit(4, D, P)[0:24, c * P:(c + 1) * P], ident[0:24, 0:24])
            last.then_inc(par_tr, 1)
            leave(pe, pe_stage)

            enter(pe, S_NORM0)
            norm_pe(pe, 0)
            leave(pe, pe_stage)

            enter(pe, S_PROJ0)
            for j in range(20):
                slab = j // 4
                if j % 4 == 0:
                    slab_wait(pe, slab)
                if j >= 2:
                    pe.wait_ge(fm_taken, j - 1)
                proj_fm(pe, j, slab, j % 4, HT0).then_inc(fm_ready, 1)
                if j % 4 == 3:
                    pe.drain().then_inc(slab_used, 1)
            for j in range(2 * NT):
                slab = 5 + j // NT
                if j % NT == 0:
                    slab_wait(pe, slab)
                if j >= 2:
                    pe.wait_ge(tmj_taken, j - 1)
                n = j % NT
                for k in range(KC):
                    last = pe.matmul(ps[:, 6 + j % 2, :], HT0[:, k, n * P:(n + 1) * P], slabs[:, slab % 2, k, :],
                                     start=(k == 0), stop=(k == KC - 1))
                last.then_inc(tmj_ready, 1)
                if n == NT - 1:
                    pe.drain().then_inc(slab_used, 1)
            pe.wait_ge(fm_taken, 20)
            pe.wait_ge(tmj_taken, 2 * NT)
            pe.wait_ge(gate_in, 16 * 6)
            for g, (c, m) in enumerate(((0, 8), (8, 4), (12, 4))):
                for b, (t0, t1) in enumerate(((0, 512), (512, 1024), (1024, T))):
                    out = ps[0:m, 2 * g + b, :] if b < 2 else ps[0:m, 6, g * P:(g + 1) * P]
                    for k in range(KC):
                        last = pe.matmul(out, wg[:, k, c:c + m], HT0[:, k, t0:t1], start=(k == 0), stop=(k == KC - 1))
            last.then_inc(gate_ready, 1)
            leave(pe, pe_stage)

            enter(pe, S_GATES)
            pe.wait_ge(g_rows, 1)
            for n in range(NT):
                pe.transpose(ps[:, 0, n * 8:(n + 1) * 8], LF[0:8, n * P:(n + 1) * P], ident[0:8, 0:8])
                pe.transpose(ps[:, 0, 72 + n * 4:76 + n * 4], IB[0:4, n * P:(n + 1) * P], ident[0:4, 0:4])
                last = pe.transpose(ps[:, 0, 108 + n * 4:112 + n * 4], MM[0:4, n * P:(n + 1) * P], ident[0:4, 0:4])
            last.then_inc(g_tr, 1)
            leave(pe, pe_stage)

            enter(pe, S_FOX)
            for n in range(NT):
                if n >= 2:
                    pe.wait_ge(fkT_taken, n - 1)
                for c in range(4):
                    last = pe.transpose(ps[:, 4 + n % 2, c * P:(c + 1) * P], FK[:, c, n * P:(n + 1) * P], ident)
                last.then_inc(fkT_ready, 1)
            pe.wait_ge(fkT_taken, NT)

            def scores(j):
                h, q = fox_jobs[j]
                width = (q + 1) * P
                pe.wait_ge(f_qz, 2 + h)
                if j >= 2:
                    pe.wait_ge(f_p, j - 1)
                for c in range(0, width, 512):
                    w = min(512, width - c)
                    out = ps[:, 2 * (j % 2) + c // 512, 0:w]
                    last_part = c + w == width
                    pe.matmul(out, QZ[h % 2][:, q * P:(q + 1) * P], FK[:, h // 2, c:c + w], start=True, stop=False)
                    last = pe.matmul(out, sel[:, h, :], FN[:, c:c + w], start=False, stop=not last_part)
                    if last_part:
                        last = pe.matmul(out[:, w - P:w], ident, mask(C_MQ), start=False, stop=True)
                last.then_inc(f_s, 1)

            def probs(j):
                h, q = fox_jobs[j]
                pe.wait_ge(f_p, j + 1)
                if j >= 1:
                    pe.wait_ge(f_pts, j)
                for t in range(q + 1):
                    last = pe.transpose(ps[:, 4 + t // 4, (t % 4) * P:(t % 4 + 1) * P], PR[j % 2][:, t * P:(t + 1) * P], ident)
                last.then_inc(f_pt, 1)

            def values(j):
                h, q = fox_jobs[j]
                pe.wait_ge(f_pts, j + 1)
                if j >= 2:
                    pe.wait_ge(f_oev, j - 1)
                for t in range(q + 1):
                    last = pe.matmul(ps[:, 6 + j % 2, 0:FD], PTS[j % 2][:, t * P:(t + 1) * P], FV[:, t, h * FD:(h + 1) * FD],
                                     start=(t == 0), stop=(t == q))
                last.then_inc(f_o, 1)

            scores(0)
            for j in range(NJ):
                if j + 1 < NJ:
                    scores(j + 1)
                probs(j)
                if j >= 1:
                    values(j - 1)
            values(NJ - 1)
            pe.wait_ge(f_oev, NJ)
            for n in range(PT):
                for c in range(4):
                    last = pe.transpose(ps[:, n, c * P:(c + 1) * P], otok[:, n, c * P:(c + 1) * P], ident)
                last.then_inc(f_ot, 1)
            leave(pe, pe_stage)

            enter(pe, S_FOXS)
            pe.wait_ge(later_in, 16)

            def seq_out(b):
                pe.wait_ge(s_pn, b + 1)
                for t in range(3):
                    last = pe.transpose(ps[:, 4, t * P:(t + 1) * P], SP[:, t * P:(t + 1) * P], ident)
                last.then_inc(s_pt, 1)
                pe.wait_ge(s_pts, b + 1)
                if b >= 1:
                    pe.wait_ge(s_oev, b)
                for c in range(4):
                    for t in range(3):
                        v = VIN[b % 2][:, t, c * P:(c + 1) * P] if t < 2 else FV[:, PT, c * P:(c + 1) * P]
                        last = pe.matmul(ps[:, 6, c * 32:(c + 1) * 32], v, SPT[:, t, c * 32:(c + 1) * 32],
                                         start=(t == 0), stop=(t == 2))
                last.then_inc(s_o, 1)

            for b in range(NSEQ):
                pe.wait_ge(cache_in[b % 2], 32 * (b // 2 + 1))
                if b >= 1:
                    pe.wait_ge(s_kts, b)
                for j in range(2):
                    for c in range(4):
                        at = c * 256 + j * P
                        last = pe.transpose(ps[:, at // 512, at % 512:at % 512 + P], KIN[b % 2][:, j, c * P:(c + 1) * P], ident)
                last.then_inc(s_kt, 1)
                pe.wait_ge(s_kts, b + 1)
                pe.wait_ge(s_q, b + 2)
                if b >= 2:
                    pe.wait_ge(s_p, b - 1)
                out = ps[:, 2 + b % 2, 0:384]
                for c in range(4):
                    pe.matmul(out, QB[b % 2][:, c * P:(c + 1) * P], KT[:, c, :], start=(c == 0), stop=False)
                for t in range(3):
                    pe.matmul(out, LP[:, t, :], LATER[:, t, :], start=False, stop=False)
                pe.matmul(out[:, 256:384], ident, mask(C_MW + 112 - STEP * b), start=False, stop=True).then_inc(s_s, 1)
                seq_out(b)
            leave(pe, pe_stage)

            enter(pe, S_ML)

            def ml_inputs(n):
                t = slice(n * P, (n + 1) * P)
                for h in range(MH):
                    pe.matmul(ps[:, 0, h * P:(h + 1) * P], sel[:, h, :], BM[:, t], start=True, stop=True)
                    pe.matmul(ps[:, 1, h * P:(h + 1) * P], sel[:, h, :], GL[:, t], start=True, stop=True)
                    pe.matmul(ps[:, 2, h * P:(h + 1) * P], MK[:, h, t], MQ[:, h, t], start=True, stop=True)
                    last = pe.transpose(ps[:, 3, h * P:(h + 1) * P], MK[:, h, t], ident)
                last.then_inc(m_in, 1)

            for n in range(PT):
                if n >= 1:
                    pe.wait_ge(m_kw, n)
                    pe.wait_ge(m_g, n)
                ml_inputs(n)
                pe.wait_ge(m_a, n + 1)
                pe.wait_ge(m_cn, n + 1)
                if n >= 1:
                    pe.wait_ge(m_num, n)
                for h in range(MH):
                    out = ps[:, 4 + h // 2, (h % 2) * 129:(h % 2 + 1) * 129]
                    pe.matmul(out, AT[:, h], MV[:, n, h], start=True, stop=False)
                    last = pe.matmul(out, QG[:, h], CN[:, h], start=False, stop=True)
                last.then_inc(m_o, 1)
                pe.wait_ge(m_kw, n + 1)
                for h in range(MH):
                    last = pe.matmul(ps[:, 6 + h // 2, (h % 2) * 129:(h % 2 + 1) * 129], KW[:, h], MV[:, n, h],
                                     start=True, stop=True)
                last.then_inc(m_u, 1)
            pe.wait_ge(m_cn, PT + 1)
            pe.wait_ge(m_kw, PT)
            for h in range(MH):
                last = pe.transpose(ps[:, 0, h * P:(h + 1) * P], CN[:, h, 0:128], ident)
            pe.wait_ge(n_in, 16)
            pe.transpose(ps[0:4, 1, 0:P], NNEW[:, 32:36], ident)
            pe.transpose(ps[:, 2, 0:32], NROW[0:32, :], ident[0:32, 0:32]).then_inc(c_ct, 1)
            leave(pe, pe_stage)

            enter(pe, S_MLS)
            ml_inputs(PT)
            pe.wait_ge(m_a, PT + 1)
            pe.wait_ge(m_kw, PT + 1)
            for h in range(MH):
                pe.wait_ge(c_in, 16 * (h + 1))
                for b in range(NSEQ):
                    last = pe.transpose(ps[:, b // 4, (b % 4) * P:(b % 4 + 1) * P], CRAW[:, b], ident)
                last.then_inc(c_tr, 1)
                pe.wait_ge(c_ev, h + 1)
                pe.wait_ge(c_qg, h + 1)
                out = ps[:, 4, 0:129]
                pe.matmul(out, AT[:, h], MV[:, PT, h], start=True, stop=False)
                for b in range(NSEQ):
                    last = pe.matmul(out, QGB[:, b * P:(b + 1) * P], CNS[:, b], start=False, stop=(b == NSEQ - 1))
                last.then_inc(m_o, 1)
                pe.wait_ge(c_kw, h + 1)
                for b in range(NSEQ):
                    last = pe.matmul(ps[:, 5 + b // 3, (b % 3) * 129:(b % 3 + 1) * 129], KWB[:, b], MV[:, PT, h],
                                     start=True, stop=True)
                last.then_inc(c_u, 1)
                pe.wait_ge(c_cn, h + 1)
                for b in range(NSEQ):
                    last = pe.transpose(ps[:, b // 4, (b % 4) * P:(b % 4 + 1) * P], CNS[:, b, 0:128], ident)
                last.then_inc(c_ct, 1)
                pe.wait_ge(c_ctev, h + 1)
            pe.transpose(ps[0:32, 2, 0:P], NNEW[:, 0:32], ident)
            for c in range(KC):
                last = pe.transpose(ps[0:27, 5 + c // 4, (c % 4) * P:(c % 4 + 1) * P], convstate[:, c], ident)
            last.then_inc(c_ct, 1)
            leave(pe, pe_stage)

            enter(pe, S_MLH)
            for n in range(NT):
                pe.wait_ge(h_hs, n + 1)
                if n >= 4:
                    pe.wait_ge(h_mix, n - 3)
                for h in range(MH):
                    last = pe.transpose(ps[:, n % 4, h * P:(h + 1) * P], HST[:, n % 2, h * P:(h + 1) * P], ident)
                last.then_inc(h_tr, 1)
            leave(pe, pe_stage)

            enter(pe, S_OUT0)
            out_pe(pe, 0, lambda k: FQ[:, k] if k < 4 else MO[:, k - 4])
            leave(pe, pe_stage)
            enter(pe, S_NORM1)
            norm_pe(pe, 1)
            leave(pe, pe_stage)
            enter(pe, S_FF0)
            mlp_pe(pe, 0, MLP0, features(4), features(0))
            leave(pe, pe_stage)
            enter(pe, S_NORM2)
            norm_pe(pe, 2)
            leave(pe, pe_stage)

            enter(pe, S_PROJ1)
            h1 = features(4)
            for j in range(16):
                slab = ODD + j // 4
                if j % 4 == 0:
                    slab_wait(pe, slab)
                if j >= 2:
                    pe.wait_ge(fm_taken, 20 + j - 1)
                proj_fm(pe, j, slab, j % 4, h1).then_inc(fm_ready, 1)
                if j % 4 == 3:
                    pe.drain().then_inc(slab_used, 1)
            for j in range(2 * NT):
                slab = ODD + 4 + j // NT
                if j % NT == 0:
                    slab_wait(pe, slab)
                if j >= 2:
                    pe.wait_ge(tmj_taken, 2 * NT + j - 1)
                n = j % NT
                for k in range(KC):
                    last = pe.matmul(ps[:, 6 + j % 2, :], h1[:, k, n * P:(n + 1) * P], slabs[:, slab % 2, k, :],
                                     start=(k == 0), stop=(k == KC - 1))
                last.then_inc(tmj_ready, 1)
                if n == NT - 1:
                    pe.drain().then_inc(slab_used, 1)
            pe.wait_ge(fm_taken, 36)
            pe.wait_ge(ga_in, 32)
            for n in range(3):
                for k in range(KC):
                    last = pe.matmul(ps[0:16, n, 0:GN], wg[:, k, :], h1[:, k, n * GN:(n + 1) * GN],
                                     start=(k == 0), stop=(k == KC - 1))
            last.then_inc(gate_ready, 1)
            leave(pe, pe_stage)

            enter(pe, S_CB)
            for m in range(4):
                if m >= 2:
                    pe.wait_ge(a_e, m - 1)
                for n in range(3):
                    last = pe.matmul(ps[:, 3 * (m % 2) + n, 0:GN], WA2[0:16, m * P:(m + 1) * P],
                                     GAT[0:16, n * GN:(n + 1) * GN], start=True, stop=True)
                last.then_inc(a_l, 1)
            leave(pe, pe_stage)

            enter(pe, S_GLA)
            pe.wait_ge(level_in, 16)

            def level_pair(q):
                return 2 * (q % 2)

            def gla_head(n):
                t = slice(n * P, (n + 1) * P)
                pe.wait_ge(l_ks, n + 1)
                if n >= 1:
                    pe.wait_ge(l_sn, 1 + 4 * n)
                for h in range(GH):
                    last = pe.transpose(ps[:, 6, h * P:(h + 1) * P], KS[:, h], ident)
                last.then_inc(l_kt, 1)
                pe.wait_ge(l_m, n + 1)
                for h in range(GH):
                    q = 5 * n + h
                    if q >= 2:
                        pe.wait_ge(l_free, q - 1)
                    for l in range(8):
                        out = ps[:, level_pair(q) + l // 4, (l % 4) * P:(l % 4 + 1) * P]
                        if l == 7:
                            last = pe.matmul(out, GKT[:, h, t], GQ[:, h, t], start=True, stop=True)
                        elif n < PT or LEVELS[l] <= 8:
                            pe.matmul(out, EL[n % 2][:, l, h], EL[n % 2][:, l, h], start=True, stop=True)
                    last.then_inc(l_a, 1)

            def gla_turn(n):
                q = 5 * n + 4
                pe.wait_ge(l_osc, n + 1)
                pe.wait_ge(l_free, q - 1)
                for c in range(8):
                    last = pe.transpose(ps[:, level_pair(q) + c // 4, (c % 4) * P:(c % 4 + 1) * P],
                                        OO[:, c // 2, (c % 2) * P:(c % 2 + 1) * P], ident)
                last.then_inc(l_otr, 1)

            for n in range(PT):
                gla_head(n)
                pe.wait_ge(l_qe, n + 1)
                pe.wait_ge(l_sn, 1 + 4 * n)
                if n >= 1:
                    pe.wait_ge(l_osc, n)
                for h in range(GH):
                    pe.wait_ge(l_at, 4 * n + h + 1)
                    out = ps[:, 4 + h // 2, (h % 2) * GV:(h % 2 + 1) * GV]
                    pe.matmul(out, LA[:, h], GVT[:, n, h * GV:(h + 1) * GV], start=True, stop=False)
                    last = pe.matmul(out, QE[:, h], SS[:, h], start=False, stop=True)
                last.then_inc(l_o, 1)
                pe.wait_ge(l_ktev, n + 1)
                for h in range(GH):
                    last = pe.matmul(ps[:, 6 + h // 2, (h % 2) * GV:(h % 2 + 1) * GV], KST[:, h],
                                     GVT[:, n, h * GV:(h + 1) * GV], start=True, stop=True)
                last.then_inc(l_u, 1)
                gla_turn(n)
            leave(pe, pe_stage)

            enter(pe, S_GLAS)
            gla_head(PT)
            for h in range(GH):
                pe.wait_ge(l_at, 4 * PT + h + 1)
                pe.wait_ge(l_qe, PT + h + 1)
                pe.wait_ge(st_in[h % 2], 32 * (h // 2 + 1))
                out = ps[:, 4 + h // 2, (h % 2) * GV:(h % 2 + 1) * GV]
                pe.matmul(out, LA[:, h], GVT[:, PT, h * GV:(h + 1) * GV], start=True, stop=False)
                for b in range(NSEQ):
                    last = pe.matmul(out, QEB[:, b * P:(b + 1) * P], SIN[h % 2][:, b // 4, b % 4], start=False,
                                     stop=(b == NSEQ - 1))
                last.then_inc(l_o, 1)
                pe.wait_ge(l_keb, h + 1)
                for b in range(NSEQ):
                    g = NSEQ * h + b
                    if g >= 2:
                        pe.wait_ge(l_sn, 1 + 4 * PT + g - 1)
                    pe.matmul(ps[:, 6 + g % 2, 0:GV], KEB[:, b], GVT[:, PT, h * GV:(h + 1) * GV],
                              start=True, stop=True).then_inc(l_u, 1)
            gla_turn(PT)
            leave(pe, pe_stage)

            enter(pe, S_OUT1)
            out_pe(pe, 1, lambda k: GG[:, k])
            leave(pe, pe_stage)
            enter(pe, S_NORM3)
            norm_pe(pe, 3)
            leave(pe, pe_stage)
            enter(pe, S_FF1)
            mlp_pe(pe, 1, MLP1, features(0), features(2))
            leave(pe, pe_stage)

        @block.scalar
        def _(act):
            own = [0]
            act.wait_ge(par_tr, 1)
            act.activation(params, ps[:, 0, 0:56], ACT.Copy)
            act.wait_ge(par_tr, 2)
            act.activation(history.rearrange("p c n -> p (c n)"), ps[:, 1, 0:192], ACT.Copy)
            leave(act, act_stage)

            enter(act, S_NORM0)
            norm_act(act, 0, own)
            leave(act, act_stage)

            enter(act, S_PROJ0)

            def silu(j):
                act.wait_ge(conv_done, j + 1)
                act.activation(conv_out(j), conv_out(j), ACT.Silu).then_inc(silu_done, 1)

            for j in range(20):
                act.wait_ge(fm_ready, j + 1)
                g = 3 * (j % 2)
                if j < KC:
                    act.wait_ge(conv_ready, j + 1)
                    u = conv_in(j)
                    act.activation(u[:, 3:3 + 2 * GN].rearrange("p (g t) -> p g t", g=2), ps[:, g:g + 2, 0:GN], ACT.Copy)
                    act.activation(u[:, 3 + 2 * GN:3 + SEQ], ps[:, g + 2, 0:256], ACT.Copy)
                    link(act, act_own, own, act.activation(
                        conv_seq(j)[:, :, 3:], ps[:, g + 2, 256:384].rearrange("p (b t) -> p b t", b=NSEQ), ACT.Copy))
                    act.activation(conv_out(j)[:, 0:SEQ], u[:, 0:SEQ], ACT.Identity, scale=conv_w[:, 0, j:j + 1],
                                   bias=conv_b[:, j:j + 1])
                    act.activation(sample(conv_out(j)), conv_seq(j)[:, :, 0:STEP], ACT.Identity,
                                   scale=conv_w[:, 0, j:j + 1], bias=conv_b[:, j:j + 1]).then_inc(fm_taken, 1)
                elif j < 12:
                    act.activation(as_groups(FQ[:, j - 8]), group(j), ACT.Copy, scale=FD ** -0.5).then_inc(fm_taken, 1)
                elif j < 16:
                    act.activation(as_groups(FK[:, j - 12]), group(j), ACT.Copy).then_inc(fm_taken, 1)
                else:
                    act.activation(as_groups(MO[:, j - 16]), group(j), ACT.Sigmoid).then_inc(fm_taken, 1)
                if 1 <= j <= KC:
                    silu(j - 1)
            act.wait_ge(gate_ready, 1)
            for g, (row, m) in enumerate(((RF, 8), (RI, 4), (RM, 4))):
                b = gbias[0:m, g:g + 1]
                act.activation(row[0:m, 0:SEQ].rearrange("p (g t) -> p g t", g=2), ps[0:m, 2 * g:2 * g + 2, :], ACT.Identity, bias=b)
                act.activation(row[0:m, SEQ:T], ps[0:m, 6, g * P:(g + 1) * P], ACT.Identity, bias=b)
            leave(act, act_stage)

            enter(act, S_GATES)
            act.wait_ge(g_a, 1)
            act.activation(TF[0:8, :], TF[0:8, :], ACT.Exp)
            link(act, act_own, own, act.activation(TM_[0:4, :], TM_[0:4, :], ACT.Exp))
            act.activation(TF[0:8, :], TF[0:8, :], ACT.Ln, bias=1.0)
            act.activation(TM_[0:4, :], TM_[0:4, :], ACT.Ln, bias=1.0).then_inc(g_b, 1)
            act.wait_ge(g_tr, 1)
            act.activation(lfT.rearrange("p n h -> p (n h)"), ps[:, 0, 0:72], ACT.Copy)
            act.activation(ibT.rearrange("p n h -> p (n h)"), ps[:, 0, 72:108], ACT.Copy)
            act.activation(enmT.rearrange("p n h -> p (n h)"), ps[:, 0, 108:144], ACT.Exp, scale=-1.0).then_inc(g_cols, 1)
            leave(act, act_stage)

            enter(act, S_FOX)
            for n in range(NT):
                act.wait_ge(fkT_ready, n + 1)
                if n >= 2:
                    act.wait_ge(fk_out[n % 2], 16 * (n // 2))
                act.activation(FKST[n % 2], ps[:, 4 + n % 2, :], ACT.Copy).then_inc(fkT_taken, 1)
            for j, (h, q) in enumerate(fox_jobs):
                act.wait_ge(f_mx, j + 1)
                if j >= 2:
                    act.wait_ge(f_pt, j - 1)
                w = (q + 1) * P
                src = ps[:, 2 * (j % 2):2 * (j % 2) + 2, :].rearrange("p b k -> p (b k)")[:, 0:w]
                act.activation(PR[j % 2][:, 0:w], src, ACT.Exp, bias=stat[:, 4 + j % 4:5 + j % 4],
                               accum_out=stat[:, 8 + j % 4:9 + j % 4]).then_inc(f_p, 1)
            for n in range(PT):
                act.wait_ge(f_ot, n + 1)
                act.activation(FQ[:, :, n * P:(n + 1) * P], ps[:, n, :].rearrange("p (c t) -> p c t", c=4), ACT.Copy)
            leave(act, act_stage)

            enter(act, S_FOXS)
            for b in range(NSEQ):
                act.wait_ge(s_kt, b + 1)
                if b >= 1:
                    act.wait_ge(s_s, b)
                act.activation(KT[:, :, 0:256], ps[:, 0:2, :].rearrange("p b (c k) -> p (b c) k", c=2), ACT.Copy).then_inc(s_kts, 1)
                act.wait_ge(s_mx, b + 1)
                if b >= 1:
                    act.wait_ge(s_pt, b)
                act.activation(SP, ps[:, 2 + b % 2, 0:384], ACT.Exp, bias=stat[:, 1:2], accum_out=stat[:, 2:3]).then_inc(s_p, 1)
                act.wait_ge(s_pt, b + 1)
                if b >= 1:
                    act.wait_ge(s_o, b)
                act.activation(SPT_, ps[:, 4, 0:384], ACT.Copy).then_inc(s_pts, 1)
            leave(act, act_stage)

            enter(act, S_ML)

            def ml_act(n):
                act.wait_ge(m_dm, n + 1)
                for h in range(MH):
                    last = act.activation(WT[:, h], WT[:, h], ACT.Exp, bias=ibT[:, n, h:h + 1])
                last.then_inc(m_w, 1)
                if n >= 1:
                    act.wait_ge(m_cn, n + 1)
                act.activation(GB.rearrange("p h t -> p (h t)"), ps[:, 1, :], ACT.Exp).then_inc(m_g, 1)

            for n in range(PT):
                ml_act(n)
                act.wait_ge(m_o, n + 1)
                act.activation(NUM[:, n].rearrange("p (b h) d -> p b (h d)", b=2), ps[:, 4:6, 0:258], ACT.Copy).then_inc(m_num, 1)
            act.wait_ge(c_ct, 1)
            act.activation(QG.rearrange("p h t -> p (h t)"), ps[:, 0, :], ACT.Copy)
            act.activation(NOUT[0:4, :], ps[0:4, 1, 0:P], ACT.Copy)
            act.activation(NCOL, ps[:, 2, 0:32], ACT.Copy)
            leave(act, act_stage)

            enter(act, S_MLS)
            ml_act(PT)
            for h in range(MH):
                act.wait_ge(c_tr, h + 1)
                act.activation(CNS[:, :, 0:128], ps[:, 0:2, :].rearrange("p b (s d) -> p (b s) d", s=4), ACT.Copy)
                act.activation(CNS[:, :, 128:129], NCOL.rearrange("p (b h) -> p b h", h=MH)[:, :, h:h + 1], ACT.Copy).then_inc(c_ev, 1)
                act.wait_ge(m_o, PT + h + 1)
                act.activation(NUM[:, PT, h], ps[:, 4, 0:129], ACT.Copy).then_inc(m_num, 1)
                act.wait_ge(c_ct, h + 2)
                act.activation(CRAW.rearrange("p (a b) d -> p a (b d)", a=2), ps[:, 0:2, :], ACT.Copy).then_inc(c_ctev, 1)
            act.wait_ge(c_ct, MH + 2)
            act.activation(NROW[0:32, :], ps[0:32, 2, 0:P], ACT.Copy)
            act.activation(KWB.rearrange("p (a b) d -> p a (b d)", a=2)[0:27], ps[0:27, 5:7, :], ACT.Copy).then_inc(c_o, 1)
            leave(act, act_stage)

            enter(act, S_MLH)
            for n in range(NT):
                for h in range(MH):
                    link(act, act_own, own, act.activation(HJUNK, NUM[:, n, h, 0:128], ACT.Square,
                                                           accum_out=SSQ[:, n * MH + h:n * MH + h + 1]))
            act.sem_inc(h_sq, 1)
            act.wait_ge(h_rt, 1)
            act.activation(HTMP, SSQ, ACT.Sqrt).then_inc(h_root, 1)
            leave(act, act_stage)

            enter(act, S_OUT0)
            leave(act, act_stage)
            enter(act, S_NORM1)
            norm_act(act, 1, own)
            leave(act, act_stage)
            enter(act, S_FF0)
            mlp_act(act, 0, features(0))
            leave(act, act_stage)
            enter(act, S_NORM2)
            norm_act(act, 2, own)
            leave(act, act_stage)

            enter(act, S_PROJ1)
            for j in range(16):
                act.wait_ge(fm_ready, 20 + j + 1)
                if j < 4:
                    act.activation(as_groups(GQ[:, j]), group(j), ACT.Copy, scale=GK ** -0.5).then_inc(fm_taken, 1)
                elif j < 8:
                    act.activation(as_groups(GKT[:, j - 4]), group(j), ACT.Copy).then_inc(fm_taken, 1)
                else:
                    act.activation(as_groups(GG[:, j - 8]), group(j), ACT.Silu).then_inc(fm_taken, 1)
            act.wait_ge(gate_ready, 2)
            act.activation(as_groups(GAT)[0:16], ps[0:16, 0:3, 0:GN], ACT.Copy)
            leave(act, act_stage)

            enter(act, S_CB)
            tmp = fm(4)
            for m in range(4):
                act.wait_ge(a_l, m + 1)
                act.activation(as_groups(CB[:, m]), group(m), ACT.Identity, bias=b_gla[:, m:m + 1]).then_inc(a_e, 1)
            for m in range(4):
                act.wait_ge(a_cb, m + 1)
                link(act, act_own, own, act.activation(tmp[:, m], tmp[:, m], ACT.Exp))
                act.activation(tmp[:, m], tmp[:, m], ACT.Ln, bias=1.0).then_inc(a_e, 1)
            leave(act, act_stage)

            enter(act, S_GLA)

            def gla_exp(n):
                act.wait_ge(l_d, 2 * n + 1)
                first = 0 if n < PT else 3
                act.activation(EL[n % 2][:, first:].rearrange("p l h t -> p (l h t)"),
                               EL[n % 2][:, first:].rearrange("p l h t -> p (l h t)"), ACT.Exp).then_inc(l_e, 1)
                act.wait_ge(l_d, 2 * n + 2)
                act.activation(KS.rearrange("p h t -> p (h t)"), KS.rearrange("p h t -> p (h t)"), ACT.Exp).then_inc(l_eb, 1)
                if n >= 1:
                    act.wait_ge(l_o, n)
                cb = CB[:, :, n * P:(n + 1) * P]
                act.activation(QE, cb, ACT.Exp)
                if n < PT:
                    act.activation(ecl[:, n % 2, :, 0:1], cb[:, :, P - 1:P], ACT.Exp).then_inc(l_eb, 1)
                else:
                    act.activation(ecl[:, n % 2], cb[:, :, STEP - 1:P:STEP], ACT.Exp).then_inc(l_eb, 1)

            def gla_norm(n):
                act.wait_ge(l_o, n + 1 if n < PT else PT + GH)
                for h in range(GH):
                    link(act, act_own, own, act.activation(junk256, ps[:, 4 + h // 2, (h % 2) * GV:(h % 2 + 1) * GV], ACT.Square,
                                                           accum_out=osum[:, h:h + 1]))
                act.sem_inc(l_osq, 1)
                act.wait_ge(l_oln, 2 * n + 1)
                link(act, act_own, own, act.activation(osum[:, 4:8], osum[:, 0:4], ACT.Ln))
                act.activation(osum[:, 4:8], osum[:, 4:8], ACT.Exp, scale=-0.5).then_inc(l_oln, 1)

            def gla_keys(n):
                act.wait_ge(l_kt, n + 1)
                act.activation(KST.rearrange("p h t -> p (h t)"), ps[:, 6, :], ACT.Copy).then_inc(l_ktev, 1)

            for n in range(PT):
                gla_exp(n)
                if n >= 1:
                    act.wait_ge(l_u, n)
                gla_keys(n)
                gla_norm(n)
            leave(act, act_stage)

            enter(act, S_GLAS)
            gla_exp(PT)
            gla_keys(PT)
            gla_norm(PT)
            leave(act, act_stage)

            enter(act, S_OUT1)
            leave(act, act_stage)
            enter(act, S_NORM3)
            norm_act(act, 3, own)
            leave(act, act_stage)
            enter(act, S_FF1)
            mlp_act(act, 1, features(2))
            leave(act, act_stage)

            enter(act, S_FINAL)
            for n in range(NT):
                link(act, act_own, own, act.activation(unit(6, D, D), tokens(4)[:, n], ACT.Square, accum_out=ssum[:, n:n + 1]))
            act.sem_inc(sq_done, 1)
            act.wait_ge(root_in, 5)
            act.activation(rstd, ssum, ACT.Sqrt).then_inc(root_ready, 1)

        @block.vector
        def _(dve):
            own = [0]

            def after(ins):
                link(dve, dve_own, own, ins)

            leave(dve, dve_stage)
            enter(dve, S_NORM0)
            norm_dve(dve, 0, own)
            leave(dve, dve_stage)

            enter(dve, S_PROJ0)

            def conv(j):
                dve.wait_ge(fm_taken, j + 1)
                u, v = conv_in(j), conv_out(j)
                for tap in range(1, TAPS):
                    w = conv_w[:, tap, j:j + 1]
                    first = dve.scalar_tensor_tensor(out=v[:, 0:SEQ], in0=u[:, tap:tap + SEQ], scalar=w, in1=v[:, 0:SEQ],
                                                     op0=ALU.mult, op1=ALU.add)
                    second = dve.scalar_tensor_tensor(out=sample(v), in0=conv_seq(j)[:, :, tap:tap + STEP], scalar=w,
                                                      in1=sample(v), op0=ALU.mult, op1=ALU.add)
                    if tap < TAPS - 1:
                        after(second)
                dve.tensor_copy(convstate[:, j, 0:3], u[:, SEQ:SEQ + 3])
                dve.tensor_copy(convstate[:, j, 3:27].rearrange("p (b t) -> p b t", b=NSEQ),
                                conv_seq(j)[:, :, STEP:STEP + 3]).then_inc(conv_done, 1)

            for j in range(KC):
                conv(j)
            for j in range(2 * NT):
                dve.wait_ge(tmj_ready, j + 1)
                n = j % NT
                src = ps[:, 6 + j % 2, :]
                if j < NT:
                    dve.tensor_copy(FV[:, n], src).then_inc(tmj_taken, 1)
                else:
                    dve.tensor_copy(MV[:, n, :, 0:128], src.rearrange("p (h d) -> p h d", h=MH)).then_inc(tmj_taken, 1)
            leave(dve, dve_stage)

            enter(dve, S_GATES)
            for row in (FN, BM, IB, MM):
                dve.memset(row, 0.0)
            dve.memset(ONES, 1.0)
            after(dve.memset(RESET, 1.0))
            dve.memset(RESET[:, starts(0)], 0.0)
            after(dve.memset(RESET[:, starts(1)], 0.0))
            dve.scalar_tensor_tensor(out=TF[0:8, :], in0=RF[0:8, :], scalar=-1.0, in1=RF[0:8, :], op0=ALU.mult, op1=ALU.min)
            dve.scalar_tensor_tensor(out=TM_[0:4, :], in0=RM[0:4, :], scalar=-1.0, in1=RM[0:4, :], op0=ALU.mult,
                                     op1=ALU.min).then_inc(g_a, 1)
            dve.wait_ge(g_b, 1)
            dve.scalar_tensor_tensor(out=LF[0:8, :], in0=RF[0:8, :], scalar=0.0, in1=TF[0:8, :], op0=ALU.min, op1=ALU.subtract)
            after(dve.scalar_tensor_tensor(out=LM[0:4, :], in0=RM[0:4, :], scalar=0.0, in1=TM_[0:4, :], op0=ALU.min,
                                           op1=ALU.subtract))
            dve.tensor_tensor_scan(FN[0:8, 0:SEQ], ONES[0:8, :], LF[0:8, 0:SEQ], 0.0, ALU.mult, ALU.subtract)
            B_ = TF
            after(dve.tensor_tensor_scan(B_[0:4, :], RESET[0:4, :], LM[0:4, :], 0.0, ALU.mult, ALU.add))
            after(dve.tensor_copy(TM_[0:4, :], RI[0:4, :]))
            after(dve.tensor_tensor(IB[0:4, :], RI[0:4, :], B_[0:4, :], ALU.subtract))
            for cols, m0 in ((slice(0, 1), mbefore[0:4, 0:1]), (slice(SEQ, T, STEP), mbefore[0:4, 1:9])):
                after(dve.tensor_tensor(RM[0:4, cols], LM[0:4, cols], m0, ALU.add))
                after(dve.tensor_tensor(TM_[0:4, cols], RM[0:4, cols], RI[0:4, cols], ALU.max))
                after(dve.memset(LM[0:4, cols], -BIG))
            after(dve.tensor_tensor_scan(MM[0:4, :], LM[0:4, :], TM_[0:4, :], 0.0, ALU.add, ALU.max))
            after(dve.tensor_tensor(BM[0:4, :], B_[0:4, :], MM[0:4, :], ALU.subtract))
            after(dve.memset(GL, 0.0))
            after(dve.tensor_copy(GL[0:4, 0:P], BM[0:4, 0:P]))
            dve.tensor_tensor(GL[0:4, P:SEQ].rearrange("p (n t) -> p n t", t=P), BM[0:4, P:SEQ].rearrange("p (n t) -> p n t", t=P),
                              MM[0:4, P - 1:SEQ - 1:P].unsqueeze(2).broadcast_to([4, PT - 1, P]), ALU.add)
            dve.tensor_tensor(sample(GL)[0:4], sample(BM)[0:4],
                              mbefore[0:4, 1:9].unsqueeze(2).broadcast_to([4, NSEQ, STEP]), ALU.add).then_inc(g_rows, 1)
            leave(dve, dve_stage)

            enter(dve, S_FOX)

            def queries(h):
                if h == 0:
                    dve.wait_ge(f_qz, 1)
                if h >= 2:
                    dve.wait_ge(f_s, PT * (h - 1))
                r = 64 * (h % 2)
                dve.tensor_copy(QZ[h % 2][r:r + 64, :], FQ[r:r + 64, h // 2, 0:SEQ]).then_inc(f_qz, 1)

            def biggest(j):
                h, q = fox_jobs[j]
                w = (q + 1) * P
                dve.wait_ge(f_s, j + 1)
                src = ps[:, 2 * (j % 2):2 * (j % 2) + 2, :].rearrange("p b k -> p (b k)")[:, 0:w]
                top = stat[:, 16 + j % 4:17 + j % 4]
                after(dve.tensor_reduce(top, src, AX.X, ALU.max))
                dve.tensor_scalar(stat[:, 4 + j % 4:5 + j % 4], top, -1.0, None, ALU.mult).then_inc(f_mx, 1)

            def probs_out(j):
                h, q = fox_jobs[j]
                w = (q + 1) * P
                dve.wait_ge(f_pt, j + 1)
                if j >= 2:
                    dve.wait_ge(f_o, j - 1)
                dve.tensor_copy(PTS[j % 2][:, 0:w], ps[:, 4:6, :].rearrange("p b k -> p (b k)")[:, 0:w]).then_inc(f_pts, 1)

            def output(j):
                h, q = fox_jobs[j]
                inverse = stat[:, 12 + j % 2:13 + j % 2]
                dve.wait_ge(f_o, j + 1)
                after(dve.reciprocal(inverse, stat[:, 8 + j % 4:9 + j % 4]))
                dve.tensor_scalar(otok[:, q, h * FD:(h + 1) * FD], ps[:, 6 + j % 2, 0:FD], inverse, None,
                                  ALU.mult).then_inc(f_oev, 1)

            dve.wait_ge(fk_out[0], 16 * 5)
            dve.wait_ge(fk_out[1], 16 * 4)
            queries(0)
            queries(1)
            biggest(0)
            for j in range(NJ):
                if j + 1 < NJ:
                    biggest(j + 1)
                probs_out(j)
                if j % PT == 0 and 2 <= j // PT + 1 < FH:
                    queries(j // PT + 1)
                if j >= 1:
                    output(j - 1)
            output(NJ - 1)
            leave(dve, dve_stage)

            enter(dve, S_FOXS)
            dve.tensor_copy(KT[:, :, 256:384], FK[:, :, SEQ:T])
            dve.wait_ge(pastlf_in, 32)
            dve.wait_ge(s_q, 1)
            plf = PLF.rearrange("p (b j h) -> p b j h", b=NSEQ, j=2)
            after(dve.tensor_tensor(LNEW.rearrange("p (h q) -> p h q", q=STEP), lfT[:, PT].unsqueeze(2).broadcast_to([P, FH, STEP]),
                                    mask(C_C16, 16).unsqueeze(1).broadcast_to([P, FH, STEP]), ALU.mult))
            for b in range(NSEQ):
                if b >= 1:
                    dve.wait_ge(s_s, b)
                t = slice(SEQ + b * STEP, SEQ + (b + 1) * STEP)
                for r in range(2):
                    dve.tensor_copy(QB[b % 2][64 * r:64 * r + 64].rearrange("p (c x) -> p c x", x=160)[:, :, r * 16:r * 16 + 16],
                                    FQ[64 * r:64 * r + 64, :, t])
                for jt in range(2):
                    dve.tensor_copy(LP[:, jt].rearrange("p (h q) -> p h q", q=STEP),
                                    plf[:, b, jt].unsqueeze(2).broadcast_to([P, FH, STEP]))
                dve.tensor_scalar(LP[:, 2], LNEW, mask(C_IND + b, 1), None, ALU.mult).then_inc(s_q, 1)
                dve.wait_ge(s_s, b + 1)
                after(dve.tensor_reduce(stat[:, 0:1], ps[:, 2 + b % 2, 0:384], AX.X, ALU.max))
                dve.tensor_scalar(stat[:, 1:2], stat[:, 0:1], -1.0, None, ALU.mult).then_inc(s_mx, 1)
                dve.wait_ge(s_p, b + 1)
                after(dve.reciprocal(stat[:, 3:4], stat[:, 2:3]))
                dve.tensor_scalar(SP, SP, stat[:, 3:4], None, ALU.mult).then_inc(s_pn, 1)
                dve.wait_ge(s_o, b + 1)
                for r in range(2):
                    last = dve.tensor_copy(FQ[64 * r:64 * r + 64, :, t],
                                           ps[64 * r:64 * r + 64, 6, 0:128].rearrange("p (c x) -> p c x", x=32)[:, :, 16 * r:16 * r + 16])
                last.then_inc(s_oev, 1)
            leave(dve, dve_stage)

            enter(dve, S_ML)

            def ml_dve(n, m):
                t = slice(n * P, (n + 1) * P)
                dve.wait_ge(m_in, n + 1)
                dve.tensor_tensor(WT, ps[:, 0, :].rearrange("p (h t) -> p h t", h=MH),
                                  mask(m).unsqueeze(1).broadcast_to([P, MH, P]), ALU.add).then_inc(m_dm, 1)
                dve.wait_ge(m_g, n + 1)
                if n >= 1:
                    dve.wait_ge(m_o, n)
                dve.tensor_tensor(QG, MQ[:, :, t], GB, ALU.mult)
                dve.wait_ge(m_w, n + 1)
                dve.tensor_tensor(AT, WT, ps[:, 2, :].rearrange("p (h t) -> p h t", h=MH), ALU.mult).then_inc(m_a, 1)

            for n in range(PT):
                if n >= 1:
                    dve.wait_ge(m_a, n)
                ml_dve(n, C_MC)
                if n >= 1:
                    dve.wait_ge(m_u, n)
                for h in range(MH):
                    last = dve.tensor_scalar(KW[:, h], ps[:, 3, h * P:(h + 1) * P], WT[:, h, P - 1:P], None, ALU.mult)
                last.then_inc(m_kw, 1)
                dve.wait_ge(m_u, n + 1)
                for h in range(MH):
                    last = dve.scalar_tensor_tensor(out=CN[:, h], in0=CN[:, h], scalar=GB[:, h, P - 1:P],
                                                    in1=ps[:, 6 + h // 2, (h % 2) * 129:(h % 2 + 1) * 129],
                                                    op0=ALU.mult, op1=ALU.add)
                if n < PT - 1:
                    last.then_inc(m_cn, 1)
                else:
                    after(last)
            dve.tensor_copy(NNEW[:, 32:36].unsqueeze(2), CN[:, :, 128:129]).then_inc(m_cn, 1)
            leave(dve, dve_stage)

            enter(dve, S_MLS)
            dve.wait_ge(out_done, 16 * 8)
            ml_dve(PT, C_MB)
            dve.tensor_copy(KW.rearrange("p h t -> p (h t)"), ps[:, 3, :]).then_inc(m_kw, 1)
            dve.wait_ge(m_kw, PT + 1)
            for h in range(MH):
                if h >= 1:
                    dve.wait_ge(m_o, PT + h)
                    dve.wait_ge(c_u, h)
                dve.tensor_copy(QGB.rearrange("p (b x) -> p b x", x=144)[:, :, 0:STEP],
                                QG[:, h].rearrange("p (b t) -> p b t", b=NSEQ)).then_inc(c_qg, 1)
                for b in range(NSEQ):
                    e = b * STEP + STEP - 1
                    last = dve.tensor_scalar(KWB[:, b], KW[:, h], WT[:, h, e:e + 1], None, ALU.mult)
                last.then_inc(c_kw, 1)
                dve.wait_ge(c_u, h + 1)
                for b in range(NSEQ):
                    e = b * STEP + STEP - 1
                    last = dve.scalar_tensor_tensor(out=CNS[:, b], in0=CNS[:, b], scalar=GB[:, h, e:e + 1],
                                                    in1=ps[:, 5 + b // 3, (b % 3) * 129:(b % 3 + 1) * 129],
                                                    op0=ALU.mult, op1=ALU.add)
                after(last)
                dve.tensor_copy(NNEW[:, 0:32].rearrange("p (b h) -> p b h", h=MH)[:, :, h:h + 1], CNS[:, :, 128:129]).then_inc(c_cn, 1)
            leave(dve, dve_stage)

            enter(dve, S_MLH)
            den4 = NUM[:, :, :, 128:129].rearrange("p n h o -> p (n h) o")
            RD3 = RD.unsqueeze(2)
            after(dve.scalar_tensor_tensor(out=RD3, in0=den4, scalar=-1.0, in1=den4, op0=ALU.mult, op1=ALU.max))
            after(dve.tensor_tensor(RD, RD, enmT.rearrange("p n h -> p (n h)"), ALU.max))
            after(dve.reciprocal(HSC, RD))
            dve.wait_ge(h_sq, 1)
            after(dve.tensor_tensor(SSQ, SSQ, HSC, ALU.mult))
            after(dve.tensor_tensor(SSQ, SSQ, HSC, ALU.mult))
            dve.tensor_scalar(SSQ, SSQ, 1.0 / MD, EPS, ALU.mult, ALU.add).then_inc(h_rt, 1)
            dve.wait_ge(h_root, 1)
            after(dve.reciprocal(RD, HTMP))
            after(dve.tensor_tensor(HSC, HSC, RD, ALU.mult))

            def mix(n):
                dve.wait_ge(h_tr, n + 1)
                for h in range(MH):
                    v = MO[:, h, n * P:(n + 1) * P]
                    last = dve.scalar_tensor_tensor(out=v, in0=ps[:, n % 4, h * P:(h + 1) * P], scalar=g_ml[:, h:h + 1], in1=v,
                                                    op0=ALU.mult, op1=ALU.mult)
                last.then_inc(h_mix, 1)

            for n in range(NT):
                if n >= 2:
                    mix(n - 2)
                dve.tensor_tensor(HST[:, n % 2].rearrange("p (h d) -> p h d", h=MH), NUM[:, n, :, 0:128],
                                  HSC[:, n * MH:(n + 1) * MH].unsqueeze(2).broadcast_to([P, MH, MD]), ALU.mult).then_inc(h_hs, 1)
            mix(NT - 2)
            mix(NT - 1)
            leave(dve, dve_stage)

            enter(dve, S_OUT0)
            dve.wait_ge(xb_in, 16 * NT)
            out_dve(dve, 0, tokens(2))
            leave(dve, dve_stage)
            enter(dve, S_NORM1)
            norm_dve(dve, 1, own)
            leave(dve, dve_stage)
            enter(dve, S_FF0)
            mlp_dve(dve, 0, tokens(2), features(0))
            leave(dve, dve_stage)
            enter(dve, S_NORM2)
            norm_dve(dve, 2, own)
            leave(dve, dve_stage)

            enter(dve, S_PROJ1)
            for j in range(2 * NT):
                dve.wait_ge(tmj_ready, 2 * NT + j + 1)
                half, n = j // NT, j % NT
                dve.tensor_copy(GVT[:, n, half * SLAB:(half + 1) * SLAB], ps[:, 6 + j % 2, :]).then_inc(tmj_taken, 1)
            leave(dve, dve_stage)

            enter(dve, S_CB)
            tmp = fm(4)
            for m in range(4):
                dve.wait_ge(a_e, m + 1)
                dve.scalar_tensor_tensor(out=tmp[:, m], in0=CB[:, m], scalar=-1.0, in1=CB[:, m], op0=ALU.mult,
                                         op1=ALU.min).then_inc(a_cb, 1)
            dve.wait_ge(a_pre, 1)
            for m in range(4):
                dve.wait_ge(a_e, 4 + m + 1)
                after(dve.scalar_tensor_tensor(out=tmp[:, m], in0=CB[:, m], scalar=0.0, in1=tmp[:, m], op0=ALU.min,
                                               op1=ALU.subtract))
                after(dve.tensor_scalar(tmp[:, m], tmp[:, m], 1.0 / TAU, None, ALU.mult))
                dve.tensor_tensor_scan(CB[:, m], RESET, tmp[:, m], 0.0, ALU.mult, ALU.add)
            leave(dve, dve_stage)

            enter(dve, S_GLA)

            def gla_factors(n):
                t = slice(n * P, (n + 1) * P)
                dve.wait_ge(l_e, n + 1)
                for l, w in enumerate(LEVELS):
                    if n == PT and w > 8:
                        continue
                    e = EL[n % 2][:, l].rearrange("p h (n w) -> p h n w", w=2 * w)
                    k = GKT[:, :, t].rearrange("p h (n w) -> p h n w", w=2 * w)
                    q = GQ[:, :, t].rearrange("p h (n w) -> p h n w", w=2 * w)
                    dve.tensor_tensor(e[:, :, :, 0:w], e[:, :, :, 0:w], k[:, :, :, 0:w], ALU.mult)
                    last = dve.tensor_tensor(e[:, :, :, w:2 * w], e[:, :, :, w:2 * w], q[:, :, :, w:2 * w], ALU.mult)
                last.then_inc(l_m, 1)
                dve.wait_ge(l_eb, 2 * n + 1)
                dve.tensor_tensor(KS, KS, GKT[:, :, t], ALU.mult).then_inc(l_ks, 1)
                dve.wait_ge(l_eb, 2 * n + 2)
                if n < PT:
                    dve.tensor_tensor(QE, QE, GQ[:, :, t], ALU.mult).then_inc(l_qe, 1)
                else:
                    after(dve.tensor_tensor(QE, QE, GQ[:, :, t], ALU.mult))

            def gla_levels(n, h):
                q = 5 * n + h
                first = 0 if n < PT else 3
                dve.wait_ge(l_a, 4 * n + h + 1)
                if n >= 1 and h == 0:
                    dve.wait_ge(l_o, n)
                b = 2 * (q % 2)
                src = ps[:, b:b + 2, :].rearrange("p b (l t) -> p (b l) t", t=P)
                if n or h:
                    dve.wait_ge(l_at, 4 * n + h)
                dve.tensor_tensor(LT[:, first:], src[:, first:], sel[:, first:], ALU.mult).then_inc(l_free, 1)
                dve.wait_ge(l_free, q + 1)
                dve.tensor_reduce(LA[:, h], LT[:, first:].rearrange("p l t -> p t l"), AX.X, ALU.add).then_inc(l_at, 1)

            def gla_scale(n):
                dve.wait_ge(l_osq, n + 1)
                dve.tensor_scalar(osum[:, 0:4], osum[:, 0:4], 1.0 / GV, EPS, ALU.mult, ALU.add).then_inc(l_oln, 1)
                dve.wait_ge(l_oln, 2 * n + 2)
                if n >= 1:
                    dve.wait_ge(l_otr, n)
                for h in range(GH):
                    last = dve.tensor_scalar(OO[:, h], ps[:, 4 + h // 2, (h % 2) * GV:(h % 2 + 1) * GV],
                                             osum[:, 4 + h:5 + h], None, ALU.mult)
                last.then_inc(l_osc, 1)

            def gla_mix(n):
                q = 5 * n + 4
                dve.wait_ge(l_otr, n + 1)
                for c in range(8):
                    v = GG[:, c, n * P:(n + 1) * P]
                    last = dve.scalar_tensor_tensor(out=v, in0=ps[:, 2 * (q % 2) + c // 4, (c % 4) * P:(c % 4 + 1) * P],
                                                    scalar=g_gla[:, c:c + 1], in1=v, op0=ALU.mult, op1=ALU.mult)
                last.then_inc(l_free, 1)

            for n in range(PT):
                gla_factors(n)
                for h in range(GH):
                    gla_levels(n, h)
                dve.wait_ge(l_u, n + 1)
                for h in range(GH):
                    dve.scalar_tensor_tensor(out=SS[:, h], in0=SS[:, h], scalar=ecl[:, n % 2, h, 0:1],
                                             in1=ps[:, 6 + h // 2, (h % 2) * GV:(h % 2 + 1) * GV],
                                             op0=ALU.mult, op1=ALU.add).then_inc(l_sn, 1)
                gla_scale(n)
                gla_mix(n)
            leave(dve, dve_stage)

            enter(dve, S_GLAS)
            dve.wait_ge(l_v, 1)
            gla_factors(PT)
            for h in range(GH):
                gla_levels(PT, h)
            dve.wait_ge(l_ktev, PT + 1)
            for h in range(GH):
                if h >= 1:
                    dve.wait_ge(l_o, PT + h)
                    dve.wait_ge(l_u, PT + NSEQ * h)
                dve.tensor_copy(QEB.rearrange("p (b x) -> p b x", x=144)[:, :, 0:STEP],
                                QE[:, h].rearrange("p (b t) -> p b t", b=NSEQ)).then_inc(l_qe, 1)
                for b in range(NSEQ):
                    last = dve.tensor_scalar(KEB[:, b], KST[:, h], mask(C_IND + b, 1), None, ALU.mult)
                last.then_inc(l_keb, 1)
                if h >= 2:
                    dve.wait_ge(st_out[h % 2], 32 * (h // 2))
                for b in range(NSEQ):
                    g = NSEQ * h + b
                    dve.wait_ge(l_u, PT + g + 1)
                    dve.scalar_tensor_tensor(out=SNEW[h % 2][:, b // 4, b % 4], in0=SIN[h % 2][:, b // 4, b % 4],
                                             scalar=ecl[:, PT % 2, h, b:b + 1], in1=ps[:, 6 + g % 2, 0:GV],
                                             op0=ALU.mult, op1=ALU.add).then_inc(l_sn, 1)
            gla_scale(PT)
            gla_mix(PT)
            leave(dve, dve_stage)

            enter(dve, S_OUT1)
            dve.wait_ge(respill_in, 16)
            out_dve(dve, 1, tokens(4))
            leave(dve, dve_stage)
            enter(dve, S_NORM3)
            norm_dve(dve, 3, own)
            leave(dve, dve_stage)
            enter(dve, S_FF1)
            mlp_dve(dve, 1, tokens(4), features(2))
            leave(dve, dve_stage)

            enter(dve, S_FINAL)
            dve.wait_ge(sq_done, 5)
            dve.tensor_scalar(ssum, ssum, 1.0 / D, EPS, ALU.mult, ALU.add).then_inc(root_in, 1)
            dve.wait_ge(root_ready, 5)
            after(dve.reciprocal(ssum, rstd))
            dve.wait_ge(gain_in, 16 * 5)
            for n in range(NT):
                if n >= 4:
                    dve.wait_ge(y_out[n % 4], 16 * (n // 4))
                dve.scalar_tensor_tensor(out=unit(0, D, (n % 4) * D), in0=tokens(4)[:, n], scalar=ssum[:, n:n + 1],
                                         in1=unit(6, D), op0=ALU.mult, op1=ALU.mult).then_inc(y_ready, 1)


INPUTS = ["x_prompt", "x_sample", "cache_fox_k", "cache_fox_v", "cache_fox_logf", "state_mlstm_c", "state_mlstm_n",
          "state_mlstm_m", "state_mlstm_conv", "state_gla_s", "norm_mix", "norm_ffn", "norm_final", "w_in_even",
          "b_fox_f", "conv_w_ml", "conv_b_ml", "b_ml_i", "b_ml_f", "g_ml", "w_in_odd", "w_gla_a2", "b_gla_a", "g_gla",
          "w_out", "w_ff1", "w_ff2"]
OUTPUTS = {
    "y_prompt": (1, SEQ, D), "y_sample": (NSEQ, STEP, D),
    "p_fox_k": (1, 1, SEQ, FH, FD), "p_fox_v": (1, 1, SEQ, FH, FD), "p_fox_logf": (1, 1, SEQ, FH),
    "p_mlstm_c": (1, 1, MH, MD, MD), "p_mlstm_n": (1, 1, MH, MD), "p_mlstm_m": (1, 1, MH),
    "p_mlstm_conv": (1, 1, 3, D), "p_gla_s": (1, 1, GH, GK, GV),
    "s_fox_k": (1, NSEQ, STEP, FH, FD), "s_fox_v": (1, NSEQ, STEP, FH, FD), "s_fox_logf": (1, NSEQ, STEP, FH),
    "s_mlstm_c": (1, NSEQ, MH, MD, MD), "s_mlstm_n": (1, NSEQ, MH, MD), "s_mlstm_m": (1, NSEQ, MH),
    "s_mlstm_conv": (1, NSEQ, 3, D), "s_gla_s": (1, NSEQ, GH, GK, GV),
}


def kernel(**inputs):
    import concourse.bacc as bacc
    from concourse.bass_utils import run_bass_kernel_spmd

    nc = bacc.Bacc("TRN2", target_bir_lowering=False, num_devices=1, dynamic_dma_scratch_size=2048)
    arrays, i, o = {}, {}, {}
    for name in INPUTS:
        arrays[name] = np.ascontiguousarray(inputs[name])
    arrays.update(constants())
    for name, a in arrays.items():
        i[name] = nc.dram_tensor(name, a.shape, F32, kind="ExternalInput").ap()
    for name, shape in OUTPUTS.items():
        o[name] = nc.dram_tensor("out_" + name, shape, F32, kind="ExternalOutput").ap()
    scratch = nc.dram_tensor("stream", (P, NT * D), F32, kind="Internal").ap()
    streaming_step(nc, i, o, scratch)
    r = run_bass_kernel_spmd(nc, [arrays], core_ids=[0])
    return tuple(r.results[0]["out_" + name] for name in OUTPUTS)
```

```python
from contextlib import ExitStack

import numpy as np

import concourse.bass as bass
from concourse import mybir

F32 = mybir.dt.float32
F32R = mybir.dt.float32r
ALU = mybir.AluOpType
ACT = mybir.ActivationFunctionType
AX = mybir.AxisListType

P = 128
D = 1024
KC = D // P
SEQ, NSEQ, STEP, PAST = 1024, 8, 16, 256
T = SEQ + NSEQ * STEP
NT = T // P
PT = SEQ // P
GN = T // 3
FH, FD = 8, 64
MH, MD = 4, 128
GH, GK, GV = 4, 128, 256
TAPS = 4
FF = 4 * D
SLAB = 2048
COLS = 256
EPS = 1e-6
BIG = 1e30
TAU = 16.0
LEVELS = [64, 32, 16, 8, 4, 2, 1]
UNIT = 4672
UPAD = 3 + SEQ + NSEQ * (STEP + 3)

E_FQ, E_FK, E_FV, E_FF, E_MQK, E_MV, E_MO, E_MI, E_MF = 0, 512, 1024, 1536, 1544, 2568, 3080, 3592, 3596
O_GQ, O_GK, O_GV, O_GG, O_GA = 0, 512, 1024, 2048, 3072

C_ID, C_MQ, C_MC, C_MB, C_ONE, C_MW, C_IND, C_C16 = 0, 128, 256, 384, 512, 640, 880, 888
C_N = 904


def constants():
    a, b = np.arange(P)[:, None], np.arange(P)[None, :]
    same = (a // STEP) == (b // STEP)
    c = np.zeros((P, C_N), np.float32)
    c[:, C_ID:C_ID + P] = np.eye(P)
    c[:, C_MQ:C_MQ + P] = np.where(b <= a, 0, -BIG)
    c[:, C_MC:C_MC + P] = np.where(a <= b, 0, -BIG)
    c[:, C_MB:C_MB + P] = np.where((a <= b) & same, 0, -BIG)
    c[:, C_ONE:C_ONE + P] = 1
    wide = np.full((P, 240), -BIG, np.float32)
    wide[:, 112:128] = np.where(np.arange(STEP)[None, :] <= (np.arange(P) % STEP)[:, None], 0, -BIG)
    c[:, C_MW:C_MW + 240] = wide
    c[:, C_IND:C_IND + 8] = (a // STEP) == np.arange(NSEQ)[None, :]
    c[:, C_C16:C_C16 + 16] = (a % STEP) <= np.arange(STEP)[None, :]
    sel = np.zeros((P, 8, P), np.float32)
    for h in range(8):
        sel[h, h, :] = 1
    gmask = np.zeros((P, 8, P), np.float32)
    for i, w in enumerate(LEVELS):
        gmask[:, i] = (a // (2 * w) == b // (2 * w)) & (a % (2 * w) < w) & (b % (2 * w) >= w)
    gmask[:, 7] = np.eye(P)
    later = np.zeros((P, 3, 384), np.float32)
    strict = (b < a).astype(np.float32)
    later[:, 0, 0:128] = strict
    later[:, 1, 0:128] = 1
    later[:, 1, 128:256] = strict
    later[:, 2, 0:256] = 1
    later[:, 2, 256:384] = strict * same
    return {"c_masks": c, "c_sel": sel.reshape(P, 1024), "c_levels": gmask.reshape(P, 1024),
            "c_later": later.reshape(P, 1152)}


def link(eng, sem, count, instruction):
    count[0] += 1
    instruction.then_inc(sem, 1)
    eng.wait_ge(sem, count[0])


def streaming_step(nc, i, o, scratch, park_mo, park_mv, park_gv):
    ctx = ExitStack()
    with ctx:
        def sb(name, shape):
            return ctx.enter_context(nc.sbuf_tensor(name, shape, F32))

        def sem(name):
            return ctx.enter_context(nc.semaphore(name))

        at_units = -(-nc.sbuf_base // 32) * 32
        pairs = [sb(f"units{2 * q}", [P, 2 * UNIT]) for q in range(4)]
        pairs_r = [nc.alloc_sbuf_tensor_at(f"units{2 * q}_r", [P, 2 * UNIT], F32R, offset=at_units + q * 8 * UNIT)
                   for q in range(4)]

        def span(start, end, of=pairs):
            q = start // (2 * UNIT)
            assert end <= (q + 1) * 2 * UNIT
            return of[q][:, start - q * 2 * UNIT:end - q * 2 * UNIT]

        raw = sb("raw", [P, 2, SLAB])
        at_split = -(-nc.sbuf_base // 32) * 32
        lend = sb("lend", [P, 4 * SLAB])
        split = nc.alloc_sbuf_tensor_at("split", [P, 2, 2, SLAB], F32R, offset=at_split)
        masks = sb("masks", [P, C_N])
        sel = sb("sel", [P, 8, P])
        spare = sb("spare", [P, 2048])
        glrow = sb("glrow", [P, T])
        small = sb("small", [P, 880])
        junk256 = sb("junk256", [P, GV])[:, :]
        ps = ctx.enter_context(nc.psum_tensor("ps", [P, 8, 512], F32))

        used = [0]

        def few(n):
            used[0] += n
            assert used[0] <= 880
            return small[:, used[0] - n:used[0]]

        def unit(k, n=4608, at=0):
            return span(k * UNIT + at, k * UNIT + at + n)

        def fm(k, chunks=4):
            return unit(k, chunks * T).rearrange("p (c t) -> p c t", c=chunks)

        def tm(k, width):
            return unit(k, NT * width).rearrange("p (n w) -> p n w", n=NT)

        def mask(c, n=P):
            return masks[:, c:c + n]

        ident = mask(C_ID)
        convstate = few(KC * 27).rearrange("p (c n) -> p c n", c=KC)
        history = few(KC * 24).rearrange("p (c n) -> p c n", c=KC)
        params = few(56)
        gbias = few(3)
        lfT = few(NT * 8).rearrange("p (n h) -> p n h", n=NT)
        ssum, rstd = few(NT), few(NT)
        stat = few(32)
        conv_w = params[:, 0:32].rearrange("p (j c) -> p j c", j=TAPS)
        conv_b, g_ml, b_gla, g_gla = params[:, 32:40], params[:, 40:44], params[:, 44:48], params[:, 48:56]

        pe_stage, act_stage, dve_stage, pool_stage = (sem(n) for n in ("pe_stage", "act_stage", "dve_stage", "pool_stage"))
        dve_own, act_own, pool_own = sem("dve_own"), sem("act_own"), sem("pool_own")
        raw_in = [sem("raw_in0"), sem("raw_in1")]
        hi_ready, lo_ready, slab_begun = sem("hi_ready"), sem("lo_ready"), sem("slab_begun")
        const_in, x_in, param_in, gate_in, later_in, level_in, ga_in = (
            sem(n) for n in ("const_in", "x_in", "param_in", "gate_in", "later_in", "level_in", "ga_in"))
        xb_in = sem("xb_in")
        gain_in = sem("gain_in")
        out_done = sem("out_done")
        spill_done, respill_in = sem("spill_done"), sem("respill_in")
        par_tr, par_ev = sem("par_tr"), sem("par_ev")
        sq_done, xs_ready, tr_ready, tr_taken, root_ready, root_in = (
            sem(n) for n in ("sq_done", "xs_ready", "tr_ready", "tr_taken", "root_ready", "root_in"))
        fm_ready, fm_taken, tmj_ready, tmj_taken, gate_ready = (
            sem(n) for n in ("fm_ready", "fm_taken", "tmj_ready", "tmj_taken", "gate_ready"))
        conv_ready, conv_done = sem("conv_ready"), sem("conv_done")
        g_a, g_b, g_rows, g_tr, g_cols, m0_in = (sem(n) for n in ("g_a", "g_b", "g_rows", "g_tr", "g_cols", "m0_in"))
        fkT_ready, fkT_taken = sem("fkT_ready"), sem("fkT_taken")
        fk_out = [sem("fk_out0"), sem("fk_out1")]
        f_qz, f_s, f_mx, f_p, f_pt, f_pts, f_o, f_oev, f_ot = (
            sem(n) for n in ("f_qz", "f_s", "f_mx", "f_p", "f_pt", "f_pts", "f_o", "f_oev", "f_ot"))
        s_kin, s_kt, s_kts, s_q, s_s, s_mx, s_p, s_pn, s_pt, s_pts, s_o, s_oev = (
            sem("s_" + n) for n in ("kin", "kt", "kts", "q", "s", "mx", "p", "pn", "pt", "pts", "o", "oev"))
        cache_in = [sem("cache_in0"), sem("cache_in1")]
        pastlf_in = sem("pastlf_in")
        m_in, m_dm, m_w, m_g, m_a, m_kw, m_o, m_num, m_u, m_cn = (
            sem("m_" + n) for n in ("in", "dm", "w", "g", "a", "kw", "o", "num", "u", "cn"))
        c_in, n_in, c_tr, c_ev, c_qg, c_kw, c_u, c_cn, c_ct, c_ctev, c_o, c_out = (
            sem("c_" + n) for n in ("in", "nin", "tr", "ev", "qg", "kw", "u", "cn", "ct", "ctev", "o", "out"))
        h_sq, h_root, h_rt, h_hs, h_tr, h_mix = (sem("h_" + n) for n in ("sq", "root", "rt", "hs", "tr", "mix"))
        w_y, w_add = sem("w_y"), sem("w_add")
        ff_h, ff_relu, ff_sq, ff_hi, ff_lo, ff_y, ff_add = (sem("ff_" + n) for n in ("h", "relu", "sq", "hi", "lo", "y", "add"))
        norm_hi, mix_hi, mix_lo = sem("norm_hi"), sem("mix_hi"), sem("mix_lo")
        gate_out, piece_out = [sem(f"gate_out{r}") for r in range(2)], [sem(f"piece_out{r}") for r in range(3)]
        fv_back, mv_back, mo_back, gv_back = (sem(n) for n in ("fv_back", "mv_back", "mo_back", "gv_back"))
        a_e, a_l, a_cb, a_pre = (sem("a_" + n) for n in ("e", "l", "cb", "pre"))
        l_d, l_e, l_m, l_ks, l_kt, l_ktev, l_eb, l_qe = (sem("l_" + n) for n in ("d", "e", "m", "ks", "kt", "ktev", "eb", "qe"))
        l_free, l_keb = sem("l_free"), sem("l_keb")
        l_a, l_at, l_o, l_u, l_sn, l_osq, l_oln, l_osc, l_otr, l_mix = (
            sem("l_" + n) for n in ("a", "at", "o", "u", "sn", "osq", "oln", "osc", "otr", "mix"))
        l_v = sem("l_v")
        st_in, st_out = [sem("st_in0"), sem("st_in1")], [sem("st_out0"), sem("st_out1")]
        y_ready, y_out = sem("y_ready"), [sem(f"y_out{r}") for r in range(4)]

        def columns(w, at):
            return w[:, at:at + COLS].rearrange("(k p) n -> p k n", p=P)

        def slabs_of(w, at, n):
            return [columns(w, at + COLS * c) for c in range(n)]

        we, wo_ = i["w_in_even"][0], i["w_in_odd"][0]
        first_slabs = slabs_of(we, E_MQK, 4) + slabs_of(we, E_FQ, 2) + slabs_of(we, E_FK, 2) + slabs_of(we, E_MO, 2)
        first_slabs += slabs_of(we, E_FV, 2) + slabs_of(we, E_MV, 2)
        GATES0 = len(first_slabs)
        first_slabs += [((0, 8, E_FF), (32, 4, E_MI), (64, 4, E_MF))]
        OUT0 = len(first_slabs)
        first_slabs += slabs_of(i["w_out"][0], 0, 4)
        MLP0 = len(first_slabs)
        HB = 512
        BLOCKS = FF // HB
        ODD = MLP0 + 4 * BLOCKS
        odd_slabs = slabs_of(wo_, O_GQ, 2) + slabs_of(wo_, O_GK, 2) + slabs_of(wo_, O_GG, 4) + slabs_of(wo_, O_GV, 4)
        GATES1 = ODD + len(odd_slabs)
        odd_slabs += [((0, 16, O_GA),)]
        OUT1 = ODD + len(odd_slabs)
        odd_slabs += slabs_of(i["w_out"][1], 0, 4)
        MLP1 = ODD + len(odd_slabs)

        def hi_of(act, n, blk=0, free=False):
            act.wait_ge(raw_in[n % 2], raw_count(n) + blk * 32)
            if not free:
                act.wait_ge(slab_begun, blk * 4 + n)
            act.activation(split[:, n % 2, 0, :], raw[:, n % 2, :], ACT.Copy).then_inc(hi_ready, 1)

        def lo_of(pool, n, blk=0):
            pool.wait_ge(hi_ready, blk * 4 + (n + 1))
            pool.tensor_tensor(split[:, n % 2, 1, :], raw[:, n % 2, :], split[:, n % 2, 0, :], ALU.subtract).then_inc(lo_ready, 1)

        def raw_count(n):
            more = {GATES0: 2, GATES1: 0}
            return 16 * (n // 2 + 1 + sum(m for g, m in more.items() if g <= n and g % 2 == n % 2))

        def weights(n, part, k, c0, width, chunk=COLS):
            return split[:, n % 2, part, :].rearrange("p (k n) -> p k n", n=chunk)[:, k, c0:c0 + width]

        PASSES = ((0, 0), (0, 1), (1, 0))

        def enter(eng, stage):
            for s in (pe_stage, act_stage, dve_stage, pool_stage):
                eng.wait_ge(s, stage)

        def leave(eng, s):
            eng.drain().then_inc(s, 1)

        block = ctx.enter_context(nc.Block())

        (S_LOAD, S_NORM0, S_PROJ0, S_GATES, S_FOX, S_FOXS, S_ML, S_MLS, S_MLH, S_OUT0, S_NORM1, S_FF0,
         S_NORM2, S_PROJ1, S_CB, S_GLA, S_GLAS, S_OUT1, S_NORM3, S_FF1, S_FINAL) = range(21)

        def wide(k):
            return span(k * UNIT, k * UNIT + NT * D)

        def tokens(k):
            return wide(k).rearrange("p (n d) -> p n d", n=NT)

        def features(k):
            return wide(k).rearrange("p (c t) -> p c t", c=KC)

        def part(k):
            return span(k * UNIT, k * UNIT + NT * D, pairs_r).rearrange("p (c t) -> p c t", c=KC)

        def hidden(k):
            return span(k * UNIT, k * UNIT + 4 * T, pairs_r).rearrange("p (c t) -> p c t", c=4)

        HID0, HID1 = (hidden(6), hidden(7)), (hidden(2), hidden(3))
        MQ, MK, FK, FQ = fm(4), fm(5), fm(6), fm(7)
        FV, MO = tm(0, 512), fm(6)
        MV = unit(1, NT * MH * 129).rearrange("p (n h d) -> p n h d", n=NT, h=MH)
        norms = [
            (tokens(4), 0, 2, 6, i["norm_mix"][0]),
            (tokens(2), 0, 4, 6, i["norm_ffn"][0]),
            (tokens(2), 0, 4, 6, i["norm_mix"][1]),
            (tokens(6), 0, 4, 2, i["norm_ffn"][1]),
        ]
        GQ, GKT, GG, GVT, CB = fm(6), fm(7), features(2), tokens(0), fm(4)

        def norm_parts(k):
            s = norms[k][3]
            return (unit(s, 2048).rearrange("p (b d) -> p b d", b=2), unit(s, 1024, 2048), unit(s, 1024, 3072))

        stage_of_norm = [S_NORM0, S_NORM1, S_NORM2, S_NORM3]

        def two_banks(n):
            b = 2 * (n % 4)
            return ps[:, b:b + 2, :].rearrange("p b (c t) -> p (b c) t", c=4)

        def norm_act(act, k, own):
            x, hi, _, _, _ = norms[k]
            _, junk, _ = norm_parts(k)
            if k == 0:
                act.wait_ge(x_in, 16 * NT)
            for n in range(NT):
                link(act, act_own, own, act.activation(junk, x[:, n], ACT.Square, accum_out=ssum[:, n:n + 1]))
            act.sem_inc(sq_done, 1)
            act.wait_ge(root_in, k + 1)
            act.activation(rstd, ssum, ACT.Sqrt).then_inc(root_ready, 1)
            for n in range(NT):
                act.wait_ge(tr_ready, NT * k + n + 1)
                act.activation(part(hi)[:, :, n * P:(n + 1) * P], two_banks(n), ACT.Copy).then_inc(norm_hi, 1)

        def norm_dve(dve, k, own):
            x, hi, lo, _, _ = norms[k]
            xs, _, _gain = norm_parts(k)
            dve.wait_ge(sq_done, k + 1)
            dve.tensor_scalar(ssum, ssum, 1.0 / D, EPS, ALU.mult, ALU.add).then_inc(root_in, 1)
            dve.wait_ge(root_ready, k + 1)
            link(dve, dve_own, own, dve.reciprocal(ssum, rstd))
            dve.wait_ge(gain_in, 16 * (k + 1))

            def low(n):
                t = slice(n * P, (n + 1) * P)
                dve.wait_ge(norm_hi, NT * k + n + 1)
                dve.tensor_tensor(part(lo)[:, :, t], two_banks(n), part(hi)[:, :, t], ALU.subtract).then_inc(tr_taken, 1)

            for n in range(NT):
                if n >= 2:
                    dve.wait_ge(tr_ready, NT * k + n - 1)
                dve.scalar_tensor_tensor(out=xs[:, n % 2], in0=x[:, n], scalar=ssum[:, n:n + 1], in1=_gain,
                                         op0=ALU.mult, op1=ALU.mult).then_inc(xs_ready, 1)
                if n >= 1:
                    low(n - 1)
            low(NT - 1)

        def norm_pe(pe, k):
            xs, _, _ = norm_parts(k)
            for n in range(NT):
                pe.wait_ge(xs_ready, NT * k + n + 1)
                if n >= 4:
                    pe.wait_ge(tr_taken, NT * k + n - 3)
                for c in range(KC):
                    last = pe.transpose(ps[:, 2 * (n % 4) + c // 4, (c % 4) * P:(c % 4 + 1) * P],
                                        xs[:, n % 2, c * P:(c + 1) * P], ident)
                last.then_inc(tr_ready, 1)

        def begin(instruction, first):
            if first:
                instruction.then_inc(slab_begun, 1)

        def proj_fm(pe, bank, slab, c0, h):
            for k in range(KC):
                for q, (a, b) in enumerate(PASSES):
                    for n in range(3):
                        last = pe.matmul(ps[:, bank + n, 0:GN], weights(slab, a, k, c0, P),
                                         h[b][:, k, n * GN:(n + 1) * GN],
                                         start=(k == 0 and q == 0), stop=(k == KC - 1 and q == 2))
                        begin(last, c0 == 0 and k == 0 and q == 0 and n == 0)
            return last

        def proj_tm(pe, out, slab, h, n, first):
            for k in range(KC):
                for q, (a, b) in enumerate(PASSES):
                    last = pe.matmul(out, h[b][:, k, n * P:(n + 1) * P], weights(slab, a, k, 0, COLS),
                                     start=(k == 0 and q == 0), stop=(k == KC - 1 and q == 2))
                    begin(last, first and k == 0 and q == 0)
            return last

        def group(job):
            g = 3 * (job % 2)
            return ps[:, g:g + 3, 0:GN]

        def as_groups(row):
            return row.rearrange("p (g t) -> p g t", g=3)

        def out_act(act, layer, sources):
            base = (OUT0, OUT1)[layer]
            hi_of(act, base, free=True)
            for n in range(NT):
                t = slice(n * P, (n + 1) * P)
                for c, src in enumerate(sources):
                    last = act.activation(part(0)[:, 4 * c:4 * c + 4, t], src[:, :, t], ACT.Copy)
                last.then_inc(mix_hi, 1)
                if n == 0:
                    hi_of(act, base + 1, free=True)
            for m in range(2, 5):
                hi_of(act, base + m)

        def out_pool(pool, layer):
            for m in range(5):
                lo_of(pool, (OUT0, OUT1)[layer] + m)

        def out_pe(pe, layer):
            h = part(0), part(4)
            for c in range(4):
                s = (OUT0, OUT1)[layer] + c
                pe.wait_ge(lo_ready, s + 1)
                for n in range(NT):
                    j = c * NT + n
                    if c == 0:
                        pe.wait_ge(mix_lo, NT * layer + n + 1)
                    if j >= 4:
                        pe.wait_ge(w_add, 4 * NT * layer + j - 3)
                    proj_tm(pe, ps[:, j % 4, 0:COLS], s, h, n, n == 0).then_inc(w_y, 1)

        def out_dve(dve, layer, x, sources):
            def add(j):
                dve.wait_ge(w_y, 4 * NT * layer + j + 1)
                xx = x[:, j % NT, (j // NT) * COLS:(j // NT + 1) * COLS]
                dve.tensor_tensor(xx, xx, ps[:, j % 4, 0:COLS], ALU.add).then_inc(w_add, 1)

            for n in range(NT):
                t = slice(n * P, (n + 1) * P)
                dve.wait_ge(mix_hi, NT * layer + n + 1)
                for c, src in enumerate(sources):
                    last = dve.tensor_tensor(part(4)[:, 4 * c:4 * c + 4, t], src[:, :, t],
                                             part(0)[:, 4 * c:4 * c + 4, t], ALU.subtract)
                last.then_inc(mix_lo, 1)
                if n >= 1:
                    add(n - 1)
            for j in range(NT - 1, 4 * NT):
                add(j)

        HC = HB // P
        YJ = 2 * NT
        YBANK = (6, 7, 3, 4, 5)
        YLAG = 4
        HTMP_ = (spare[:, 0:T], glrow[:, :])

        def hidden_bank(j):
            return 3 if j % 2 == 0 else 0

        def blocks(eng, body, last):
            with eng.Fori(0, BLOCKS - last) as blk:
                body(blk, False)
            if last:
                body(BLOCKS - 1, True)

        def mlp_pe(pe, layer, base, h, hid):
            def body(blk, last):
                for j in range(HC):
                    slab = base + j // 2
                    if j % 2 == 0:
                        pe.wait_ge(lo_ready, blk * 4 + (slab + 1))
                    if j >= 2:
                        pe.wait_ge(ff_relu, blk * HC + (layer * FF // P + j - 1))
                    proj_fm(pe, hidden_bank(j), slab, (j % 2) * P, h).then_inc(ff_h, 1)

                def pieces(j, chunks):
                    half, n = j // NT, j % NT
                    for k in chunks:
                        for q, (a, b) in enumerate(PASSES):
                            one = pe.matmul(ps[:, YBANK[j % 5], :], hid[b][:, k, n * P:(n + 1) * P],
                                            weights(base + 2 + half, a, k, 0, 512, 512),
                                            start=(k == 0 and q == 0), stop=(k == HC - 1 and q == 2))
                            begin(one, n == 0 and q == 0 and k == (0, HC - 1)[half])
                    return one

                for j in range(YJ + YLAG):
                    if j < YJ:
                        if j % NT == 0:
                            pe.wait_ge(lo_ready, blk * 4 + (base + 3 + j // NT))
                        if j == 0:
                            pe.wait_ge(ff_lo, blk * HC + (layer * FF // P + HC - 1))
                        if j >= 5:
                            pe.wait_ge(ff_add, blk * YJ + (layer * YJ * BLOCKS + j - 4))
                        pieces(j, range(HC - 1))
                    if j >= YLAG:
                        if j == YLAG:
                            pe.wait_ge(ff_lo, blk * HC + (layer * FF // P + HC))
                        pieces(j - YLAG, (HC - 1,)).then_inc(ff_y, 1)
                pe.wait_ge(ff_add, blk * YJ + (layer * YJ * BLOCKS + YJ))

            blocks(pe, body, 0)

        def mlp_act(act, layer, base, hid):
            def body(blk, last):
                def high(j):
                    act.wait_ge(ff_sq, blk * HC + (layer * FF // P + j + 1))
                    act.activation(hid[0][:, j], HTMP_[j % 2], ACT.Copy).then_inc(ff_hi, 1)

                for j in range(HC):
                    if j % 2 == 0:
                        hi_of(act, base + j // 2 + 1, blk)
                    act.wait_ge(ff_h, blk * HC + (layer * FF // P + j + 1))
                    if j >= 2:
                        act.wait_ge(ff_lo, blk * HC + (layer * FF // P + j - 1))
                    b = hidden_bank(j)
                    act.activation(as_groups(HTMP_[j % 2]), ps[:, b:b + 3, 0:GN], ACT.Relu).then_inc(ff_relu, 1)
                    if j >= 1:
                        high(j - 1)
                high(HC - 1)
                hi_of(act, base + 3, blk)
                if not last:
                    hi_of(act, base + 4, blk)

            blocks(act, body, layer)

        def mlp_pool(pool, layer, base):
            def body(blk, last):
                for j in range(1, 4 if last else 5):
                    lo_of(pool, base + j, blk)

            blocks(pool, body, layer)

        def mlp_dve(dve, layer, x, hid):
            def body(blk, last):
                for j in range(HC):
                    tmp = HTMP_[j % 2]
                    dve.wait_ge(ff_relu, blk * HC + (layer * FF // P + j + 1))
                    dve.tensor_tensor(tmp, tmp, tmp, ALU.mult).then_inc(ff_sq, 1)
                    dve.wait_ge(ff_hi, blk * HC + (layer * FF // P + j + 1))
                    dve.tensor_tensor(hid[1][:, j], tmp, hid[0][:, j], ALU.subtract).then_inc(ff_lo, 1)
                for j in range(YJ):
                    half, n = j // NT, j % NT
                    dve.wait_ge(ff_y, blk * YJ + (layer * YJ * BLOCKS + j + 1))
                    xx = x[:, n, half * 512:(half + 1) * 512]
                    dve.tensor_tensor(xx, xx, ps[:, YBANK[j % 5], :], ALU.add).then_inc(ff_add, 1)

            blocks(dve, body, 0)

        base2 = 2 * UNIT

        def scratch_row(n):
            return span(base2 + n * T, base2 + (n + 1) * T)

        RF, RI, RM, LF, LM, TF, TM_ = (scratch_row(n) for n in range(7))
        FN = span(base2 + 2 * UNIT - T, base2 + 2 * UNIT)
        BM, IB, MM = (lend[:, n * T:(n + 1) * T] for n in range(3))
        GL, RESET = glrow[:, :], glrow[:, :]
        ONES = spare[:, 0:SEQ]
        mbefore = few(9)
        enmT = few(NT * MH).rearrange("p (n h) -> p n h", n=NT)
        ibT = few(NT * MH).rearrange("p (n h) -> p n h", n=NT)
        ecl = few(2 * 32).rearrange("p (r h b) -> p r h b", r=2, h=GH)
        osum = few(8)

        otok = span(base2, base2 + 4096).rearrange("p (b f) -> p b f", b=PT)
        QZ = [span(base2 + 4096 + 1024 * r, base2 + 5120 + 1024 * r) for r in range(2)]
        PR = [span(base2 + 6144 + 1024 * r, base2 + 7168 + 1024 * r) for r in range(2)]
        PTS = [spare[:, 1024 * r:1024 * (r + 1)] for r in range(2)]
        FKST = [spare[:, 1024 * r:1024 * r + 512] for r in range(2)]
        fox_jobs = [(h, q) for h in range(FH) for q in range(PT)]
        NJ = len(fox_jobs)

        place = [base2]

        def take(n):
            place[0] += n
            return span(place[0] - n, place[0])

        KIN = [take(1024).rearrange("p (j f) -> p j f", j=2) for _ in range(2)]
        VIN = [take(1024).rearrange("p (j f) -> p j f", j=2) for _ in range(2)]
        KT = take(1536).rearrange("p (c k) -> p c k", c=4)
        QB = [take(640) for _ in range(2)]
        LP = take(384).rearrange("p (j r) -> p j r", j=3)
        LNEW, SP, SPT_, PLF = take(128), take(384), take(384), take(128)
        SPT = SPT_.rearrange("p (j r) -> p j r", j=3)
        assert place[0] <= base2 + 2 * UNIT
        LATER = spare[:, 0:1152].rearrange("p (j k) -> p j k", j=3)

        place[0] = base2
        WT, GB, AT, QG, KW = (take(512).rearrange("p (h t) -> p h t", h=MH) for _ in range(5))
        CN = take(MH * 129).rearrange("p (h d) -> p h d", h=MH)
        CRAW = take(1024).rearrange("p (b d) -> p b d", b=NSEQ)
        CNS = take(NSEQ * 129).rearrange("p (b d) -> p b d", b=NSEQ)
        QGB = take(NSEQ * 144)
        KWB = take(1024).rearrange("p (b d) -> p b d", b=NSEQ)
        NROW, NOUT = take(128), take(128)
        NCOL, NNEW = take(32), take(36)
        assert place[0] <= base2 + 2 * UNIT
        NUM = unit(0, NT * MH * 129).rearrange("p (n h d) -> p n h d", n=NT, h=MH)
        HST = unit(5, 1024).rearrange("p (b d) -> p b d", b=2)
        HJUNK = unit(5, 128, 1024)
        RD, SSQ, HSC, HTMP = (unit(5, 36, 1152 + 36 * r) for r in range(4))

        EL = [lend[:, 3584 * r:3584 * (r + 1)].rearrange("p (l h t) -> p l h t", l=7, h=GH)
              for r in range(2)]
        place[0] = 5 * UNIT
        LT = take(1024).rearrange("p (l t) -> p l t", l=8)
        LA = take(512).rearrange("p (h t) -> p h t", h=GH)
        QE = take(512).rearrange("p (h t) -> p h t", h=GH)
        assert place[0] <= 6 * UNIT
        KS = glrow[:, 0:512].rearrange("p (h t) -> p h t", h=GH)
        KST = glrow[:, 512:1024].rearrange("p (h t) -> p h t", h=GH)
        SS = spare[:, 0:1024].rearrange("p (h v) -> p h v", h=GH)
        OO = spare[:, 1024:2048].rearrange("p (h v) -> p h v", h=GH)
        GAT, WA2 = spare[:, 0:1152], spare[:, 1152:1664]
        SIN = [GQ[:, 2 * r:2 * r + 2, 0:SEQ].rearrange("p c (b v) -> p c b v", v=GV) for r in range(2)]
        SNEW = [GKT[:, 2 * r:2 * r + 2, 0:SEQ].rearrange("p c (b v) -> p c b v", v=GV) for r in range(2)]
        QEB = lend[:, 3584:3584 + NSEQ * 144]
        KEB = lend[:, 3584 + 1152:3584 + 2176].rearrange("p (b k) -> p b k", b=NSEQ)

        def sample(row):
            return row[:, SEQ:T].rearrange("p (b t) -> p b t", b=NSEQ)

        def starts(n):
            return slice(SEQ, T, STEP) if n else slice(0, SEQ, P)

        GATE_ST = (glrow[:, :], spare[:, 0:T])
        PIECE_ST = [spare[:, T + COLS * r:T + COLS * (r + 1)] for r in range(3)]
        def conv_in(j):
            return unit(6, UPAD, (j % 3) * UPAD)

        def conv_seq(j):
            return conv_in(j)[:, 3 + SEQ:].rearrange("p (b t) -> p b t", b=NSEQ)

        def conv_out(j):
            return (MQ if j < 4 else MK)[:, j % 4]

        @block.sync
        def _(sp):
            def place_of(n, chunk):
                return raw[:, n % 2, :].rearrange("p (k n) -> p k n", n=chunk)

            def load(n, src):
                if n >= 2:
                    sp.wait_ge(lo_ready, n - 1)
                if isinstance(src, tuple):
                    for at, width, column in src:
                        w = we if n == GATES0 else wo_
                        sp.dma_start(place_of(n, COLS)[:, :, at:at + width],
                                     w[:, column:column + width].rearrange("(k p) n -> p k n", p=P)).then_inc(raw_in[n % 2], 16)
                else:
                    sp.dma_start(place_of(n, COLS), src).then_inc(raw_in[n % 2], 16)

            for n, src in enumerate(first_slabs):
                load(n, src)

            def mlp(layer, base):
                w1 = i["w_ff1"][layer].rearrange("(k p) (b n) -> b p k n", p=P, n=COLS)
                w2 = i["w_ff2"][layer].rearrange("(b k p) n -> b p k n", p=P, k=HC)
                with sp.Fori(0, BLOCKS) as blk:
                    for j, w in ((0, w1), (1, w1), (2, w2), (3, w2)):
                        n = base + j
                        sp.wait_ge(lo_ready, blk * 4 + (n - 1))
                        src = w[bass.ds(blk * 2 + j, 1)] if j < 2 else w[bass.ds(blk, 1), :, :, (j - 2) * 512:(j - 1) * 512]
                        src = src.rearrange("o p k n -> (o p) k n")
                        sp.dma_start(place_of(n, COLS if j < 2 else 512), src).then_inc(raw_in[n % 2], 16)

            mlp(0, MLP0)
            for n, src in enumerate(odd_slabs):
                load(ODD + n, src)
            mlp(1, MLP1)

        @block.gpsimd
        def _(pool):
            outs, pown = [0], [0]

            def put(dst, src):
                outs[0] += 16
                pool.dma_start(dst, src).then_inc(out_done, 16)

            pool.dma_start(masks[:, :], i["c_masks"]).then_inc(const_in, 16)
            pool.dma_start(sel.rearrange("p h t -> p (h t)"), i["c_sel"]).then_inc(const_in, 16)
            rows = unit(0, P)
            for r, src in ((0, i["conv_w_ml"][0].rearrange("j (c p) -> (j c) p", p=P)),
                           (32, i["conv_b_ml"][0].rearrange("(c p) -> c p", p=P)),
                           (40, i["g_ml"][0].rearrange("(c p) -> c p", p=P)),
                           (44, i["b_gla_a"][0].rearrange("(c p) -> c p", p=P)),
                           (48, i["g_gla"][0].rearrange("(c p) -> c p", p=P))):
                pool.dma_start(rows[r:r + src.shape[0], :], src).then_inc(param_in, 16)
            pool.dma_start(unit(0, D, P)[0:24, :], i["state_mlstm_conv"][0].rearrange("b j f -> (b j) f")).then_inc(param_in, 16)
            pool.dma_start(gbias[0:8, 0:1], i["b_fox_f"].rearrange("o h -> h o")).then_inc(gate_in, 16)
            pool.dma_start(gbias[0:4, 1:2], i["b_ml_i"].rearrange("o h -> h o")).then_inc(gate_in, 16)
            pool.dma_start(gbias[0:4, 2:3], i["b_ml_f"].rearrange("o h -> h o")).then_inc(gate_in, 16)
            with nc.allow_non_contiguous_dma(reason="32 values"):
                pool.dma_start(mbefore[0:4, 1:9], i["state_mlstm_m"][0].rearrange("b h -> h b")).then_inc(gate_in, 16)
            x = tokens(4)
            for n in range(PT):
                pool.dma_start(x[:, n], i["x_prompt"][0, n * P:(n + 1) * P, :]).then_inc(x_in, 16)
            pool.dma_start(x[:, PT], i["x_sample"].rearrange("b t d -> (b t) d")).then_inc(x_in, 16)
            pool.memset(mbefore[0:4, 0:1], 0.0)
            leave(pool, pool_stage)

            def gain(k):
                pool.dma_start(norm_parts(k)[2], norms[k][4].partition_broadcast(P)).then_inc(gain_in, 16)

            enter(pool, S_NORM0)
            gain(0)
            lo_of(pool, 0)
            lo_of(pool, 1)
            leave(pool, pool_stage)

            def piece_to(j):
                c, n = j // NT, j % NT
                if c < 2 and n < PT:
                    return o["p_fox_v"][0, 0, n * P:(n + 1) * P, 4 * c:4 * c + 4, :].rearrange("t h d -> t (h d)")
                if c < 2:
                    return o["s_fox_v"][0, :, :, 4 * c:4 * c + 4, :].rearrange("b t h d -> (b t) (h d)")
                to, c = (park_mv, c - 2) if c < 4 else (park_gv, c - 4)
                return to[n * P:(n + 1) * P, c * COLS:(c + 1) * COLS]

            def pieces_out(first):
                for j in range(first, first + NT):
                    pool.wait_ge(tmj_taken, j + 1)
                    pool.dma_start(piece_to(j), PIECE_ST[j % 3]).then_inc(piece_out[j % 3], 16)

            def all_pieces_out(n):
                for r in range(3):
                    pool.wait_ge(piece_out[r], 16 * (n // 3))

            enter(pool, S_PROJ0)
            for r in range(3):
                last = pool.memset(conv_in(r)[:, 0:3], 0.0)
            last.then_inc(conv_ready, 1)
            for m in range(1, GATES0):
                lo_of(pool, m + 1)
                if m in (8, 9):
                    for c in (2 * m - 16, 2 * m - 15):
                        pool.wait_ge(fm_taken, 16 + c + 1)
                        pool.dma_start(park_mo[:, c], GATE_ST[c % 2]).then_inc(gate_out[c % 2], 16)
                elif m >= 10:
                    pieces_out(NT * (m - 10))
            pool.wait_ge(gate_out[0], 32)
            pool.wait_ge(gate_out[1], 32)
            all_pieces_out(4 * NT)
            leave(pool, pool_stage)

            enter(pool, S_GATES)
            pool.dma_start(FV[:, 0:PT], o["p_fox_v"][0, 0].rearrange("(n p) h d -> p n (h d)", p=P)).then_inc(fv_back, 16)
            pool.dma_start(FV[:, PT], o["s_fox_v"][0].rearrange("b t h d -> (b t) (h d)")).then_inc(fv_back, 16)
            pool.memset(MV[:, :, :, 128:129], 1.0)
            for n in range(NT):
                pool.dma_start(MV[:, n, :, 0:128],
                               park_mv[n * P:(n + 1) * P].rearrange("p (h d) -> p h d", h=MH)).then_inc(mv_back, 16)
            pool.wait_ge(g_cols, 1)
            put(o["p_fox_logf"][0, 0].rearrange("(n p) h -> p n h", p=P), lfT[:, 0:PT])
            put(o["s_fox_logf"][0].rearrange("b t h -> (b t) h"), lfT[:, PT])
            pool.wait_ge(g_rows, 1)
            with nc.allow_non_contiguous_dma(reason="36 values"):
                put(o["p_mlstm_m"][0].rearrange("o h -> h o"), MM[0:4, SEQ - 1:SEQ])
                put(o["s_mlstm_m"][0].rearrange("b h -> h b"), MM[0:4, SEQ + STEP - 1:T:STEP])
            leave(pool, pool_stage)

            enter(pool, S_FOX)
            pool.memset(QZ[0][64:128, :], 0.0)
            pool.memset(QZ[1][0:64, :], 0.0).then_inc(f_qz, 1)
            for n in range(NT):
                pool.wait_ge(fkT_taken, n + 1)
                dst = o["p_fox_k"][0, 0, n * P:(n + 1) * P].rearrange("t h d -> t (h d)") if n < PT \
                    else o["s_fox_k"][0].rearrange("b t h d -> (b t) (h d)")
                pool.dma_start(dst, FKST[n % 2]).then_inc(fk_out[n % 2], 16)
            pool.wait_ge(fk_out[0], 16 * 5)
            pool.wait_ge(fk_out[1], 16 * 4)
            leave(pool, pool_stage)

            enter(pool, S_FOXS)
            pool.memset(QB[0], 0.0)
            pool.memset(QB[1], 0.0).then_inc(s_q, 1)
            pool.dma_start(LATER.rearrange("p j k -> p (j k)"), i["c_later"]).then_inc(later_in, 16)
            for jt in range(2):
                pool.dma_start(PLF.rearrange("p (b j h) -> p b j h", b=NSEQ, j=2)[:, :, jt],
                               i["cache_fox_logf"][0, :, jt * P:(jt + 1) * P].rearrange("b p h -> p b h")).then_inc(pastlf_in, 16)
            for b in range(NSEQ):
                if b >= 2:
                    pool.wait_ge(s_o, b - 1)
                for buf, src in ((KIN, i["cache_fox_k"]), (VIN, i["cache_fox_v"])):
                    pool.dma_start(buf[b % 2], src[0, b].rearrange("(j p) h d -> p j (h d)", p=P)).then_inc(cache_in[b % 2], 16)
            leave(pool, pool_stage)

            enter(pool, S_ML)
            pool.dma_start(fm(6), park_mo).then_inc(mo_back, 16)
            pool.memset(CN.rearrange("p h d -> p (h d)"), 0.0).then_inc(m_cn, 1)
            pool.memset(QGB, 0.0)
            pool.dma_start(NROW[0:32, :], i["state_mlstm_n"][0].rearrange("b h d -> (b h) d")).then_inc(n_in, 16)
            pool.dma_start(CRAW, i["state_mlstm_c"][0, :, 0].rearrange("b e d -> e b d")).then_inc(c_in, 16)
            leave(pool, pool_stage)

            enter(pool, S_MLS)
            put(o["p_mlstm_c"][0, 0].rearrange("h e d -> e h d"), QG)
            put(o["p_mlstm_n"][0, 0], NOUT[0:4, :])
            for h in range(MH):
                pool.wait_ge(c_ctev, h + 1)
                pool.dma_start(o["s_mlstm_c"][0, :, h].rearrange("b e d -> e b d"), CRAW).then_inc(c_out, 16)
                if h < MH - 1:
                    pool.wait_ge(c_out, 16 * (h + 1))
                    pool.dma_start(CRAW, i["state_mlstm_c"][0, :, h + 1].rearrange("b e d -> e b d")).then_inc(c_in, 16)
            pool.wait_ge(c_out, 16 * MH)
            pool.wait_ge(c_o, 1)
            put(o["s_mlstm_n"][0].rearrange("b h d -> (b h) d"), NROW[0:32, :])
            leave(pool, pool_stage)

            enter(pool, S_MLH)
            cs = KWB.rearrange("p b d -> p (b d)")
            put(o["p_mlstm_conv"][0, 0], cs[0:3, :])
            put(o["s_mlstm_conv"][0].rearrange("b j f -> (b j) f"), cs[3:27, :])
            pool.wait_ge(out_done, outs[0])
            leave(pool, pool_stage)

            enter(pool, S_OUT0)
            x = tokens(2)
            for n in range(PT):
                pool.dma_start(x[:, n], i["x_prompt"][0, n * P:(n + 1) * P, :]).then_inc(xb_in, 16)
            pool.dma_start(x[:, PT], i["x_sample"].rearrange("b t d -> (b t) d")).then_inc(xb_in, 16)
            out_pool(pool, 0)
            leave(pool, pool_stage)
            enter(pool, S_NORM1)
            gain(1)
            leave(pool, pool_stage)
            enter(pool, S_FF0)
            mlp_pool(pool, 0, MLP0)
            leave(pool, pool_stage)

            enter(pool, S_NORM2)
            gain(2)
            pool.dma_start(sel.rearrange("p h t -> p (h t)"), i["c_levels"]).then_inc(level_in, 16)
            pool.dma_start(scratch, wide(2)).then_inc(spill_done, 16)
            pool.wait_ge(spill_done, 16)
            leave(pool, pool_stage)

            enter(pool, S_PROJ1)
            for m in range(ODD, GATES1):
                lo_of(pool, m + 1)
                if m >= ODD + 8:
                    pieces_out(4 * NT + NT * (m - ODD - 8))
            all_pieces_out(8 * NT)
            pool.dma_start(WA2[0:16, :], i["w_gla_a2"][0]).then_inc(ga_in, 16)
            leave(pool, pool_stage)

            enter(pool, S_CB)
            pool.dma_start(GVT, park_gv.rearrange("(n p) d -> p n d", p=P)).then_inc(gv_back, 16)
            link(pool, pool_own, pown, pool.memset(RESET, 1.0))
            pool.memset(RESET[:, starts(0)], 0.0)
            pool.memset(RESET[:, starts(1)], 0.0).then_inc(a_pre, 1)
            leave(pool, pool_stage)

            enter(pool, S_GLA)
            pool.memset(SS.rearrange("p h v -> p (h v)"), 0.0).then_inc(l_sn, 1)

            def exponents(n):
                cb = CB[:, :, n * P:(n + 1) * P]
                if n >= 2:
                    pool.wait_ge(l_a, 4 * (n - 1))
                for l, w in enumerate(LEVELS):
                    if n == PT and w > 8:
                        continue
                    np_ = P // (2 * w)
                    pairs = cb.rearrange("p h (n w) -> p h n w", w=2 * w)
                    e = EL[n % 2][:, l].rearrange("p h (n w) -> p h n w", w=2 * w)
                    edge = pairs[:, :, :, w - 1:w].broadcast_to([P, GH, np_, w])
                    pool.tensor_tensor(e[:, :, :, 0:w], edge, pairs[:, :, :, 0:w], ALU.subtract)
                    last = pool.tensor_tensor(e[:, :, :, w:2 * w], pairs[:, :, :, w:2 * w], edge, ALU.subtract)
                last.then_inc(l_d, 1)
                if n >= 1:
                    pool.wait_ge(l_kt, n)
                seg = P if n < PT else STEP
                ends = cb.rearrange("p h (b t) -> p h b t", t=seg)
                pool.tensor_tensor(KS.rearrange("p h (b t) -> p h b t", t=seg),
                                   ends[:, :, :, seg - 1:seg].broadcast_to([P, GH, P // seg, seg]), ends,
                                   ALU.subtract).then_inc(l_d, 1)

            for n in range(PT):
                exponents(n)
            leave(pool, pool_stage)

            enter(pool, S_GLAS)
            put(o["p_gla_s"][0, 0].rearrange("h k v -> k h v"), SS)
            pool.memset(QEB, 0.0).then_inc(l_v, 1)
            exponents(PT)

            def state_in(h):
                for c in range(2):
                    pool.dma_start(SIN[h % 2][:, c],
                                   i["state_gla_s"][0, 4 * c:4 * c + 4, h].rearrange("b k v -> k b v")).then_inc(st_in[h % 2], 16)

            state_in(0)
            state_in(1)
            for h in range(GH):
                pool.wait_ge(l_sn, 1 + 4 * PT + NSEQ * (h + 1))
                for c in range(2):
                    pool.dma_start(o["s_gla_s"][0, 4 * c:4 * c + 4, h].rearrange("b k v -> k b v"),
                                   SNEW[h % 2][:, c]).then_inc(st_out[h % 2], 16)
                if h + 2 < GH:
                    state_in(h + 2)
            pool.wait_ge(st_out[0], 64)
            pool.wait_ge(st_out[1], 64)
            pool.wait_ge(out_done, outs[0])
            leave(pool, pool_stage)

            enter(pool, S_OUT1)
            pool.dma_start(wide(6), scratch).then_inc(respill_in, 16)
            out_pool(pool, 1)
            leave(pool, pool_stage)
            enter(pool, S_NORM3)
            gain(3)
            leave(pool, pool_stage)
            enter(pool, S_FF1)
            mlp_pool(pool, 1, MLP1)
            leave(pool, pool_stage)

            enter(pool, S_FINAL)
            pool.dma_start(unit(2, D), i["norm_final"].partition_broadcast(P)).then_inc(gain_in, 16)
            for n in range(NT):
                pool.wait_ge(y_ready, n + 1)
                dst = o["y_prompt"][0, n * P:(n + 1) * P] if n < PT else o["y_sample"].rearrange("b t d -> (b t) d")
                pool.dma_start(dst, unit(0, D, (n % 4) * D)).then_inc(y_out[n % 4], 16)
            for r in range(4):
                pool.wait_ge(y_out[r], 16 * len(range(r, NT, 4)))

        @block.tensor
        def _(pe):
            pe.wait_ge(const_in, 32)
            pe.wait_ge(param_in, 16 * 6)
            pe.transpose(ps[:, 0, 0:56], unit(0, P)[0:56, :], ident[0:56, 0:56]).then_inc(par_tr, 1)
            for c in range(KC):
                last = pe.transpose(ps[:, 1, c * 24:(c + 1) * 24], unit(0, D, P)[0:24, c * P:(c + 1) * P], ident[0:24, 0:24])
            last.then_inc(par_tr, 1)
            leave(pe, pe_stage)

            enter(pe, S_NORM0)
            norm_pe(pe, 0)
            leave(pe, pe_stage)

            enter(pe, S_PROJ0)
            h = part(0), part(2)

            def fm_jobs(jobs, base, before):
                for j in range(jobs):
                    if j % 2 == 0:
                        pe.wait_ge(lo_ready, base + j // 2 + 1)
                    if j >= 2:
                        pe.wait_ge(fm_taken, before + j - 1)
                    proj_fm(pe, 3 * (j % 2), base + j // 2, (j % 2) * P, h).then_inc(fm_ready, 1)

            def tm_jobs(slabs, base, before):
                for j in range(slabs * NT):
                    if j % NT == 0:
                        pe.wait_ge(lo_ready, base + j // NT + 1)
                    if j >= 2:
                        pe.wait_ge(tmj_taken, before + j - 1)
                    proj_tm(pe, ps[:, 6 + j % 2, 0:COLS], base + j // NT, h, j % NT, j % NT == 0).then_inc(tmj_ready, 1)

            fm_jobs(20, 0, 0)
            tm_jobs(4, 10, 0)
            pe.wait_ge(lo_ready, GATES0 + 1)
            pe.wait_ge(fm_taken, 20)
            proj_fm(pe, 0, GATES0, 0, h).then_inc(gate_ready, 1)
            pe.wait_ge(tmj_taken, 4 * NT)
            leave(pe, pe_stage)

            enter(pe, S_GATES)
            pe.wait_ge(g_rows, 1)
            for n in range(NT):
                pe.transpose(ps[:, 0, n * 8:(n + 1) * 8], LF[0:8, n * P:(n + 1) * P], ident[0:8, 0:8])
                pe.transpose(ps[:, 0, 72 + n * 4:76 + n * 4], IB[0:4, n * P:(n + 1) * P], ident[0:4, 0:4])
                last = pe.transpose(ps[:, 0, 108 + n * 4:112 + n * 4], MM[0:4, n * P:(n + 1) * P], ident[0:4, 0:4])
            last.then_inc(g_tr, 1)
            leave(pe, pe_stage)

            enter(pe, S_FOX)
            for n in range(NT):
                if n >= 2:
                    pe.wait_ge(fkT_taken, n - 1)
                for c in range(4):
                    last = pe.transpose(ps[:, 4 + n % 2, c * P:(c + 1) * P], FK[:, c, n * P:(n + 1) * P], ident)
                last.then_inc(fkT_ready, 1)
            pe.wait_ge(fkT_taken, NT)
            pe.wait_ge(fv_back, 32)

            def scores(j):
                h, q = fox_jobs[j]
                width = (q + 1) * P
                pe.wait_ge(f_qz, 2 + h)
                if j >= 2:
                    pe.wait_ge(f_p, j - 1)
                for c in range(0, width, 512):
                    w = min(512, width - c)
                    out = ps[:, 2 * (j % 2) + c // 512, 0:w]
                    last_part = c + w == width
                    pe.matmul(out, QZ[h % 2][:, q * P:(q + 1) * P], FK[:, h // 2, c:c + w], start=True, stop=False)
                    last = pe.matmul(out, sel[:, h, :], FN[:, c:c + w], start=False, stop=not last_part)
                    if last_part:
                        last = pe.matmul(out[:, w - P:w], ident, mask(C_MQ), start=False, stop=True)
                last.then_inc(f_s, 1)

            def probs(j):
                h, q = fox_jobs[j]
                pe.wait_ge(f_p, j + 1)
                if j >= 1:
                    pe.wait_ge(f_pts, j)
                for t in range(q + 1):
                    last = pe.transpose(ps[:, 4 + t // 4, (t % 4) * P:(t % 4 + 1) * P], PR[j % 2][:, t * P:(t + 1) * P], ident)
                last.then_inc(f_pt, 1)

            def values(j):
                h, q = fox_jobs[j]
                pe.wait_ge(f_pts, j + 1)
                if j >= 2:
                    pe.wait_ge(f_oev, j - 1)
                for t in range(q + 1):
                    last = pe.matmul(ps[:, 6 + j % 2, 0:FD], PTS[j % 2][:, t * P:(t + 1) * P], FV[:, t, h * FD:(h + 1) * FD],
                                     start=(t == 0), stop=(t == q))
                last.then_inc(f_o, 1)

            scores(0)
            for j in range(NJ):
                if j + 1 < NJ:
                    scores(j + 1)
                probs(j)
                if j >= 1:
                    values(j - 1)
            values(NJ - 1)
            pe.wait_ge(f_oev, NJ)
            for n in range(PT):
                for c in range(4):
                    last = pe.transpose(ps[:, n, c * P:(c + 1) * P], otok[:, n, c * P:(c + 1) * P], ident)
                last.then_inc(f_ot, 1)
            leave(pe, pe_stage)

            enter(pe, S_FOXS)
            pe.wait_ge(later_in, 16)

            def seq_out(b):
                pe.wait_ge(s_pn, b + 1)
                for t in range(3):
                    last = pe.transpose(ps[:, 4, t * P:(t + 1) * P], SP[:, t * P:(t + 1) * P], ident)
                last.then_inc(s_pt, 1)
                pe.wait_ge(s_pts, b + 1)
                if b >= 1:
                    pe.wait_ge(s_oev, b)
                for c in range(4):
                    for t in range(3):
                        v = VIN[b % 2][:, t, c * P:(c + 1) * P] if t < 2 else FV[:, PT, c * P:(c + 1) * P]
                        last = pe.matmul(ps[:, 6, c * 32:(c + 1) * 32], v, SPT[:, t, c * 32:(c + 1) * 32],
                                         start=(t == 0), stop=(t == 2))
                last.then_inc(s_o, 1)

            for b in range(NSEQ):
                pe.wait_ge(cache_in[b % 2], 32 * (b // 2 + 1))
                if b >= 1:
                    pe.wait_ge(s_kts, b)
                for j in range(2):
                    for c in range(4):
                        at = c * 256 + j * P
                        last = pe.transpose(ps[:, at // 512, at % 512:at % 512 + P], KIN[b % 2][:, j, c * P:(c + 1) * P], ident)
                last.then_inc(s_kt, 1)
                pe.wait_ge(s_kts, b + 1)
                pe.wait_ge(s_q, b + 2)
                if b >= 2:
                    pe.wait_ge(s_p, b - 1)
                out = ps[:, 2 + b % 2, 0:384]
                for c in range(4):
                    pe.matmul(out, QB[b % 2][:, c * P:(c + 1) * P], KT[:, c, :], start=(c == 0), stop=False)
                for t in range(3):
                    pe.matmul(out, LP[:, t, :], LATER[:, t, :], start=False, stop=False)
                pe.matmul(out[:, 256:384], ident, mask(C_MW + 112 - STEP * b), start=False, stop=True).then_inc(s_s, 1)
                seq_out(b)
            leave(pe, pe_stage)

            enter(pe, S_ML)
            pe.wait_ge(mv_back, 16 * NT)

            def ml_inputs(n):
                t = slice(n * P, (n + 1) * P)
                for h in range(MH):
                    pe.matmul(ps[:, 0, h * P:(h + 1) * P], sel[:, h, :], BM[:, t], start=True, stop=True)
                    pe.matmul(ps[:, 1, h * P:(h + 1) * P], sel[:, h, :], GL[:, t], start=True, stop=True)
                    pe.matmul(ps[:, 2, h * P:(h + 1) * P], MK[:, h, t], MQ[:, h, t], start=True, stop=True)
                    last = pe.transpose(ps[:, 3, h * P:(h + 1) * P], MK[:, h, t], ident)
                last.then_inc(m_in, 1)

            for n in range(PT):
                if n >= 1:
                    pe.wait_ge(m_kw, n)
                    pe.wait_ge(m_g, n)
                ml_inputs(n)
                pe.wait_ge(m_a, n + 1)
                pe.wait_ge(m_cn, n + 1)
                if n >= 1:
                    pe.wait_ge(m_num, n)
                for h in range(MH):
                    out = ps[:, 4 + h // 2, (h % 2) * 129:(h % 2 + 1) * 129]
                    pe.matmul(out, AT[:, h], MV[:, n, h], start=True, stop=False)
                    last = pe.matmul(out, QG[:, h], CN[:, h], start=False, stop=True)
                last.then_inc(m_o, 1)
                pe.wait_ge(m_kw, n + 1)
                for h in range(MH):
                    last = pe.matmul(ps[:, 6 + h // 2, (h % 2) * 129:(h % 2 + 1) * 129], KW[:, h], MV[:, n, h],
                                     start=True, stop=True)
                last.then_inc(m_u, 1)
            pe.wait_ge(m_cn, PT + 1)
            pe.wait_ge(m_kw, PT)
            for h in range(MH):
                last = pe.transpose(ps[:, 0, h * P:(h + 1) * P], CN[:, h, 0:128], ident)
            pe.wait_ge(n_in, 16)
            pe.transpose(ps[0:4, 1, 0:P], NNEW[:, 32:36], ident)
            pe.transpose(ps[:, 2, 0:32], NROW[0:32, :], ident[0:32, 0:32]).then_inc(c_ct, 1)
            leave(pe, pe_stage)

            enter(pe, S_MLS)
            ml_inputs(PT)
            pe.wait_ge(m_a, PT + 1)
            pe.wait_ge(m_kw, PT + 1)
            for h in range(MH):
                pe.wait_ge(c_in, 16 * (h + 1))
                for b in range(NSEQ):
                    last = pe.transpose(ps[:, b // 4, (b % 4) * P:(b % 4 + 1) * P], CRAW[:, b], ident)
                last.then_inc(c_tr, 1)
                pe.wait_ge(c_ev, h + 1)
                pe.wait_ge(c_qg, h + 1)
                out = ps[:, 4, 0:129]
                pe.matmul(out, AT[:, h], MV[:, PT, h], start=True, stop=False)
                for b in range(NSEQ):
                    last = pe.matmul(out, QGB[:, b * P:(b + 1) * P], CNS[:, b], start=False, stop=(b == NSEQ - 1))
                last.then_inc(m_o, 1)
                pe.wait_ge(c_kw, h + 1)
                for b in range(NSEQ):
                    last = pe.matmul(ps[:, 5 + b // 3, (b % 3) * 129:(b % 3 + 1) * 129], KWB[:, b], MV[:, PT, h],
                                     start=True, stop=True)
                last.then_inc(c_u, 1)
                pe.wait_ge(c_cn, h + 1)
                for b in range(NSEQ):
                    last = pe.transpose(ps[:, b // 4, (b % 4) * P:(b % 4 + 1) * P], CNS[:, b, 0:128], ident)
                last.then_inc(c_ct, 1)
                pe.wait_ge(c_ctev, h + 1)
            pe.transpose(ps[0:32, 2, 0:P], NNEW[:, 0:32], ident)
            for c in range(KC):
                last = pe.transpose(ps[0:27, 5 + c // 4, (c % 4) * P:(c % 4 + 1) * P], convstate[:, c], ident)
            last.then_inc(c_ct, 1)
            leave(pe, pe_stage)

            enter(pe, S_MLH)
            for n in range(NT):
                pe.wait_ge(h_hs, n + 1)
                if n >= 4:
                    pe.wait_ge(h_mix, n - 3)
                for h in range(MH):
                    last = pe.transpose(ps[:, n % 4, h * P:(h + 1) * P], HST[:, n % 2, h * P:(h + 1) * P], ident)
                last.then_inc(h_tr, 1)
            leave(pe, pe_stage)

            enter(pe, S_OUT0)
            out_pe(pe, 0)
            leave(pe, pe_stage)
            enter(pe, S_NORM1)
            norm_pe(pe, 1)
            leave(pe, pe_stage)
            enter(pe, S_FF0)
            mlp_pe(pe, 0, MLP0, (part(0), part(4)), HID0)
            leave(pe, pe_stage)
            enter(pe, S_NORM2)
            norm_pe(pe, 2)
            leave(pe, pe_stage)

            enter(pe, S_PROJ1)
            h = part(0), part(4)
            fm_jobs(16, ODD, 20)
            tm_jobs(4, ODD + 8, 4 * NT)
            pe.wait_ge(lo_ready, GATES1 + 1)
            pe.wait_ge(fm_taken, 36)
            proj_fm(pe, 0, GATES1, 0, h).then_inc(gate_ready, 1)
            pe.wait_ge(tmj_taken, 8 * NT)
            leave(pe, pe_stage)

            enter(pe, S_CB)
            pe.wait_ge(ga_in, 16)
            for m in range(4):
                if m >= 2:
                    pe.wait_ge(a_e, m - 1)
                for n in range(3):
                    last = pe.matmul(ps[:, 3 * (m % 2) + n, 0:GN], WA2[0:16, m * P:(m + 1) * P],
                                     GAT[0:16, n * GN:(n + 1) * GN], start=True, stop=True)
                last.then_inc(a_l, 1)
            leave(pe, pe_stage)

            enter(pe, S_GLA)
            pe.wait_ge(level_in, 16)
            pe.wait_ge(gv_back, 16)

            def level_pair(q):
                return 2 * (q % 2)

            def gla_head(n):
                t = slice(n * P, (n + 1) * P)
                pe.wait_ge(l_ks, n + 1)
                if n >= 1:
                    pe.wait_ge(l_sn, 1 + 4 * n)
                for h in range(GH):
                    last = pe.transpose(ps[:, 6, h * P:(h + 1) * P], KS[:, h], ident)
                last.then_inc(l_kt, 1)
                pe.wait_ge(l_m, n + 1)
                for h in range(GH):
                    q = 5 * n + h
                    if q >= 2:
                        pe.wait_ge(l_free, q - 1)
                    for l in range(8):
                        out = ps[:, level_pair(q) + l // 4, (l % 4) * P:(l % 4 + 1) * P]
                        if l == 7:
                            last = pe.matmul(out, GKT[:, h, t], GQ[:, h, t], start=True, stop=True)
                        elif n < PT or LEVELS[l] <= 8:
                            pe.matmul(out, EL[n % 2][:, l, h], EL[n % 2][:, l, h], start=True, stop=True)
                    last.then_inc(l_a, 1)

            def gla_turn(n):
                q = 5 * n + 4
                pe.wait_ge(l_osc, n + 1)
                pe.wait_ge(l_free, q - 1)
                for c in range(8):
                    last = pe.transpose(ps[:, level_pair(q) + c // 4, (c % 4) * P:(c % 4 + 1) * P],
                                        OO[:, c // 2, (c % 2) * P:(c % 2 + 1) * P], ident)
                last.then_inc(l_otr, 1)

            for n in range(PT):
                gla_head(n)
                pe.wait_ge(l_qe, n + 1)
                pe.wait_ge(l_sn, 1 + 4 * n)
                if n >= 1:
                    pe.wait_ge(l_osc, n)
                for h in range(GH):
                    pe.wait_ge(l_at, 4 * n + h + 1)
                    out = ps[:, 4 + h // 2, (h % 2) * GV:(h % 2 + 1) * GV]
                    pe.matmul(out, LA[:, h], GVT[:, n, h * GV:(h + 1) * GV], start=True, stop=False)
                    last = pe.matmul(out, QE[:, h], SS[:, h], start=False, stop=True)
                last.then_inc(l_o, 1)
                pe.wait_ge(l_ktev, n + 1)
                for h in range(GH):
                    last = pe.matmul(ps[:, 6 + h // 2, (h % 2) * GV:(h % 2 + 1) * GV], KST[:, h],
                                     GVT[:, n, h * GV:(h + 1) * GV], start=True, stop=True)
                last.then_inc(l_u, 1)
                gla_turn(n)
            leave(pe, pe_stage)

            enter(pe, S_GLAS)
            gla_head(PT)
            for h in range(GH):
                pe.wait_ge(l_at, 4 * PT + h + 1)
                pe.wait_ge(l_qe, PT + h + 1)
                pe.wait_ge(st_in[h % 2], 32 * (h // 2 + 1))
                out = ps[:, 4 + h // 2, (h % 2) * GV:(h % 2 + 1) * GV]
                pe.matmul(out, LA[:, h], GVT[:, PT, h * GV:(h + 1) * GV], start=True, stop=False)
                for b in range(NSEQ):
                    last = pe.matmul(out, QEB[:, b * P:(b + 1) * P], SIN[h % 2][:, b // 4, b % 4], start=False,
                                     stop=(b == NSEQ - 1))
                last.then_inc(l_o, 1)
                pe.wait_ge(l_keb, h + 1)
                for b in range(NSEQ):
                    g = NSEQ * h + b
                    if g >= 2:
                        pe.wait_ge(l_sn, 1 + 4 * PT + g - 1)
                    pe.matmul(ps[:, 6 + g % 2, 0:GV], KEB[:, b], GVT[:, PT, h * GV:(h + 1) * GV],
                              start=True, stop=True).then_inc(l_u, 1)
            gla_turn(PT)
            leave(pe, pe_stage)

            enter(pe, S_OUT1)
            out_pe(pe, 1)
            leave(pe, pe_stage)
            enter(pe, S_NORM3)
            norm_pe(pe, 3)
            leave(pe, pe_stage)
            enter(pe, S_FF1)
            mlp_pe(pe, 1, MLP1, (part(0), part(4)), HID1)
            leave(pe, pe_stage)

        @block.scalar
        def _(act):
            own = [0]
            act.wait_ge(par_tr, 1)
            act.activation(params, ps[:, 0, 0:56], ACT.Copy)
            act.wait_ge(par_tr, 2)
            act.activation(history.rearrange("p c n -> p (c n)"), ps[:, 1, 0:192], ACT.Copy)
            leave(act, act_stage)

            enter(act, S_NORM0)
            hi_of(act, 0, free=True)
            hi_of(act, 1, free=True)
            norm_act(act, 0, own)
            leave(act, act_stage)

            enter(act, S_PROJ0)

            def silu(j):
                act.wait_ge(conv_done, j + 1)
                one = act.activation(conv_out(j), conv_out(j), ACT.Silu)
                if j >= 4:
                    link(act, act_own, own, one)
                    act.activation(conv_out(j), conv_out(j), ACT.Copy, scale=MD ** -0.5)

            act.wait_ge(conv_ready, 1)
            for j in range(20):
                if j % 2 == 0 and j >= 2:
                    hi_of(act, j // 2 + 1)
                act.wait_ge(fm_ready, j + 1)
                g = 3 * (j % 2)
                if j < KC:
                    if j >= 3:
                        act.wait_ge(conv_done, j - 2)
                    u = conv_in(j)
                    act.activation(conv_seq(j)[:, :, 0:3], history[:, j].rearrange("p (b t) -> p b t", b=NSEQ), ACT.Copy)
                    act.activation(u[:, 3:3 + 2 * GN].rearrange("p (g t) -> p g t", g=2), ps[:, g:g + 2, 0:GN], ACT.Copy)
                    act.activation(u[:, 3 + 2 * GN:3 + SEQ], ps[:, g + 2, 0:256], ACT.Copy)
                    link(act, act_own, own, act.activation(
                        conv_seq(j)[:, :, 3:], ps[:, g + 2, 256:384].rearrange("p (b t) -> p b t", b=NSEQ), ACT.Copy))
                    act.activation(conv_out(j)[:, 0:SEQ], u[:, 0:SEQ], ACT.Identity, scale=conv_w[:, 0, j:j + 1],
                                   bias=conv_b[:, j:j + 1])
                    act.activation(sample(conv_out(j)), conv_seq(j)[:, :, 0:STEP], ACT.Identity,
                                   scale=conv_w[:, 0, j:j + 1], bias=conv_b[:, j:j + 1]).then_inc(fm_taken, 1)
                elif j < 12:
                    act.activation(as_groups(FQ[:, j - 8]), group(j), ACT.Copy, scale=FD ** -0.5).then_inc(fm_taken, 1)
                elif j < 16:
                    act.activation(as_groups(FK[:, j - 12]), group(j), ACT.Copy).then_inc(fm_taken, 1)
                else:
                    if j >= 18:
                        act.wait_ge(gate_out[j % 2], 16)
                    act.activation(as_groups(GATE_ST[j % 2]), group(j), ACT.Sigmoid).then_inc(fm_taken, 1)
                if 1 <= j <= KC:
                    silu(j - 1)
            for m in range(10, GATES0):
                hi_of(act, m + 1)
            act.wait_ge(gate_ready, 1)
            for g, (row, m) in enumerate(((RF, 8), (RI, 4), (RM, 4))):
                act.activation(as_groups(row)[0:m], ps[32 * g:32 * g + m, 0:3, 0:GN], ACT.Identity, bias=gbias[0:m, g:g + 1])
            leave(act, act_stage)

            enter(act, S_GATES)
            act.wait_ge(g_a, 1)
            act.activation(TF[0:8, :], TF[0:8, :], ACT.Exp)
            link(act, act_own, own, act.activation(TM_[0:4, :], TM_[0:4, :], ACT.Exp))
            act.activation(TF[0:8, :], TF[0:8, :], ACT.Ln, bias=1.0)
            act.activation(TM_[0:4, :], TM_[0:4, :], ACT.Ln, bias=1.0).then_inc(g_b, 1)
            act.wait_ge(g_tr, 1)
            act.activation(lfT.rearrange("p n h -> p (n h)"), ps[:, 0, 0:72], ACT.Copy)
            act.activation(ibT.rearrange("p n h -> p (n h)"), ps[:, 0, 72:108], ACT.Copy)
            act.activation(enmT.rearrange("p n h -> p (n h)"), ps[:, 0, 108:144], ACT.Exp, scale=-1.0).then_inc(g_cols, 1)
            leave(act, act_stage)

            enter(act, S_FOX)
            for n in range(NT):
                act.wait_ge(fkT_ready, n + 1)
                if n >= 2:
                    act.wait_ge(fk_out[n % 2], 16 * (n // 2))
                act.activation(FKST[n % 2], ps[:, 4 + n % 2, :], ACT.Copy).then_inc(fkT_taken, 1)
            for j, (h, q) in enumerate(fox_jobs):
                act.wait_ge(f_mx, j + 1)
                if j >= 2:
                    act.wait_ge(f_pt, j - 1)
                w = (q + 1) * P
                src = ps[:, 2 * (j % 2):2 * (j % 2) + 2, :].rearrange("p b k -> p (b k)")[:, 0:w]
                act.activation(PR[j % 2][:, 0:w], src, ACT.Exp, bias=stat[:, 4 + j % 4:5 + j % 4],
                               accum_out=stat[:, 8 + j % 4:9 + j % 4]).then_inc(f_p, 1)
            for n in range(PT):
                act.wait_ge(f_ot, n + 1)
                act.activation(FQ[:, :, n * P:(n + 1) * P], ps[:, n, :].rearrange("p (c t) -> p c t", c=4), ACT.Copy)
            leave(act, act_stage)

            enter(act, S_FOXS)
            for b in range(NSEQ):
                act.wait_ge(s_kt, b + 1)
                if b >= 1:
                    act.wait_ge(s_s, b)
                act.activation(KT[:, :, 0:256], ps[:, 0:2, :].rearrange("p b (c k) -> p (b c) k", c=2), ACT.Copy).then_inc(s_kts, 1)
                act.wait_ge(s_mx, b + 1)
                if b >= 1:
                    act.wait_ge(s_pt, b)
                act.activation(SP, ps[:, 2 + b % 2, 0:384], ACT.Exp, bias=stat[:, 1:2], accum_out=stat[:, 2:3]).then_inc(s_p, 1)
                act.wait_ge(s_pt, b + 1)
                if b >= 1:
                    act.wait_ge(s_o, b)
                act.activation(SPT_, ps[:, 4, 0:384], ACT.Copy).then_inc(s_pts, 1)
            leave(act, act_stage)

            enter(act, S_ML)

            def ml_act(n):
                act.wait_ge(m_dm, n + 1)
                for h in range(MH):
                    last = act.activation(WT[:, h], WT[:, h], ACT.Exp, bias=ibT[:, n, h:h + 1])
                last.then_inc(m_w, 1)
                if n >= 1:
                    act.wait_ge(m_cn, n + 1)
                act.activation(GB.rearrange("p h t -> p (h t)"), ps[:, 1, :], ACT.Exp).then_inc(m_g, 1)

            for n in range(PT):
                ml_act(n)
                act.wait_ge(m_o, n + 1)
                act.activation(NUM[:, n].rearrange("p (b h) d -> p b (h d)", b=2), ps[:, 4:6, 0:258], ACT.Copy).then_inc(m_num, 1)
            act.wait_ge(c_ct, 1)
            act.activation(QG.rearrange("p h t -> p (h t)"), ps[:, 0, :], ACT.Copy)
            act.activation(NOUT[0:4, :], ps[0:4, 1, 0:P], ACT.Copy)
            act.activation(NCOL, ps[:, 2, 0:32], ACT.Copy)
            leave(act, act_stage)

            enter(act, S_MLS)
            ml_act(PT)
            for h in range(MH):
                act.wait_ge(c_tr, h + 1)
                act.activation(CNS[:, :, 0:128], ps[:, 0:2, :].rearrange("p b (s d) -> p (b s) d", s=4), ACT.Copy)
                act.activation(CNS[:, :, 128:129], NCOL.rearrange("p (b h) -> p b h", h=MH)[:, :, h:h + 1], ACT.Copy).then_inc(c_ev, 1)
                act.wait_ge(m_o, PT + h + 1)
                act.activation(NUM[:, PT, h], ps[:, 4, 0:129], ACT.Copy).then_inc(m_num, 1)
                act.wait_ge(c_ct, h + 2)
                act.activation(CRAW.rearrange("p (a b) d -> p a (b d)", a=2), ps[:, 0:2, :], ACT.Copy).then_inc(c_ctev, 1)
            act.wait_ge(c_ct, MH + 2)
            act.activation(NROW[0:32, :], ps[0:32, 2, 0:P], ACT.Copy)
            act.activation(KWB.rearrange("p (a b) d -> p a (b d)", a=2)[0:27], ps[0:27, 5:7, :], ACT.Copy).then_inc(c_o, 1)
            leave(act, act_stage)

            enter(act, S_MLH)
            for n in range(NT):
                for h in range(MH):
                    link(act, act_own, own, act.activation(HJUNK, NUM[:, n, h, 0:128], ACT.Square,
                                                           accum_out=SSQ[:, n * MH + h:n * MH + h + 1]))
            act.sem_inc(h_sq, 1)
            act.wait_ge(h_rt, 1)
            act.activation(HTMP, SSQ, ACT.Sqrt).then_inc(h_root, 1)
            leave(act, act_stage)

            enter(act, S_OUT0)
            out_act(act, 0, (FQ, MO))
            leave(act, act_stage)
            enter(act, S_NORM1)
            norm_act(act, 1, own)
            leave(act, act_stage)
            enter(act, S_FF0)
            mlp_act(act, 0, MLP0, HID0)
            leave(act, act_stage)
            enter(act, S_NORM2)
            norm_act(act, 2, own)
            leave(act, act_stage)

            enter(act, S_PROJ1)
            for j in range(16):
                if j % 2 == 0:
                    hi_of(act, ODD + j // 2 + 1)
                act.wait_ge(fm_ready, 20 + j + 1)
                if j < 4:
                    act.activation(as_groups(GQ[:, j]), group(j), ACT.Copy, scale=GK ** -0.5).then_inc(fm_taken, 1)
                elif j < 8:
                    act.activation(as_groups(GKT[:, j - 4]), group(j), ACT.Copy).then_inc(fm_taken, 1)
                else:
                    act.activation(as_groups(GG[:, j - 8]), group(j), ACT.Silu).then_inc(fm_taken, 1)
            for m in range(ODD + 8, GATES1):
                hi_of(act, m + 1)
            act.wait_ge(gate_ready, 2)
            act.activation(as_groups(GAT)[0:16], ps[0:16, 0:3, 0:GN], ACT.Copy)
            leave(act, act_stage)

            enter(act, S_CB)
            tmp = fm(5)
            for m in range(4):
                act.wait_ge(a_l, m + 1)
                act.activation(as_groups(CB[:, m]), group(m), ACT.Identity, bias=b_gla[:, m:m + 1]).then_inc(a_e, 1)
            for m in range(4):
                act.wait_ge(a_cb, m + 1)
                link(act, act_own, own, act.activation(tmp[:, m], tmp[:, m], ACT.Exp))
                act.activation(tmp[:, m], tmp[:, m], ACT.Ln, bias=1.0).then_inc(a_e, 1)
            leave(act, act_stage)

            enter(act, S_GLA)

            def gla_exp(n):
                act.wait_ge(l_d, 2 * n + 1)
                first = 0 if n < PT else 3
                act.activation(EL[n % 2][:, first:].rearrange("p l h t -> p (l h t)"),
                               EL[n % 2][:, first:].rearrange("p l h t -> p (l h t)"), ACT.Exp).then_inc(l_e, 1)
                act.wait_ge(l_d, 2 * n + 2)
                act.activation(KS.rearrange("p h t -> p (h t)"), KS.rearrange("p h t -> p (h t)"), ACT.Exp).then_inc(l_eb, 1)
                if n >= 1:
                    act.wait_ge(l_o, n)
                cb = CB[:, :, n * P:(n + 1) * P]
                act.activation(QE, cb, ACT.Exp)
                if n < PT:
                    act.activation(ecl[:, n % 2, :, 0:1], cb[:, :, P - 1:P], ACT.Exp).then_inc(l_eb, 1)
                else:
                    act.activation(ecl[:, n % 2], cb[:, :, STEP - 1:P:STEP], ACT.Exp).then_inc(l_eb, 1)

            def gla_norm(n):
                act.wait_ge(l_o, n + 1 if n < PT else PT + GH)
                for h in range(GH):
                    link(act, act_own, own, act.activation(junk256, ps[:, 4 + h // 2, (h % 2) * GV:(h % 2 + 1) * GV], ACT.Square,
                                                           accum_out=osum[:, h:h + 1]))
                act.sem_inc(l_osq, 1)
                act.wait_ge(l_oln, 2 * n + 1)
                link(act, act_own, own, act.activation(osum[:, 4:8], osum[:, 0:4], ACT.Ln))
                act.activation(osum[:, 4:8], osum[:, 4:8], ACT.Exp, scale=-0.5).then_inc(l_oln, 1)

            def gla_keys(n):
                act.wait_ge(l_kt, n + 1)
                act.activation(KST.rearrange("p h t -> p (h t)"), ps[:, 6, :], ACT.Copy).then_inc(l_ktev, 1)

            for n in range(PT):
                gla_exp(n)
                if n >= 1:
                    act.wait_ge(l_u, n)
                gla_keys(n)
                gla_norm(n)
            leave(act, act_stage)

            enter(act, S_GLAS)
            gla_exp(PT)
            gla_keys(PT)
            gla_norm(PT)
            leave(act, act_stage)

            enter(act, S_OUT1)
            out_act(act, 1, (GG[:, 0:4], GG[:, 4:8]))
            leave(act, act_stage)
            enter(act, S_NORM3)
            norm_act(act, 3, own)
            leave(act, act_stage)
            enter(act, S_FF1)
            mlp_act(act, 1, MLP1, HID1)
            leave(act, act_stage)

            enter(act, S_FINAL)
            for n in range(NT):
                link(act, act_own, own, act.activation(unit(2, D, D), tokens(6)[:, n], ACT.Square, accum_out=ssum[:, n:n + 1]))
            act.sem_inc(sq_done, 1)
            act.wait_ge(root_in, 5)
            act.activation(rstd, ssum, ACT.Sqrt).then_inc(root_ready, 1)

        @block.vector
        def _(dve):
            own = [0]

            def after(ins):
                link(dve, dve_own, own, ins)

            leave(dve, dve_stage)
            enter(dve, S_NORM0)
            norm_dve(dve, 0, own)
            leave(dve, dve_stage)

            enter(dve, S_PROJ0)

            def conv(j):
                dve.wait_ge(fm_taken, j + 1)
                u, v = conv_in(j), conv_out(j)
                for tap in range(1, TAPS):
                    w = conv_w[:, tap, j:j + 1]
                    first = dve.scalar_tensor_tensor(out=v[:, 0:SEQ], in0=u[:, tap:tap + SEQ], scalar=w, in1=v[:, 0:SEQ],
                                                     op0=ALU.mult, op1=ALU.add)
                    second = dve.scalar_tensor_tensor(out=sample(v), in0=conv_seq(j)[:, :, tap:tap + STEP], scalar=w,
                                                      in1=sample(v), op0=ALU.mult, op1=ALU.add)
                    if tap < TAPS - 1:
                        after(second)
                dve.tensor_copy(convstate[:, j, 0:3], u[:, SEQ:SEQ + 3])
                dve.tensor_copy(convstate[:, j, 3:27].rearrange("p (b t) -> p b t", b=NSEQ),
                                conv_seq(j)[:, :, STEP:STEP + 3]).then_inc(conv_done, 1)

            for j in range(KC):
                conv(j)

            def pieces(first):
                for j in range(first, first + 4 * NT):
                    dve.wait_ge(tmj_ready, j + 1)
                    if j >= 3:
                        dve.wait_ge(piece_out[j % 3], 16 * (j // 3))
                    dve.tensor_copy(PIECE_ST[j % 3], ps[:, 6 + j % 2, 0:COLS]).then_inc(tmj_taken, 1)

            pieces(0)
            leave(dve, dve_stage)

            enter(dve, S_GATES)
            for row in (FN, BM, IB, MM):
                dve.memset(row, 0.0)
            dve.memset(ONES, 1.0)
            after(dve.memset(RESET, 1.0))
            dve.memset(RESET[:, starts(0)], 0.0)
            after(dve.memset(RESET[:, starts(1)], 0.0))
            dve.scalar_tensor_tensor(out=TF[0:8, :], in0=RF[0:8, :], scalar=-1.0, in1=RF[0:8, :], op0=ALU.mult, op1=ALU.min)
            dve.scalar_tensor_tensor(out=TM_[0:4, :], in0=RM[0:4, :], scalar=-1.0, in1=RM[0:4, :], op0=ALU.mult,
                                     op1=ALU.min).then_inc(g_a, 1)
            dve.wait_ge(g_b, 1)
            dve.scalar_tensor_tensor(out=LF[0:8, :], in0=RF[0:8, :], scalar=0.0, in1=TF[0:8, :], op0=ALU.min, op1=ALU.subtract)
            after(dve.scalar_tensor_tensor(out=LM[0:4, :], in0=RM[0:4, :], scalar=0.0, in1=TM_[0:4, :], op0=ALU.min,
                                           op1=ALU.subtract))
            dve.tensor_tensor_scan(FN[0:8, 0:SEQ], ONES[0:8, :], LF[0:8, 0:SEQ], 0.0, ALU.mult, ALU.subtract)
            B_ = TF
            after(dve.tensor_tensor_scan(B_[0:4, :], RESET[0:4, :], LM[0:4, :], 0.0, ALU.mult, ALU.add))
            after(dve.tensor_copy(TM_[0:4, :], RI[0:4, :]))
            after(dve.tensor_tensor(IB[0:4, :], RI[0:4, :], B_[0:4, :], ALU.subtract))
            for cols, m0 in ((slice(0, 1), mbefore[0:4, 0:1]), (slice(SEQ, T, STEP), mbefore[0:4, 1:9])):
                after(dve.tensor_tensor(RM[0:4, cols], LM[0:4, cols], m0, ALU.add))
                after(dve.tensor_tensor(TM_[0:4, cols], RM[0:4, cols], RI[0:4, cols], ALU.max))
                after(dve.memset(LM[0:4, cols], -BIG))
            after(dve.tensor_tensor_scan(MM[0:4, :], LM[0:4, :], TM_[0:4, :], 0.0, ALU.add, ALU.max))
            after(dve.tensor_tensor(BM[0:4, :], B_[0:4, :], MM[0:4, :], ALU.subtract))
            after(dve.memset(GL, 0.0))
            after(dve.tensor_copy(GL[0:4, 0:P], BM[0:4, 0:P]))
            dve.tensor_tensor(GL[0:4, P:SEQ].rearrange("p (n t) -> p n t", t=P), BM[0:4, P:SEQ].rearrange("p (n t) -> p n t", t=P),
                              MM[0:4, P - 1:SEQ - 1:P].unsqueeze(2).broadcast_to([4, PT - 1, P]), ALU.add)
            dve.tensor_tensor(sample(GL)[0:4], sample(BM)[0:4],
                              mbefore[0:4, 1:9].unsqueeze(2).broadcast_to([4, NSEQ, STEP]), ALU.add).then_inc(g_rows, 1)
            leave(dve, dve_stage)

            enter(dve, S_FOX)

            def queries(h):
                if h == 0:
                    dve.wait_ge(f_qz, 1)
                if h >= 2:
                    dve.wait_ge(f_s, PT * (h - 1))
                r = 64 * (h % 2)
                dve.tensor_copy(QZ[h % 2][r:r + 64, :], FQ[r:r + 64, h // 2, 0:SEQ]).then_inc(f_qz, 1)

            def biggest(j):
                h, q = fox_jobs[j]
                w = (q + 1) * P
                dve.wait_ge(f_s, j + 1)
                src = ps[:, 2 * (j % 2):2 * (j % 2) + 2, :].rearrange("p b k -> p (b k)")[:, 0:w]
                top = stat[:, 16 + j % 4:17 + j % 4]
                after(dve.tensor_reduce(top, src, AX.X, ALU.max))
                dve.tensor_scalar(stat[:, 4 + j % 4:5 + j % 4], top, -1.0, None, ALU.mult).then_inc(f_mx, 1)

            def probs_out(j):
                h, q = fox_jobs[j]
                w = (q + 1) * P
                dve.wait_ge(f_pt, j + 1)
                if j >= 2:
                    dve.wait_ge(f_o, j - 1)
                dve.tensor_copy(PTS[j % 2][:, 0:w], ps[:, 4:6, :].rearrange("p b k -> p (b k)")[:, 0:w]).then_inc(f_pts, 1)

            def output(j):
                h, q = fox_jobs[j]
                inverse = stat[:, 12 + j % 2:13 + j % 2]
                dve.wait_ge(f_o, j + 1)
                after(dve.reciprocal(inverse, stat[:, 8 + j % 4:9 + j % 4]))
                dve.tensor_scalar(otok[:, q, h * FD:(h + 1) * FD], ps[:, 6 + j % 2, 0:FD], inverse, None,
                                  ALU.mult).then_inc(f_oev, 1)

            dve.wait_ge(fk_out[0], 16 * 5)
            dve.wait_ge(fk_out[1], 16 * 4)
            queries(0)
            queries(1)
            biggest(0)
            for j in range(NJ):
                if j + 1 < NJ:
                    biggest(j + 1)
                probs_out(j)
                if j % PT == 0 and 2 <= j // PT + 1 < FH:
                    queries(j // PT + 1)
                if j >= 1:
                    output(j - 1)
            output(NJ - 1)
            leave(dve, dve_stage)

            enter(dve, S_FOXS)
            dve.tensor_copy(KT[:, :, 256:384], FK[:, :, SEQ:T])
            dve.wait_ge(pastlf_in, 32)
            dve.wait_ge(s_q, 1)
            plf = PLF.rearrange("p (b j h) -> p b j h", b=NSEQ, j=2)
            after(dve.tensor_tensor(LNEW.rearrange("p (h q) -> p h q", q=STEP), lfT[:, PT].unsqueeze(2).broadcast_to([P, FH, STEP]),
                                    mask(C_C16, 16).unsqueeze(1).broadcast_to([P, FH, STEP]), ALU.mult))
            for b in range(NSEQ):
                if b >= 1:
                    dve.wait_ge(s_s, b)
                t = slice(SEQ + b * STEP, SEQ + (b + 1) * STEP)
                for r in range(2):
                    dve.tensor_copy(QB[b % 2][64 * r:64 * r + 64].rearrange("p (c x) -> p c x", x=160)[:, :, r * 16:r * 16 + 16],
                                    FQ[64 * r:64 * r + 64, :, t])
                for jt in range(2):
                    dve.tensor_copy(LP[:, jt].rearrange("p (h q) -> p h q", q=STEP),
                                    plf[:, b, jt].unsqueeze(2).broadcast_to([P, FH, STEP]))
                dve.tensor_scalar(LP[:, 2], LNEW, mask(C_IND + b, 1), None, ALU.mult).then_inc(s_q, 1)
                dve.wait_ge(s_s, b + 1)
                after(dve.tensor_reduce(stat[:, 0:1], ps[:, 2 + b % 2, 0:384], AX.X, ALU.max))
                dve.tensor_scalar(stat[:, 1:2], stat[:, 0:1], -1.0, None, ALU.mult).then_inc(s_mx, 1)
                dve.wait_ge(s_p, b + 1)
                after(dve.reciprocal(stat[:, 3:4], stat[:, 2:3]))
                dve.tensor_scalar(SP, SP, stat[:, 3:4], None, ALU.mult).then_inc(s_pn, 1)
                dve.wait_ge(s_o, b + 1)
                for r in range(2):
                    last = dve.tensor_copy(FQ[64 * r:64 * r + 64, :, t],
                                           ps[64 * r:64 * r + 64, 6, 0:128].rearrange("p (c x) -> p c x", x=32)[:, :, 16 * r:16 * r + 16])
                last.then_inc(s_oev, 1)
            leave(dve, dve_stage)

            enter(dve, S_ML)

            def ml_dve(n, m):
                t = slice(n * P, (n + 1) * P)
                dve.wait_ge(m_in, n + 1)
                dve.tensor_tensor(WT, ps[:, 0, :].rearrange("p (h t) -> p h t", h=MH),
                                  mask(m).unsqueeze(1).broadcast_to([P, MH, P]), ALU.add).then_inc(m_dm, 1)
                dve.wait_ge(m_g, n + 1)
                if n >= 1:
                    dve.wait_ge(m_o, n)
                dve.tensor_tensor(QG, MQ[:, :, t], GB, ALU.mult)
                dve.wait_ge(m_w, n + 1)
                dve.tensor_tensor(AT, WT, ps[:, 2, :].rearrange("p (h t) -> p h t", h=MH), ALU.mult).then_inc(m_a, 1)

            for n in range(PT):
                if n >= 1:
                    dve.wait_ge(m_a, n)
                ml_dve(n, C_MC)
                if n >= 1:
                    dve.wait_ge(m_u, n)
                for h in range(MH):
                    last = dve.tensor_scalar(KW[:, h], ps[:, 3, h * P:(h + 1) * P], WT[:, h, P - 1:P], None, ALU.mult)
                last.then_inc(m_kw, 1)
                dve.wait_ge(m_u, n + 1)
                for h in range(MH):
                    last = dve.scalar_tensor_tensor(out=CN[:, h], in0=CN[:, h], scalar=GB[:, h, P - 1:P],
                                                    in1=ps[:, 6 + h // 2, (h % 2) * 129:(h % 2 + 1) * 129],
                                                    op0=ALU.mult, op1=ALU.add)
                if n < PT - 1:
                    last.then_inc(m_cn, 1)
                else:
                    after(last)
            dve.tensor_copy(NNEW[:, 32:36].unsqueeze(2), CN[:, :, 128:129]).then_inc(m_cn, 1)
            leave(dve, dve_stage)

            enter(dve, S_MLS)
            dve.wait_ge(out_done, 16 * 6)
            ml_dve(PT, C_MB)
            dve.tensor_copy(KW.rearrange("p h t -> p (h t)"), ps[:, 3, :]).then_inc(m_kw, 1)
            dve.wait_ge(m_kw, PT + 1)
            for h in range(MH):
                if h >= 1:
                    dve.wait_ge(m_o, PT + h)
                    dve.wait_ge(c_u, h)
                dve.tensor_copy(QGB.rearrange("p (b x) -> p b x", x=144)[:, :, 0:STEP],
                                QG[:, h].rearrange("p (b t) -> p b t", b=NSEQ)).then_inc(c_qg, 1)
                for b in range(NSEQ):
                    e = b * STEP + STEP - 1
                    last = dve.tensor_scalar(KWB[:, b], KW[:, h], WT[:, h, e:e + 1], None, ALU.mult)
                last.then_inc(c_kw, 1)
                dve.wait_ge(c_u, h + 1)
                for b in range(NSEQ):
                    e = b * STEP + STEP - 1
                    last = dve.scalar_tensor_tensor(out=CNS[:, b], in0=CNS[:, b], scalar=GB[:, h, e:e + 1],
                                                    in1=ps[:, 5 + b // 3, (b % 3) * 129:(b % 3 + 1) * 129],
                                                    op0=ALU.mult, op1=ALU.add)
                after(last)
                dve.tensor_copy(NNEW[:, 0:32].rearrange("p (b h) -> p b h", h=MH)[:, :, h:h + 1], CNS[:, :, 128:129]).then_inc(c_cn, 1)
            leave(dve, dve_stage)

            enter(dve, S_MLH)
            dve.wait_ge(mo_back, 16)
            den4 = NUM[:, :, :, 128:129].rearrange("p n h o -> p (n h) o")
            RD3 = RD.unsqueeze(2)
            after(dve.scalar_tensor_tensor(out=RD3, in0=den4, scalar=-1.0, in1=den4, op0=ALU.mult, op1=ALU.max))
            after(dve.tensor_tensor(RD, RD, enmT.rearrange("p n h -> p (n h)"), ALU.max))
            after(dve.reciprocal(HSC, RD))
            dve.wait_ge(h_sq, 1)
            after(dve.tensor_tensor(SSQ, SSQ, HSC, ALU.mult))
            after(dve.tensor_tensor(SSQ, SSQ, HSC, ALU.mult))
            dve.tensor_scalar(SSQ, SSQ, 1.0 / MD, EPS, ALU.mult, ALU.add).then_inc(h_rt, 1)
            dve.wait_ge(h_root, 1)
            after(dve.reciprocal(RD, HTMP))
            after(dve.tensor_tensor(HSC, HSC, RD, ALU.mult))

            def mix(n):
                dve.wait_ge(h_tr, n + 1)
                for h in range(MH):
                    v = MO[:, h, n * P:(n + 1) * P]
                    last = dve.scalar_tensor_tensor(out=v, in0=ps[:, n % 4, h * P:(h + 1) * P], scalar=g_ml[:, h:h + 1], in1=v,
                                                    op0=ALU.mult, op1=ALU.mult)
                last.then_inc(h_mix, 1)

            for n in range(NT):
                if n >= 2:
                    mix(n - 2)
                dve.tensor_tensor(HST[:, n % 2].rearrange("p (h d) -> p h d", h=MH), NUM[:, n, :, 0:128],
                                  HSC[:, n * MH:(n + 1) * MH].unsqueeze(2).broadcast_to([P, MH, MD]), ALU.mult).then_inc(h_hs, 1)
            mix(NT - 2)
            mix(NT - 1)
            leave(dve, dve_stage)

            enter(dve, S_OUT0)
            dve.wait_ge(xb_in, 16 * NT)
            out_dve(dve, 0, tokens(2), (FQ, MO))
            leave(dve, dve_stage)
            enter(dve, S_NORM1)
            norm_dve(dve, 1, own)
            leave(dve, dve_stage)
            enter(dve, S_FF0)
            mlp_dve(dve, 0, tokens(2), HID0)
            leave(dve, dve_stage)
            enter(dve, S_NORM2)
            norm_dve(dve, 2, own)
            leave(dve, dve_stage)

            enter(dve, S_PROJ1)
            pieces(4 * NT)
            leave(dve, dve_stage)

            enter(dve, S_CB)
            tmp = fm(5)
            for m in range(4):
                dve.wait_ge(a_e, m + 1)
                dve.scalar_tensor_tensor(out=tmp[:, m], in0=CB[:, m], scalar=-1.0, in1=CB[:, m], op0=ALU.mult,
                                         op1=ALU.min).then_inc(a_cb, 1)
            dve.wait_ge(a_pre, 1)
            for m in range(4):
                dve.wait_ge(a_e, 4 + m + 1)
                after(dve.scalar_tensor_tensor(out=tmp[:, m], in0=CB[:, m], scalar=0.0, in1=tmp[:, m], op0=ALU.min,
                                               op1=ALU.subtract))
                after(dve.tensor_scalar(tmp[:, m], tmp[:, m], 1.0 / TAU, None, ALU.mult))
                dve.tensor_tensor_scan(CB[:, m], RESET, tmp[:, m], 0.0, ALU.mult, ALU.add)
            leave(dve, dve_stage)

            enter(dve, S_GLA)

            def gla_factors(n):
                t = slice(n * P, (n + 1) * P)
                dve.wait_ge(l_e, n + 1)
                for l, w in enumerate(LEVELS):
                    if n == PT and w > 8:
                        continue
                    e = EL[n % 2][:, l].rearrange("p h (n w) -> p h n w", w=2 * w)
                    k = GKT[:, :, t].rearrange("p h (n w) -> p h n w", w=2 * w)
                    q = GQ[:, :, t].rearrange("p h (n w) -> p h n w", w=2 * w)
                    dve.tensor_tensor(e[:, :, :, 0:w], e[:, :, :, 0:w], k[:, :, :, 0:w], ALU.mult)
                    last = dve.tensor_tensor(e[:, :, :, w:2 * w], e[:, :, :, w:2 * w], q[:, :, :, w:2 * w], ALU.mult)
                last.then_inc(l_m, 1)
                dve.wait_ge(l_eb, 2 * n + 1)
                dve.tensor_tensor(KS, KS, GKT[:, :, t], ALU.mult).then_inc(l_ks, 1)
                dve.wait_ge(l_eb, 2 * n + 2)
                if n < PT:
                    dve.tensor_tensor(QE, QE, GQ[:, :, t], ALU.mult).then_inc(l_qe, 1)
                else:
                    after(dve.tensor_tensor(QE, QE, GQ[:, :, t], ALU.mult))

            def gla_levels(n, h):
                q = 5 * n + h
                first = 0 if n < PT else 3
                dve.wait_ge(l_a, 4 * n + h + 1)
                if n >= 1 and h == 0:
                    dve.wait_ge(l_o, n)
                b = 2 * (q % 2)
                src = ps[:, b:b + 2, :].rearrange("p b (l t) -> p (b l) t", t=P)
                if n or h:
                    dve.wait_ge(l_at, 4 * n + h)
                dve.tensor_tensor(LT[:, first:], src[:, first:], sel[:, first:], ALU.mult).then_inc(l_free, 1)
                dve.wait_ge(l_free, q + 1)
                dve.tensor_reduce(LA[:, h], LT[:, first:].rearrange("p l t -> p t l"), AX.X, ALU.add).then_inc(l_at, 1)

            def gla_scale(n):
                dve.wait_ge(l_osq, n + 1)
                dve.tensor_scalar(osum[:, 0:4], osum[:, 0:4], 1.0 / GV, EPS, ALU.mult, ALU.add).then_inc(l_oln, 1)
                dve.wait_ge(l_oln, 2 * n + 2)
                if n >= 1:
                    dve.wait_ge(l_otr, n)
                for h in range(GH):
                    last = dve.tensor_scalar(OO[:, h], ps[:, 4 + h // 2, (h % 2) * GV:(h % 2 + 1) * GV],
                                             osum[:, 4 + h:5 + h], None, ALU.mult)
                last.then_inc(l_osc, 1)

            def gla_mix(n):
                q = 5 * n + 4
                dve.wait_ge(l_otr, n + 1)
                for c in range(8):
                    v = GG[:, c, n * P:(n + 1) * P]
                    last = dve.scalar_tensor_tensor(out=v, in0=ps[:, 2 * (q % 2) + c // 4, (c % 4) * P:(c % 4 + 1) * P],
                                                    scalar=g_gla[:, c:c + 1], in1=v, op0=ALU.mult, op1=ALU.mult)
                last.then_inc(l_free, 1)

            for n in range(PT):
                gla_factors(n)
                for h in range(GH):
                    gla_levels(n, h)
                dve.wait_ge(l_u, n + 1)
                for h in range(GH):
                    dve.scalar_tensor_tensor(out=SS[:, h], in0=SS[:, h], scalar=ecl[:, n % 2, h, 0:1],
                                             in1=ps[:, 6 + h // 2, (h % 2) * GV:(h % 2 + 1) * GV],
                                             op0=ALU.mult, op1=ALU.add).then_inc(l_sn, 1)
                gla_scale(n)
                gla_mix(n)
            leave(dve, dve_stage)

            enter(dve, S_GLAS)
            dve.wait_ge(l_v, 1)
            gla_factors(PT)
            for h in range(GH):
                gla_levels(PT, h)
            dve.wait_ge(l_ktev, PT + 1)
            for h in range(GH):
                if h >= 1:
                    dve.wait_ge(l_o, PT + h)
                    dve.wait_ge(l_u, PT + NSEQ * h)
                dve.tensor_copy(QEB.rearrange("p (b x) -> p b x", x=144)[:, :, 0:STEP],
                                QE[:, h].rearrange("p (b t) -> p b t", b=NSEQ)).then_inc(l_qe, 1)
                for b in range(NSEQ):
                    last = dve.tensor_scalar(KEB[:, b], KST[:, h], mask(C_IND + b, 1), None, ALU.mult)
                last.then_inc(l_keb, 1)
                if h >= 2:
                    dve.wait_ge(st_out[h % 2], 32 * (h // 2))
                for b in range(NSEQ):
                    g = NSEQ * h + b
                    dve.wait_ge(l_u, PT + g + 1)
                    dve.scalar_tensor_tensor(out=SNEW[h % 2][:, b // 4, b % 4], in0=SIN[h % 2][:, b // 4, b % 4],
                                             scalar=ecl[:, PT % 2, h, b:b + 1], in1=ps[:, 6 + g % 2, 0:GV],
                                             op0=ALU.mult, op1=ALU.add).then_inc(l_sn, 1)
            gla_scale(PT)
            gla_mix(PT)
            leave(dve, dve_stage)

            enter(dve, S_OUT1)
            dve.wait_ge(respill_in, 16)
            out_dve(dve, 1, tokens(6), (GG[:, 0:4], GG[:, 4:8]))
            leave(dve, dve_stage)
            enter(dve, S_NORM3)
            norm_dve(dve, 3, own)
            leave(dve, dve_stage)
            enter(dve, S_FF1)
            mlp_dve(dve, 1, tokens(6), HID1)
            leave(dve, dve_stage)

            enter(dve, S_FINAL)
            dve.wait_ge(sq_done, 5)
            dve.tensor_scalar(ssum, ssum, 1.0 / D, EPS, ALU.mult, ALU.add).then_inc(root_in, 1)
            dve.wait_ge(root_ready, 5)
            after(dve.reciprocal(ssum, rstd))
            dve.wait_ge(gain_in, 16 * 5)
            for n in range(NT):
                if n >= 4:
                    dve.wait_ge(y_out[n % 4], 16 * (n // 4))
                dve.scalar_tensor_tensor(out=unit(0, D, (n % 4) * D), in0=tokens(6)[:, n], scalar=ssum[:, n:n + 1],
                                         in1=unit(2, D), op0=ALU.mult, op1=ALU.mult).then_inc(y_ready, 1)


INPUTS = ["x_prompt", "x_sample", "cache_fox_k", "cache_fox_v", "cache_fox_logf", "state_mlstm_c", "state_mlstm_n",
          "state_mlstm_m", "state_mlstm_conv", "state_gla_s", "norm_mix", "norm_ffn", "norm_final", "w_in_even",
          "b_fox_f", "conv_w_ml", "conv_b_ml", "b_ml_i", "b_ml_f", "g_ml", "w_in_odd", "w_gla_a2", "b_gla_a", "g_gla",
          "w_out", "w_ff1", "w_ff2"]
OUTPUTS = {
    "y_prompt": (1, SEQ, D), "y_sample": (NSEQ, STEP, D),
    "p_fox_k": (1, 1, SEQ, FH, FD), "p_fox_v": (1, 1, SEQ, FH, FD), "p_fox_logf": (1, 1, SEQ, FH),
    "p_mlstm_c": (1, 1, MH, MD, MD), "p_mlstm_n": (1, 1, MH, MD), "p_mlstm_m": (1, 1, MH),
    "p_mlstm_conv": (1, 1, 3, D), "p_gla_s": (1, 1, GH, GK, GV),
    "s_fox_k": (1, NSEQ, STEP, FH, FD), "s_fox_v": (1, NSEQ, STEP, FH, FD), "s_fox_logf": (1, NSEQ, STEP, FH),
    "s_mlstm_c": (1, NSEQ, MH, MD, MD), "s_mlstm_n": (1, NSEQ, MH, MD), "s_mlstm_m": (1, NSEQ, MH),
    "s_mlstm_conv": (1, NSEQ, 3, D), "s_gla_s": (1, NSEQ, GH, GK, GV),
}


def kernel(**inputs):
    import concourse.bacc as bacc
    from concourse.bass_utils import run_bass_kernel_spmd

    nc = bacc.Bacc("TRN2", target_bir_lowering=False, num_devices=1, dynamic_dma_scratch_size=2048)
    arrays, i, o = {}, {}, {}
    for name in INPUTS:
        arrays[name] = np.ascontiguousarray(inputs[name])
    arrays.update(constants())
    for name, a in arrays.items():
        i[name] = nc.dram_tensor(name, a.shape, F32, kind="ExternalInput").ap()
    for name, shape in OUTPUTS.items():
        o[name] = nc.dram_tensor("out_" + name, shape, F32, kind="ExternalOutput").ap()
    scratch = nc.dram_tensor("stream", (P, NT * D), F32, kind="Internal").ap()
    park_mo = nc.dram_tensor("park_mo", (P, 4, T), F32, kind="Internal").ap()
    park_mv = nc.dram_tensor("park_mv", (T, MH * MD), F32, kind="Internal").ap()
    park_gv = nc.dram_tensor("park_gv", (T, GH * GV), F32, kind="Internal").ap()
    streaming_step(nc, i, o, scratch, park_mo, park_mv, park_gv)
    r = run_bass_kernel_spmd(nc, [arrays], core_ids=[0])
    return tuple(r.results[0]["out_" + name] for name in OUTPUTS)
```

```python
from contextlib import ExitStack

import numpy as np

import concourse.bass as bass
from concourse import mybir

F32 = mybir.dt.float32
F32R = mybir.dt.float32r
ALU = mybir.AluOpType
ACT = mybir.ActivationFunctionType
AX = mybir.AxisListType

P = 128
D = 1024
KC = D // P
SEQ, NSEQ, STEP, PAST = 1024, 8, 16, 256
T = SEQ + NSEQ * STEP
NT = T // P
PT = SEQ // P
GN = T // 3
FH, FD = 8, 64
MH, MD = 4, 128
GH, GK, GV = 4, 128, 256
TAPS = 4
FF = 4 * D
SLAB = 2048
COLS = 256
EPS = 1e-6
BIG = 1e30
TAU = 16.0
LEVELS = [64, 32, 16, 8, 4, 2, 1]
UNIT = 4672
UPAD = 3 + SEQ + NSEQ * (STEP + 3)

E_FQ, E_FK, E_FV, E_FF, E_MQK, E_MV, E_MO, E_MI, E_MF = 0, 512, 1024, 1536, 1544, 2568, 3080, 3592, 3596
O_GQ, O_GK, O_GV, O_GG, O_GA = 0, 512, 1024, 2048, 3072

C_ID, C_MQ, C_MC, C_MB, C_ONE, C_MW, C_IND, C_C16 = 0, 128, 256, 384, 512, 640, 880, 888
C_N = 904


def constants():
    a, b = np.arange(P)[:, None], np.arange(P)[None, :]
    same = (a // STEP) == (b // STEP)
    c = np.zeros((P, C_N), np.float32)
    c[:, C_ID:C_ID + P] = np.eye(P)
    c[:, C_MQ:C_MQ + P] = np.where(b <= a, 0, -BIG)
    c[:, C_MC:C_MC + P] = np.where(a <= b, 0, -BIG)
    c[:, C_MB:C_MB + P] = np.where((a <= b) & same, 0, -BIG)
    c[:, C_ONE:C_ONE + P] = 1
    wide = np.full((P, 240), -BIG, np.float32)
    wide[:, 112:128] = np.where(np.arange(STEP)[None, :] <= (np.arange(P) % STEP)[:, None], 0, -BIG)
    c[:, C_MW:C_MW + 240] = wide
    c[:, C_IND:C_IND + 8] = (a // STEP) == np.arange(NSEQ)[None, :]
    c[:, C_C16:C_C16 + 16] = (a % STEP) <= np.arange(STEP)[None, :]
    sel = np.zeros((P, 8, P), np.float32)
    for h in range(8):
        sel[h, h, :] = 1
    gmask = np.zeros((P, 8, P), np.float32)
    for i, w in enumerate(LEVELS):
        gmask[:, i] = (a // (2 * w) == b // (2 * w)) & (a % (2 * w) < w) & (b % (2 * w) >= w)
    gmask[:, 7] = np.eye(P)
    later = np.zeros((P, 3, 384), np.float32)
    strict = (b < a).astype(np.float32)
    later[:, 0, 0:128] = strict
    later[:, 1, 0:128] = 1
    later[:, 1, 128:256] = strict
    later[:, 2, 0:256] = 1
    later[:, 2, 256:384] = strict * same
    return {"c_masks": c, "c_sel": sel.reshape(P, 1024), "c_levels": gmask.reshape(P, 1024),
            "c_later": later.reshape(P, 1152)}


def link(eng, sem, count, instruction):
    count[0] += 1
    instruction.then_inc(sem, 1)
    eng.wait_ge(sem, count[0])


def streaming_step(nc, i, o, scratch, park_mo, park_mv, park_gv):
    ctx = ExitStack()
    with ctx:
        def sb(name, shape):
            return ctx.enter_context(nc.sbuf_tensor(name, shape, F32))

        def sem(name):
            return ctx.enter_context(nc.semaphore(name))

        at_units = -(-nc.sbuf_base // 32) * 32
        pairs = [sb(f"units{2 * q}", [P, 2 * UNIT]) for q in range(4)]
        pairs_r = [nc.alloc_sbuf_tensor_at(f"units{2 * q}_r", [P, 2 * UNIT], F32R, offset=at_units + q * 8 * UNIT)
                   for q in range(4)]

        def span(start, end, of=pairs):
            q = start // (2 * UNIT)
            assert end <= (q + 1) * 2 * UNIT
            return of[q][:, start - q * 2 * UNIT:end - q * 2 * UNIT]

        raw = sb("raw", [P, 2, SLAB])
        at_split = -(-nc.sbuf_base // 32) * 32
        lend = sb("lend", [P, 4 * SLAB])
        split = nc.alloc_sbuf_tensor_at("split", [P, 2, 2, SLAB], F32R, offset=at_split)
        masks = sb("masks", [P, C_N])
        sel = sb("sel", [P, 8, P])
        spare = sb("spare", [P, 2048])
        glrow = sb("glrow", [P, T])
        small = sb("small", [P, 920])
        at_junk = -(-nc.sbuf_base // 32) * 32
        junk256 = sb("junk256", [P, GV])[:, :]
        junk256_r = nc.alloc_sbuf_tensor_at("junk256_r", [P, GV], F32R, offset=at_junk)
        ps = ctx.enter_context(nc.psum_tensor("ps", [P, 8, 512], F32))

        used = [0]

        def few(n):
            used[0] += n
            assert used[0] <= 920
            return small[:, used[0] - n:used[0]]

        def unit(k, n=4608, at=0):
            return span(k * UNIT + at, k * UNIT + at + n)

        def fm(k, chunks=4):
            return unit(k, chunks * T).rearrange("p (c t) -> p c t", c=chunks)

        def tm(k, width):
            return unit(k, NT * width).rearrange("p (n w) -> p n w", n=NT)

        def mask(c, n=P):
            return masks[:, c:c + n]

        ident = mask(C_ID)
        convstate = few(KC * 27).rearrange("p (c n) -> p c n", c=KC)
        history = few(KC * 24).rearrange("p (c n) -> p c n", c=KC)
        params = few(56)
        gbias = few(3)
        lfT = few(NT * 8).rearrange("p (n h) -> p n h", n=NT)
        ssum, rstd = few(NT), few(NT)
        eps = few(1)
        stat = few(32)
        conv_w = params[:, 0:32].rearrange("p (j c) -> p j c", j=TAPS)
        conv_b, g_ml, b_gla, g_gla = params[:, 32:40], params[:, 40:44], params[:, 44:48], params[:, 48:56]

        pe_stage, act_stage, dve_stage, pool_stage = (sem(n) for n in ("pe_stage", "act_stage", "dve_stage", "pool_stage"))
        dve_own, act_own, pool_own = sem("dve_own"), sem("act_own"), sem("pool_own")
        raw_in = [sem("raw_in0"), sem("raw_in1")]
        hi_ready, lo_ready, slab_begun = sem("hi_ready"), sem("lo_ready"), sem("slab_begun")
        const_in, sel_in, param_in, gate_in, later_in, level_in, ga_in = (
            sem(n) for n in ("const_in", "sel_in", "param_in", "gate_in", "later_in", "level_in", "ga_in"))
        gain_in = sem("gain_in")
        out_done = sem("out_done")
        spill_done = sem("spill_done")
        par_tr, par_ev = sem("par_tr"), sem("par_ev")
        sq_done, tr_ready, tr_taken, root_ready = (sem(n) for n in ("sq_done", "tr_ready", "tr_taken", "root_ready"))
        xs_ready, x_in = sem("xs_ready"), [sem(f"x_in{r}") for r in range(3)]
        fm_ready, fm_taken, tmj_ready, tmj_taken, gate_ready = (
            sem(n) for n in ("fm_ready", "fm_taken", "tmj_ready", "tmj_taken", "gate_ready"))
        conv_ready, conv_done = sem("conv_ready"), sem("conv_done")
        g_a, g_b, g_rows, g_tr, g_cols = (sem(n) for n in ("g_a", "g_b", "g_rows", "g_tr", "g_cols"))
        fkT_ready, fkT_taken = sem("fkT_ready"), sem("fkT_taken")
        fk_out = [sem("fk_out0"), sem("fk_out1")]
        f_qz, f_kh, f_nh, f_s, f_mx, f_p, f_pt, f_pts, f_o, f_oev, f_ot = (
            sem(n) for n in ("f_qz", "f_kh", "f_nh", "f_s", "f_mx", "f_p", "f_pt", "f_pts", "f_o", "f_oev", "f_ot"))
        s_kt, s_kts, s_q, s_s, s_mx, s_p, s_pn, s_pt, s_pts, s_o, s_oev = (
            sem("s_" + n) for n in ("kt", "kts", "q", "s", "mx", "p", "pn", "pt", "pts", "o", "oev"))
        fn_in = [sem("fn_in0"), sem("fn_in1")]
        cache_in = [sem(f"cache_in{r}") for r in range(4)]
        pastlf_in = sem("pastlf_in")
        m_b, m_in, m_dm, m_w, m_g, m_a, m_kw, m_o, m_num, m_u, m_cn = (
            sem("m_" + n) for n in ("b", "in", "dm", "w", "g", "a", "kw", "o", "num", "u", "cn"))
        c_in, n_in, c_tr, c_ev, c_qg, c_kw, c_u, c_cn, c_ct, c_ctev, c_o, c_out = (
            sem("c_" + n) for n in ("in", "nin", "tr", "ev", "qg", "kw", "u", "cn", "ct", "ctev", "o", "out"))
        h_mean, h_root, h_hs, h_tr, h_mix = (sem("h_" + n) for n in ("mean", "root", "hs", "tr", "mix"))
        w_y, w_add = sem("w_y"), sem("w_add")
        ff_h, ff_relu, ff_sq, ff_hi, ff_lo, ff_y, ff_add = (sem("ff_" + n) for n in ("h", "relu", "sq", "hi", "lo", "y", "add"))
        norm_hi, mix_hi, mix_lo = sem("norm_hi"), sem("mix_hi"), sem("mix_lo")
        gate_out, piece_out = [sem(f"gate_out{r}") for r in range(2)], [sem(f"piece_out{r}") for r in range(3)]
        fv_back, mv_back, mo_back, gv_back = (sem(n) for n in ("fv_back", "mv_back", "mo_back", "gv_back"))
        a_e, a_l, a_cb, a_pre = (sem("a_" + n) for n in ("e", "l", "cb", "pre"))
        l_d, l_e, l_m, l_ks, l_kt, l_ktev, l_eb, l_qe = (sem("l_" + n) for n in ("d", "e", "m", "ks", "kt", "ktev", "eb", "qe"))
        l_free, l_keb = sem("l_free"), sem("l_keb")
        l_a, l_at, l_o, l_u, l_sn, l_osc, l_otr = (
            sem("l_" + n) for n in ("a", "at", "o", "u", "sn", "osc", "otr"))
        l_v = sem("l_v")
        st_in, st_out = [sem("st_in0"), sem("st_in1")], [sem("st_out0"), sem("st_out1")]
        y_ready, y_out = sem("y_ready"), [sem(f"y_out{r}") for r in range(4)]

        def columns(w, at):
            return w[:, at:at + COLS].rearrange("(k p) n -> p k n", p=P)

        def slabs_of(w, at, n):
            return [columns(w, at + COLS * c) for c in range(n)]

        we, wo_ = i["w_in_even"][0], i["w_in_odd"][0]
        first_slabs = slabs_of(we, E_MQK, 4) + slabs_of(we, E_FQ, 2) + slabs_of(we, E_FK, 2) + slabs_of(we, E_MO, 2)
        first_slabs += slabs_of(we, E_FV, 2) + slabs_of(we, E_MV, 2)
        GATES0 = len(first_slabs)
        first_slabs += [((0, 8, E_FF), (32, 4, E_MI), (64, 4, E_MF))]
        OUT0 = len(first_slabs)
        first_slabs += slabs_of(i["w_out"][0], 0, 4)
        MLP0 = len(first_slabs)
        HB = 512
        BLOCKS = FF // HB
        ODD = MLP0 + 4 * BLOCKS
        odd_slabs = slabs_of(wo_, O_GQ, 2) + slabs_of(wo_, O_GK, 2) + slabs_of(wo_, O_GG, 4) + slabs_of(wo_, O_GV, 4)
        GATES1 = ODD + len(odd_slabs)
        odd_slabs += [((0, 16, O_GA),)]
        OUT1 = ODD + len(odd_slabs)
        odd_slabs += slabs_of(i["w_out"][1], 0, 4)
        MLP1 = ODD + len(odd_slabs)

        def hi_of(act, n, blk=0, free=False):
            act.wait_ge(raw_in[n % 2], raw_count(n) + blk * 32)
            if not free:
                act.wait_ge(slab_begun, blk * 4 + n)
            act.activation(split[:, n % 2, 0, :], raw[:, n % 2, :], ACT.Copy).then_inc(hi_ready, 1)

        def lo_of(pool, n, blk=0):
            pool.wait_ge(hi_ready, blk * 4 + (n + 1))
            pool.tensor_tensor(split[:, n % 2, 1, :], raw[:, n % 2, :], split[:, n % 2, 0, :], ALU.subtract).then_inc(lo_ready, 1)

        def raw_count(n):
            more = {GATES0: 2, GATES1: 0}
            return 16 * (n // 2 + 1 + sum(m for g, m in more.items() if g <= n and g % 2 == n % 2))

        def weights(n, part, k, c0, width, chunk=COLS):
            return split[:, n % 2, part, :].rearrange("p (k n) -> p k n", n=chunk)[:, k, c0:c0 + width]

        PASSES = ((0, 0), (0, 1), (1, 0))

        def enter(eng, stage):
            for s in (pe_stage, act_stage, dve_stage, pool_stage):
                eng.wait_ge(s, stage)

        def leave(eng, s):
            eng.drain().then_inc(s, 1)

        block = ctx.enter_context(nc.Block())

        (S_LOAD, S_NORM0, S_PROJ0, S_GATES, S_FOX, S_FOXS, S_ML, S_MLS, S_MLH, S_OUT0, S_NORM1, S_FF0,
         S_NORM2, S_PROJ1, S_CB, S_GLA, S_GLAS, S_OUT1, S_NORM3, S_FF1, S_FINAL) = range(21)

        def wide(k):
            return span(k * UNIT, k * UNIT + NT * D)

        def tokens(k):
            return wide(k).rearrange("p (n d) -> p n d", n=NT)

        def features(k):
            return wide(k).rearrange("p (c t) -> p c t", c=KC)

        def part(k):
            return span(k * UNIT, k * UNIT + NT * D, pairs_r).rearrange("p (c t) -> p c t", c=KC)

        def hidden(k):
            return span(k * UNIT, k * UNIT + 4 * T, pairs_r).rearrange("p (c t) -> p c t", c=4)

        HID0, HID1 = (hidden(6), hidden(7)), (hidden(2), hidden(3))
        MQ, MK, FK, FQ = fm(4), fm(5), fm(6), fm(7)
        FV, MO = tm(0, 512), fm(6)
        MV = unit(1, NT * MH * 129).rearrange("p (n h d) -> p n h d", n=NT, h=MH)
        norms = [
            (tokens(4), 0, 2, 6, i["norm_mix"][0]),
            (tokens(2), 0, 4, 6, i["norm_ffn"][0]),
            (tokens(2), 0, 4, 6, i["norm_mix"][1]),
            (tokens(6), 0, 4, 2, i["norm_ffn"][1]),
        ]
        GQ, GKT, GG, GVT, CB = fm(6), fm(7), features(2), tokens(0), fm(4)

        def norm_parts(k):
            s = norms[k][3]
            return (unit(s, 2048).rearrange("p (b d) -> p b d", b=2), unit(s, 1024, 2048), unit(s, 1024, 3072))

        stage_of_norm = [S_NORM0, S_NORM1, S_NORM2, S_NORM3]

        def two_banks(n):
            b = 2 * (n % 4)
            return ps[:, b:b + 2, :].rearrange("p b (c t) -> p (b c) t", c=4)

        def x_count(g, from_inputs, from_scratch):
            return 16 * ((2 if g == 2 else 1) * from_inputs + from_scratch)

        def root_mean_square(act, own, junk, row, n):
            link(act, act_own, own, act.activation(junk, row, ACT.Square, scale=D ** -0.5, accum_out=ssum[:, n:n + 1]))
            act.activation(ssum[:, n:n + 1], ssum[:, n:n + 1], ACT.Sqrt, bias=eps).then_inc(sq_done, 1)

        def norm_act(act, k, own, between=None):
            x, hi, _, _, _ = norms[k]
            _, junk, _ = norm_parts(k)

            def mean_square(n):
                if k == 0 and n % 3 == 0:
                    act.wait_ge(x_in[n // 3], x_count(n // 3, 1, 0))
                root_mean_square(act, own, junk, x[:, n], n)

            for n in range(3):
                mean_square(n)
            if between:
                between()
            for n in range(NT):
                act.wait_ge(tr_ready, NT * k + n + 1)
                act.activation(part(hi)[:, :, n * P:(n + 1) * P], two_banks(n), ACT.Copy).then_inc(norm_hi, 1)
                if n + 3 < NT:
                    mean_square(n + 3)
                if k == 0 and n in (1, 4):
                    hi_of(act, n // 3, free=True)

        def norm_dve(dve, k):
            x, hi, lo = norms[k][:3]
            xs, _, gain_ = norm_parts(k)

            def low(n):
                t = slice(n * P, (n + 1) * P)
                dve.wait_ge(norm_hi, NT * k + n + 1)
                dve.tensor_tensor(part(lo)[:, :, t], two_banks(n), part(hi)[:, :, t], ALU.subtract).then_inc(tr_taken, 1)

            def scaled(n):
                dve.wait_ge(root_ready, NT * k + n + 1)
                if n >= 2:
                    dve.wait_ge(tr_ready, NT * k + n - 1)
                dve.scalar_tensor_tensor(out=xs[:, n % 2], in0=x[:, n], scalar=rstd[:, n:n + 1], in1=gain_,
                                         op0=ALU.mult, op1=ALU.mult).then_inc(xs_ready, 1)

            for n in range(3):
                inverse(dve, NT * k + n)
            dve.wait_ge(gain_in, 16 * (k + 1))
            scaled(0)
            scaled(1)
            for n in range(NT):
                if n + 2 < NT:
                    scaled(n + 2)
                low(n)
                if n + 3 < NT:
                    inverse(dve, NT * k + n + 3)

        def inverse(dve, n):
            dve.wait_ge(sq_done, n + 1)
            m = n % NT
            dve.reciprocal(rstd[:, m:m + 1], ssum[:, m:m + 1]).then_inc(root_ready, 1)

        def norm_pe(pe, k):
            xs, _, _ = norm_parts(k)
            for n in range(NT):
                pe.wait_ge(xs_ready, NT * k + n + 1)
                if n >= 4:
                    pe.wait_ge(tr_taken, NT * k + n - 3)
                for c in range(KC):
                    last = pe.transpose(ps[:, 2 * (n % 4) + c // 4, (c % 4) * P:(c % 4 + 1) * P],
                                        xs[:, n % 2, c * P:(c + 1) * P], ident)
                last.then_inc(tr_ready, 1)

        def begin(instruction, first):
            if first:
                instruction.then_inc(slab_begun, 1)

        def proj_fm(pe, bank, slab, c0, h):
            for k in range(KC):
                for q, (a, b) in enumerate(PASSES):
                    for n in range(3):
                        last = pe.matmul(ps[:, bank + n, 0:GN], weights(slab, a, k, c0, P),
                                         h[b][:, k, n * GN:(n + 1) * GN],
                                         start=(k == 0 and q == 0), stop=(k == KC - 1 and q == 2))
                        begin(last, c0 == 0 and k == 0 and q == 0 and n == 0)
            return last

        def proj_tm(pe, out, slab, h, n, first):
            for k in range(KC):
                for q, (a, b) in enumerate(PASSES):
                    last = pe.matmul(out, h[b][:, k, n * P:(n + 1) * P], weights(slab, a, k, 0, COLS),
                                     start=(k == 0 and q == 0), stop=(k == KC - 1 and q == 2))
                    begin(last, first and k == 0 and q == 0)
            return last

        def group(job):
            g = 3 * (job % 2)
            return ps[:, g:g + 3, 0:GN]

        def as_groups(row):
            return row.rearrange("p (g t) -> p g t", g=3)

        def out_act(act, layer, sources):
            base = (OUT0, OUT1)[layer]
            if layer:
                hi_of(act, base, free=True)
            for n in range(NT):
                t = slice(n * P, (n + 1) * P)
                for c, src in enumerate(sources):
                    last = act.activation(part(0)[:, 4 * c:4 * c + 4, t], src[:, :, t], ACT.Copy)
                last.then_inc(mix_hi, 1)
                if n == 0 and layer:
                    hi_of(act, base + 1, free=True)
            for m in range(2, 5):
                hi_of(act, base + m)

        def out_pool(pool, layer):
            for m in range(0 if layer else 2, 5):
                lo_of(pool, (OUT0, OUT1)[layer] + m)

        def out_pe(pe, layer):
            h = part(0), part(4)
            for c in range(4):
                s = (OUT0, OUT1)[layer] + c
                pe.wait_ge(lo_ready, s + 1)
                for n in range(NT):
                    j = c * NT + n
                    if c == 0:
                        pe.wait_ge(mix_lo, NT * layer + n + 1)
                    if j >= 4:
                        pe.wait_ge(w_add, 4 * NT * layer + j - 3)
                    proj_tm(pe, ps[:, j % 4, 0:COLS], s, h, n, n == 0).then_inc(w_y, 1)

        def out_dve(dve, layer, x, sources):
            def add(j):
                dve.wait_ge(w_y, 4 * NT * layer + j + 1)
                if j < NT and j % 3 == 0:
                    dve.wait_ge(x_in[j // 3], x_count(j // 3, 2, layer))
                xx = x[:, j % NT, (j // NT) * COLS:(j // NT + 1) * COLS]
                dve.tensor_tensor(xx, xx, ps[:, j % 4, 0:COLS], ALU.add).then_inc(w_add, 1)

            for n in range(NT):
                t = slice(n * P, (n + 1) * P)
                dve.wait_ge(mix_hi, NT * layer + n + 1)
                for c, src in enumerate(sources):
                    last = dve.tensor_tensor(part(4)[:, 4 * c:4 * c + 4, t], src[:, :, t],
                                             part(0)[:, 4 * c:4 * c + 4, t], ALU.subtract)
                last.then_inc(mix_lo, 1)
                if n >= 1:
                    add(n - 1)
            for j in range(NT - 1, 4 * NT):
                add(j)

        HC = HB // P
        YJ = 2 * NT
        YBANK = (6, 7, 3, 4, 5, 0, 1, 2)
        YLAG = 4
        HTMP_ = (spare[:, 0:T], glrow[:, :])

        def hidden_bank(j):
            return 3 if j % 2 == 0 else 0

        def blocks(eng, body, last):
            with eng.Fori(0, BLOCKS - last) as blk:
                body(blk, False)
            if last:
                body(BLOCKS - 1, True)

        def mlp_pe(pe, layer, base, h, hid):
            def body(blk, last):
                for j in range(HC):
                    slab = base + j // 2
                    if j % 2 == 0:
                        pe.wait_ge(lo_ready, blk * 4 + (slab + 1))
                    if j >= 2:
                        pe.wait_ge(ff_relu, blk * HC + (layer * FF // P + j - 1))
                    proj_fm(pe, hidden_bank(j), slab, (j % 2) * P, h).then_inc(ff_h, 1)

                def pieces(j, chunks):
                    half, n = j // NT, j % NT
                    for k in chunks:
                        for q, (a, b) in enumerate(PASSES):
                            one = pe.matmul(ps[:, YBANK[j % 8], :], hid[b][:, k, n * P:(n + 1) * P],
                                            weights(base + 2 + half, a, k, 0, 512, 512),
                                            start=(k == 0 and q == 0), stop=(k == HC - 1 and q == 2))
                            begin(one, n == 0 and q == 0 and k == (0, HC - 1)[half])
                    return one

                for j in range(YJ + YLAG):
                    if j < YJ:
                        if j % NT == 0:
                            pe.wait_ge(lo_ready, blk * 4 + (base + 3 + j // NT))
                        if j == 0:
                            pe.wait_ge(ff_lo, blk * HC + (layer * FF // P + HC - 1))
                        if j >= 8:
                            pe.wait_ge(ff_add, blk * YJ + (layer * YJ * BLOCKS + j - 7))
                        pieces(j, range(HC - 1))
                    if j >= YLAG:
                        if j == YLAG:
                            pe.wait_ge(ff_lo, blk * HC + (layer * FF // P + HC))
                        pieces(j - YLAG, (HC - 1,)).then_inc(ff_y, 1)
                pe.wait_ge(ff_add, blk * YJ + (layer * YJ * BLOCKS + YJ - 2))

            blocks(pe, body, 0)

        def mlp_act(act, layer, base, hid):
            def body(blk, last):
                def high(j):
                    act.wait_ge(ff_sq, blk * HC + (layer * FF // P + j + 1))
                    act.activation(hid[0][:, j], HTMP_[j % 2], ACT.Copy).then_inc(ff_hi, 1)

                for j in range(HC):
                    if j % 2 == 0:
                        hi_of(act, base + j // 2 + 1, blk)
                    act.wait_ge(ff_h, blk * HC + (layer * FF // P + j + 1))
                    if j >= 2:
                        act.wait_ge(ff_lo, blk * HC + (layer * FF // P + j - 1))
                    b = hidden_bank(j)
                    act.activation(as_groups(HTMP_[j % 2]), ps[:, b:b + 3, 0:GN], ACT.Relu).then_inc(ff_relu, 1)
                    high(j)
                hi_of(act, base + 3, blk)
                if not last:
                    hi_of(act, base + 4, blk)

            blocks(act, body, layer)

        def mlp_pool(pool, layer, base):
            def body(blk, last):
                for j in range(1, 4 if last else 5):
                    lo_of(pool, base + j, blk)

            blocks(pool, body, layer)

        def mlp_dve(dve, layer, x, hid):
            def body(blk, last):
                for j in range(HC):
                    tmp = HTMP_[j % 2]
                    dve.wait_ge(ff_relu, blk * HC + (layer * FF // P + j + 1))
                    dve.tensor_tensor(tmp, tmp, tmp, ALU.mult).then_inc(ff_sq, 1)
                    dve.wait_ge(ff_hi, blk * HC + (layer * FF // P + j + 1))
                    dve.tensor_tensor(hid[1][:, j], tmp, hid[0][:, j], ALU.subtract).then_inc(ff_lo, 1)
                for j in range(YJ):
                    half, n = j // NT, j % NT
                    dve.wait_ge(ff_y, blk * YJ + (layer * YJ * BLOCKS + j + 1))
                    xx = x[:, n, half * 512:(half + 1) * 512]
                    dve.tensor_tensor(xx, xx, ps[:, YBANK[j % 8], :], ALU.add).then_inc(ff_add, 1)

            blocks(dve, body, 0)

        base2 = 2 * UNIT

        def scratch_row(n):
            return span(base2 + n * T, base2 + (n + 1) * T)

        RF, RI, RM, LF, LM, TF, TM_ = (scratch_row(n) for n in range(7))
        FN = span(base2 + 2 * UNIT - T, base2 + 2 * UNIT)
        BM, IB, MM = (lend[:, n * T:(n + 1) * T] for n in range(3))
        GL, RESET = glrow[:, :], glrow[:, :]
        ONES = spare[:, 0:SEQ]
        mbefore = few(9)
        enmT = few(NT * MH).rearrange("p (n h) -> p n h", n=NT)
        ibT = few(NT * MH).rearrange("p (n h) -> p n h", n=NT)
        ecl = few(2 * 32).rearrange("p (r h b) -> p r h b", r=2, h=GH)
        osum = few(8)
        SSQ = few(NT * MH)

        otok = span(base2, base2 + 4096).rearrange("p (b f) -> p b f", b=PT)
        FNROW = span(base2 + 4096, base2 + 5120)
        KP = [[span(UNIT + 1024 * (2 * r + q), UNIT + 1024 * (2 * r + q + 1), pairs_r) for q in range(2)] for r in range(2)]
        split_row = split.rearrange("p a b n -> p (a b n)")
        QP = [[split_row[:, 3 * T + 1024 * (2 * r + q):3 * T + 1024 * (2 * r + q + 1)] for q in range(2)] for r in range(2)]
        ident_r, mask_r = junk256_r[:, 0:P], junk256_r[:, P:2 * P]

        def head_rows(h):
            r = 64 * (h % 2)
            return slice(r, r + 64), slice(64 - r, 65 - r)
        PR = [span(base2 + 6144 + 1024 * r, base2 + 7168 + 1024 * r) for r in range(2)]
        PTS = [spare[:, 1024 * r:1024 * (r + 1)] for r in range(2)]
        FKST = [spare[:, 1024 + 512 * r:1536 + 512 * r] for r in range(2)]
        fox_jobs = [(h, q) for h in range(FH) for q in range(PT)]
        NJ = len(fox_jobs)

        place = [base2]

        def take(n):
            place[0] += n
            return span(place[0] - n, place[0])

        KIN = [take(1024) for _ in range(2)] + [lend[:, 3 * T + 1024 * r:3 * T + 1024 * (r + 1)] for r in range(2)]
        VIN = [take(1024) for _ in range(2)] + [lend[:, 3 * T + 1024 * r:3 * T + 1024 * (r + 1)] for r in range(2, 4)]
        KIN, VIN = ([b.rearrange("p (j f) -> p j f", j=2) for b in ring] for ring in (KIN, VIN))
        KT = take(1536).rearrange("p (c k) -> p c k", c=4)
        QB = [take(640) for _ in range(2)]
        LOG_F = [take(384).rearrange("p (j r) -> p j r", j=3) for _ in range(2)]
        LNEW, SP, SPT_, PLF = take(128), take(384), take(384), take(128)
        SPT = SPT_.rearrange("p (j r) -> p j r", j=3)
        assert place[0] <= base2 + 2 * UNIT
        LATER = spare[:, 0:1152].rearrange("p (j k) -> p j k", j=3)

        place[0] = base2
        WT, GB, AT, QG, KW = (take(512).rearrange("p (h t) -> p h t", h=MH) for _ in range(5))
        CN = take(MH * 129).rearrange("p (h d) -> p h d", h=MH)
        CRAW = [lend[:, 3 * T + 1024 * h:3 * T + 1024 * (h + 1)].rearrange("p (b d) -> p b d", b=NSEQ) for h in range(MH)]
        CNS = take(NSEQ * 129).rearrange("p (b d) -> p b d", b=NSEQ)
        QGB = take(NSEQ * 144)
        KWB = take(1024).rearrange("p (b d) -> p b d", b=NSEQ)
        NROW, NOUT = take(128), take(128)
        NCOL, NNEW = take(32), take(36)
        assert place[0] <= base2 + 2 * UNIT
        NUM = unit(0, NT * MH * 129).rearrange("p (n h d) -> p n h d", n=NT, h=MH)
        HST = unit(5, 1024).rearrange("p (b d) -> p b d", b=2)
        HJUNK = junk256[:, 0:128]
        RD, HSC = (unit(5, 36, 1152 + 36 * r) for r in range(2))

        EL = [lend[:, 3584 * r:3584 * (r + 1)].rearrange("p (l h t) -> p l h t", l=7, h=GH)
              for r in range(2)]
        place[0] = 5 * UNIT
        LT = take(1024).rearrange("p (l t) -> p l t", l=8)
        LA = take(512).rearrange("p (h t) -> p h t", h=GH)
        QE = take(512).rearrange("p (h t) -> p h t", h=GH)
        assert place[0] <= 6 * UNIT
        KS = glrow[:, 0:512].rearrange("p (h t) -> p h t", h=GH)
        KST = glrow[:, 512:1024].rearrange("p (h t) -> p h t", h=GH)
        SS = spare[:, 0:1024].rearrange("p (h v) -> p h v", h=GH)
        OO = spare[:, 1024:2048].rearrange("p (h v) -> p h v", h=GH)
        GAT, WA2 = spare[:, 0:1152], spare[:, 1152:1664]
        SIN = [GQ[:, 2 * r:2 * r + 2, 0:SEQ].rearrange("p c (b v) -> p c b v", v=GV) for r in range(2)]
        SNEW = [GKT[:, 2 * r:2 * r + 2, 0:SEQ].rearrange("p c (b v) -> p c b v", v=GV) for r in range(2)]
        def levels_turn(n, h):
            return 5 * n + h - (h == 0 and 0 < n < PT)

        def state_bank(g):
            return ps[:, 6 + g % 2, 0:GV]

        def output_turn(n):
            return 5 * n + 4 + (n + 1 < PT)

        QEB = lend[:, 3584:3584 + NSEQ * 144]
        KEB = lend[:, 3584 + 1152:3584 + 2176].rearrange("p (b k) -> p b k", b=NSEQ)

        def sample(row):
            return row[:, SEQ:T].rearrange("p (b t) -> p b t", b=NSEQ)

        def starts(n):
            return slice(SEQ, T, STEP) if n else slice(0, SEQ, P)

        GATE_ST = (glrow[:, :], spare[:, 0:T])
        PIECE_ST = [spare[:, T + COLS * r:T + COLS * (r + 1)] for r in range(3)]
        def conv_in(j):
            return unit(6, UPAD, (j % 3) * UPAD)

        def conv_seq(j):
            return conv_in(j)[:, 3 + SEQ:].rearrange("p (b t) -> p b t", b=NSEQ)

        def conv_out(j):
            return (MQ if j < 4 else MK)[:, j % 4]

        @block.sync
        def _(sp):
            def place_of(n, chunk):
                return raw[:, n % 2, :].rearrange("p (k n) -> p k n", n=chunk)

            def load(n, src):
                if n >= 2:
                    sp.wait_ge(lo_ready, n - 1)
                if isinstance(src, tuple):
                    for at, width, column in src:
                        w = we if n == GATES0 else wo_
                        sp.dma_start(place_of(n, COLS)[:, :, at:at + width],
                                     w[:, column:column + width].rearrange("(k p) n -> p k n", p=P)).then_inc(raw_in[n % 2], 16)
                else:
                    sp.dma_start(place_of(n, COLS), src).then_inc(raw_in[n % 2], 16)

            def tokens_in(x):
                for g in range(3):
                    last = min(3 * g + 3, PT)
                    sp.dma_start(x[:, 3 * g:last], i["x_prompt"][0, 3 * g * P:last * P, :].rearrange("(n p) d -> p n d", p=P)
                                 ).then_inc(x_in[g], 16)
                    if g == 0:
                        sp.wait_ge(param_in, 16 * 6)
                sp.dma_start(x[:, PT], i["x_sample"].rearrange("b t d -> (b t) d")).then_inc(x_in[2], 16)

            sp.dma_start(masks[:, :], i["c_masks"]).then_inc(const_in, 16)
            tokens_in(tokens(4))
            sp.dma_start(sel.rearrange("p h t -> p (h t)"), i["c_sel"]).then_inc(sel_in, 16)
            for n, src in enumerate(first_slabs):
                load(n, src)
                if n == OUT0 + 1:
                    for t in range(NT):
                        sp.wait_ge(fkT_taken, t + 1)
                        dst = o["p_fox_k"][0, 0, t * P:(t + 1) * P].rearrange("t h d -> t (h d)") if t < PT \
                            else o["s_fox_k"][0].rearrange("b t h d -> (b t) (h d)")
                        sp.dma_start(dst, FKST[t % 2]).then_inc(fk_out[t % 2], 16)
                if n == OUT0 + 2:
                    for stage in (pe_stage, act_stage, dve_stage, pool_stage):
                        sp.wait_ge(stage, S_OUT0)
                    tokens_in(tokens(2))

            def mlp(layer, base):
                w1 = i["w_ff1"][layer].rearrange("(k p) (b n) -> b p k n", p=P, n=COLS)
                w2 = i["w_ff2"][layer].rearrange("(b k p) n -> b p k n", p=P, k=HC)
                with sp.Fori(0, BLOCKS) as blk:
                    for j, w in ((0, w1), (1, w1), (2, w2), (3, w2)):
                        n = base + j
                        sp.wait_ge(lo_ready, blk * 4 + (n - 1))
                        src = w[bass.ds(blk * 2 + j, 1)] if j < 2 else w[bass.ds(blk, 1), :, :, (j - 2) * 512:(j - 1) * 512]
                        src = src.rearrange("o p k n -> (o p) k n")
                        sp.dma_start(place_of(n, COLS if j < 2 else 512), src).then_inc(raw_in[n % 2], 16)

            mlp(0, MLP0)
            for n, src in enumerate(odd_slabs):
                load(ODD + n, src)
                if ODD + n == OUT1 + 1:
                    for stage in (pe_stage, act_stage, dve_stage, pool_stage):
                        sp.wait_ge(stage, S_OUT1)
                    for g in range(3):
                        at = slice(3 * g * D, (3 * g + 3) * D)
                        sp.dma_start(wide(6)[:, at], scratch[:, at]).then_inc(x_in[g], 16)
            mlp(1, MLP1)

        @block.gpsimd
        def _(pool):
            outs, pown = [0], [0]

            def put(dst, src):
                outs[0] += 16
                pool.dma_start(dst, src).then_inc(out_done, 16)

            def gain(k):
                pool.dma_start(norm_parts(k)[2], norms[k][4].partition_broadcast(P)).then_inc(gain_in, 16)

            gain(0)
            leave(pool, pool_stage)

            pool.dma_start(gbias[0:8, 0:1], i["b_fox_f"].rearrange("o h -> h o")).then_inc(gate_in, 16)
            pool.dma_start(gbias[0:4, 1:2], i["b_ml_i"].rearrange("o h -> h o")).then_inc(gate_in, 16)
            pool.dma_start(gbias[0:4, 2:3], i["b_ml_f"].rearrange("o h -> h o")).then_inc(gate_in, 16)
            with nc.allow_non_contiguous_dma(reason="32 values"):
                pool.dma_start(mbefore[0:4, 1:9], i["state_mlstm_m"][0].rearrange("b h -> h b")).then_inc(gate_in, 16)
            pool.memset(mbefore[0:4, 0:1], 0.0)
            lo_of(pool, 0)
            lo_of(pool, 1)
            leave(pool, pool_stage)

            def piece_to(j):
                c, n = j // NT, j % NT
                if c < 2 and n < PT:
                    return o["p_fox_v"][0, 0, n * P:(n + 1) * P, 4 * c:4 * c + 4, :].rearrange("t h d -> t (h d)")
                if c < 2:
                    return o["s_fox_v"][0, :, :, 4 * c:4 * c + 4, :].rearrange("b t h d -> (b t) (h d)")
                to, c = (park_mv, c - 2) if c < 4 else (park_gv, c - 4)
                return to[n * P:(n + 1) * P, c * COLS:(c + 1) * COLS]

            def pieces_out(first):
                for j in range(first, first + NT):
                    pool.wait_ge(tmj_taken, j + 1)
                    pool.dma_start(piece_to(j), PIECE_ST[j % 3]).then_inc(piece_out[j % 3], 16)

            def all_pieces_out(n):
                for r in range(3):
                    pool.wait_ge(piece_out[r], 16 * (n // 3))

            enter(pool, S_PROJ0)
            for r in range(3):
                last = pool.memset(conv_in(r)[:, 0:3], 0.0)
            last.then_inc(conv_ready, 1)
            for m in range(1, GATES0):
                lo_of(pool, m + 1)
                if m in (8, 9):
                    for c in (2 * m - 16, 2 * m - 15):
                        pool.wait_ge(fm_taken, 16 + c + 1)
                        pool.dma_start(park_mo[:, c], GATE_ST[c % 2]).then_inc(gate_out[c % 2], 16)
                elif m >= 10:
                    pieces_out(NT * (m - 10))
            pool.wait_ge(gate_out[0], 32)
            pool.wait_ge(gate_out[1], 32)
            all_pieces_out(4 * NT)
            leave(pool, pool_stage)

            enter(pool, S_GATES)
            pool.dma_start(FV[:, 0:PT], o["p_fox_v"][0, 0].rearrange("(n p) h d -> p n (h d)", p=P)).then_inc(fv_back, 16)
            pool.dma_start(FV[:, PT], o["s_fox_v"][0].rearrange("b t h d -> (b t) (h d)")).then_inc(fv_back, 16)
            for r in range(2):
                own_rows, row = head_rows(r)
                other = head_rows(1 - r)[0]
                for q in range(2):
                    pool.memset(KP[r][q][other].bitcast(F32), 0.0)
                    link(pool, pool_own, pown, pool.memset(QP[r][q][other].bitcast(F32), 0.0))
                pool.memset(QP[r][0][row].bitcast(F32), 1.0)

            def low_parts(h):
                r = head_rows(h)[0]
                pool.wait_ge(f_kh, h + 1)
                for two, src in ((KP[h % 2], FK), (QP[h % 2], FQ)):
                    pool.tensor_tensor(two[1][r], src[r, h // 2, 0:SEQ], two[0][r], ALU.subtract)

            def low_sums(h):
                row = head_rows(h)[1]
                pool.wait_ge(f_nh, h + 1)
                k = KP[h % 2]
                pool.tensor_tensor(k[1][row], FNROW[row], k[0][row], ALU.subtract).then_inc(f_qz, 1)

            low_parts(0)
            low_parts(1)
            pool.wait_ge(g_cols, 1)
            put(o["p_fox_logf"][0, 0].rearrange("(n p) h -> p n h", p=P), lfT[:, 0:PT])
            put(o["s_fox_logf"][0].rearrange("b t h -> (b t) h"), lfT[:, PT])
            pool.wait_ge(g_rows, 1)
            with nc.allow_non_contiguous_dma(reason="36 values"):
                put(o["p_mlstm_m"][0].rearrange("o h -> h o"), MM[0:4, SEQ - 1:SEQ])
                put(o["s_mlstm_m"][0].rearrange("b h -> h b"), MM[0:4, SEQ + STEP - 1:T:STEP])
            leave(pool, pool_stage)

            enter(pool, S_FOX)

            def sums_row(h):
                pool.dma_start(FNROW[head_rows(h)[1]], FN[h:h + 1, 0:SEQ]).then_inc(fn_in[h % 2], 16)

            sums_row(0)
            sums_row(1)
            for h in range(FH):
                if h >= 2:
                    low_parts(h)
                low_sums(h)
                if h + 2 < FH:
                    pool.wait_ge(f_qz, h + 1)
                    sums_row(h + 2)
            leave(pool, pool_stage)

            enter(pool, S_FOXS)
            pool.memset(QB[0], 0.0)
            pool.memset(QB[1], 0.0).then_inc(s_q, 1)
            pool.dma_start(LATER.rearrange("p j k -> p (j k)"), i["c_later"]).then_inc(later_in, 16)
            for jt in range(2):
                pool.dma_start(PLF.rearrange("p (b j h) -> p b j h", b=NSEQ, j=2)[:, :, jt],
                               i["cache_fox_logf"][0, :, jt * P:(jt + 1) * P].rearrange("b p h -> p b h")).then_inc(pastlf_in, 16)
            for b in range(NSEQ):
                if b >= 4:
                    pool.wait_ge(s_o, b - 3)
                for buf, src in ((KIN, i["cache_fox_k"]), (VIN, i["cache_fox_v"])):
                    pool.dma_start(buf[b % 4], src[0, b].rearrange("(j p) h d -> p j (h d)", p=P)).then_inc(cache_in[b % 4], 16)
            pool.memset(MV[:, :, :, 128:129], 1.0)
            for n in range(NT):
                pool.dma_start(MV[:, n, :, 0:128],
                               park_mv[n * P:(n + 1) * P].rearrange("p (h d) -> p h d", h=MH)).then_inc(mv_back, 16)
            leave(pool, pool_stage)

            enter(pool, S_ML)
            pool.dma_start(fm(6), park_mo).then_inc(mo_back, 16)
            pool.memset(CN.rearrange("p h d -> p (h d)"), 0.0).then_inc(m_cn, 1)
            pool.memset(QGB, 0.0)
            pool.dma_start(NROW[0:32, :], i["state_mlstm_n"][0].rearrange("b h d -> (b h) d")).then_inc(n_in, 16)
            for h in range(MH):
                pool.dma_start(CRAW[h], i["state_mlstm_c"][0, :, h].rearrange("b e d -> e b d")).then_inc(c_in, 16)
            leave(pool, pool_stage)

            enter(pool, S_MLS)
            put(o["p_mlstm_c"][0, 0].rearrange("h e d -> e h d"), QG)
            put(o["p_mlstm_n"][0, 0], NOUT[0:4, :])
            for h in range(MH):
                pool.wait_ge(c_ctev, h + 1)
                pool.dma_start(o["s_mlstm_c"][0, :, h].rearrange("b e d -> e b d"), CRAW[h]).then_inc(c_out, 16)
            pool.wait_ge(c_out, 16 * MH)
            pool.wait_ge(c_o, 1)
            put(o["s_mlstm_n"][0].rearrange("b h d -> (b h) d"), NROW[0:32, :])
            leave(pool, pool_stage)

            enter(pool, S_MLH)
            lo_of(pool, OUT0)
            lo_of(pool, OUT0 + 1)
            cs = KWB.rearrange("p b d -> p (b d)")
            put(o["p_mlstm_conv"][0, 0], cs[0:3, :])
            put(o["s_mlstm_conv"][0].rearrange("b j f -> (b j) f"), cs[3:27, :])
            pool.wait_ge(out_done, outs[0])
            leave(pool, pool_stage)

            enter(pool, S_OUT0)
            out_pool(pool, 0)
            leave(pool, pool_stage)
            enter(pool, S_NORM1)
            gain(1)
            leave(pool, pool_stage)
            enter(pool, S_FF0)
            mlp_pool(pool, 0, MLP0)
            leave(pool, pool_stage)

            enter(pool, S_NORM2)
            gain(2)
            pool.dma_start(sel.rearrange("p h t -> p (h t)"), i["c_levels"]).then_inc(level_in, 16)
            pool.dma_start(scratch, wide(2)).then_inc(spill_done, 16)
            pool.wait_ge(spill_done, 16)
            leave(pool, pool_stage)

            enter(pool, S_PROJ1)
            for m in range(ODD, GATES1):
                lo_of(pool, m + 1)
                if m >= ODD + 8:
                    pieces_out(4 * NT + NT * (m - ODD - 8))
            all_pieces_out(8 * NT)
            pool.dma_start(WA2[0:16, :], i["w_gla_a2"][0]).then_inc(ga_in, 16)
            leave(pool, pool_stage)

            enter(pool, S_CB)
            pool.dma_start(GVT, park_gv.rearrange("(n p) d -> p n d", p=P)).then_inc(gv_back, 16)
            link(pool, pool_own, pown, pool.memset(RESET, 1.0))
            pool.memset(RESET[:, starts(0)], 0.0)
            pool.memset(RESET[:, starts(1)], 0.0).then_inc(a_pre, 1)
            leave(pool, pool_stage)

            enter(pool, S_GLA)
            pool.memset(SS.rearrange("p h v -> p (h v)"), 0.0).then_inc(l_sn, 1)

            def exponents(n):
                cb = CB[:, :, n * P:(n + 1) * P]
                if n >= 2:
                    pool.wait_ge(l_a, 4 * (n - 1))
                for l, w in enumerate(LEVELS):
                    if n == PT and w > 8:
                        continue
                    np_ = P // (2 * w)
                    pairs = cb.rearrange("p h (n w) -> p h n w", w=2 * w)
                    e = EL[n % 2][:, l].rearrange("p h (n w) -> p h n w", w=2 * w)
                    edge = pairs[:, :, :, w - 1:w].broadcast_to([P, GH, np_, w])
                    pool.tensor_tensor(e[:, :, :, 0:w], edge, pairs[:, :, :, 0:w], ALU.subtract)
                    last = pool.tensor_tensor(e[:, :, :, w:2 * w], pairs[:, :, :, w:2 * w], edge, ALU.subtract)
                last.then_inc(l_d, 1)
                if n >= 1:
                    pool.wait_ge(l_kt, n)
                seg = P if n < PT else STEP
                ends = cb.rearrange("p h (b t) -> p h b t", t=seg)
                pool.tensor_tensor(KS.rearrange("p h (b t) -> p h b t", t=seg),
                                   ends[:, :, :, seg - 1:seg].broadcast_to([P, GH, P // seg, seg]), ends,
                                   ALU.subtract).then_inc(l_d, 1)

            for n in range(NT):
                exponents(n)
            leave(pool, pool_stage)

            enter(pool, S_GLAS)
            pool.memset(QEB, 0.0).then_inc(l_v, 1)
            put(o["p_gla_s"][0, 0].rearrange("h k v -> k h v"), SS)

            def state_in(h):
                for c in range(2):
                    pool.dma_start(SIN[h % 2][:, c],
                                   i["state_gla_s"][0, 4 * c:4 * c + 4, h].rearrange("b k v -> k b v")).then_inc(st_in[h % 2], 16)

            state_in(0)
            state_in(1)
            for h in range(GH):
                pool.wait_ge(l_sn, 1 + 4 * PT + NSEQ * (h + 1))
                for c in range(2):
                    pool.dma_start(o["s_gla_s"][0, 4 * c:4 * c + 4, h].rearrange("b k v -> k b v"),
                                   SNEW[h % 2][:, c]).then_inc(st_out[h % 2], 16)
                if h + 2 < GH:
                    state_in(h + 2)
            pool.wait_ge(st_out[0], 64)
            pool.wait_ge(st_out[1], 64)
            pool.wait_ge(out_done, outs[0])
            leave(pool, pool_stage)

            enter(pool, S_OUT1)
            out_pool(pool, 1)
            leave(pool, pool_stage)
            enter(pool, S_NORM3)
            gain(3)
            leave(pool, pool_stage)
            enter(pool, S_FF1)
            mlp_pool(pool, 1, MLP1)
            leave(pool, pool_stage)

            enter(pool, S_FINAL)
            pool.dma_start(unit(2, D), i["norm_final"].partition_broadcast(P)).then_inc(gain_in, 16)
            for n in range(NT):
                pool.wait_ge(y_ready, n + 1)
                dst = o["y_prompt"][0, n * P:(n + 1) * P] if n < PT else o["y_sample"].rearrange("b t d -> (b t) d")
                pool.dma_start(dst, unit(0, D, (n % 4) * D)).then_inc(y_out[n % 4], 16)
            for r in range(4):
                pool.wait_ge(y_out[r], 16 * len(range(r, NT, 4)))

        @block.tensor
        def _(pe):
            pe.wait_ge(const_in, 16)
            pe.wait_ge(param_in, 16 * 6)
            pe.transpose(ps[:, 0, 0:56], unit(0, P)[0:56, :], ident[0:56, 0:56]).then_inc(par_tr, 1)
            for c in range(KC):
                last = pe.transpose(ps[:, 1, c * 24:(c + 1) * 24], unit(0, D, P)[0:24, c * P:(c + 1) * P], ident[0:24, 0:24])
            last.then_inc(par_tr, 1)
            leave(pe, pe_stage)

            pe.wait_ge(par_ev, 1)
            norm_pe(pe, 0)
            leave(pe, pe_stage)

            enter(pe, S_PROJ0)
            h = part(0), part(2)

            def fm_jobs(jobs, base, before):
                for j in range(jobs):
                    if j % 2 == 0:
                        pe.wait_ge(lo_ready, base + j // 2 + 1)
                    if j >= 2:
                        pe.wait_ge(fm_taken, before + j - 1)
                    proj_fm(pe, 3 * (j % 2), base + j // 2, (j % 2) * P, h).then_inc(fm_ready, 1)

            def tm_jobs(slabs, base, before):
                for j in range(slabs * NT):
                    if j % NT == 0:
                        pe.wait_ge(lo_ready, base + j // NT + 1)
                    if j >= 2:
                        pe.wait_ge(tmj_taken, before + j - 1)
                    proj_tm(pe, ps[:, 6 + j % 2, 0:COLS], base + j // NT, h, j % NT, j % NT == 0).then_inc(tmj_ready, 1)

            fm_jobs(20, 0, 0)
            tm_jobs(4, 10, 0)
            pe.wait_ge(lo_ready, GATES0 + 1)
            pe.wait_ge(sel_in, 16)
            pe.wait_ge(fm_taken, 20)
            proj_fm(pe, 0, GATES0, 0, h).then_inc(gate_ready, 1)
            pe.wait_ge(tmj_taken, 4 * NT)
            leave(pe, pe_stage)

            enter(pe, S_GATES)
            for n in range(NT):
                if n >= 2:
                    pe.wait_ge(fkT_taken, n - 1)
                for c in range(4):
                    last = pe.transpose(ps[:, 4 + n % 2, c * P:(c + 1) * P], FK[:, c, n * P:(n + 1) * P], ident)
                last.then_inc(fkT_ready, 1)
            pe.wait_ge(g_rows, 1)
            for n in range(NT):
                pe.transpose(ps[:, 0, n * 8:(n + 1) * 8], LF[0:8, n * P:(n + 1) * P], ident[0:8, 0:8])
                pe.transpose(ps[:, 0, 72 + n * 4:76 + n * 4], IB[0:4, n * P:(n + 1) * P], ident[0:4, 0:4])
                last = pe.transpose(ps[:, 0, 108 + n * 4:112 + n * 4], MM[0:4, n * P:(n + 1) * P], ident[0:4, 0:4])
            last.then_inc(g_tr, 1)
            leave(pe, pe_stage)

            enter(pe, S_FOX)
            pe.wait_ge(fv_back, 32)

            def scores(j):
                h, q = fox_jobs[j]
                width = (q + 1) * P
                pe.wait_ge(f_qz, h + 1)
                if j >= 2:
                    pe.wait_ge(f_p, j - 1)
                for c in range(0, width, 512):
                    w = min(512, width - c)
                    out = ps[:, 2 * (j % 2) + c // 512, 0:w]
                    last_part = c + w == width
                    for a, b in PASSES:
                        last = pe.matmul(out, QP[h % 2][b][:, q * P:(q + 1) * P], KP[h % 2][a][:, c:c + w], start=(a + b == 0),
                                         stop=(a == 1 and not last_part))
                    if last_part:
                        last = pe.matmul(out[:, w - P:w], ident_r, mask_r, start=False, stop=True)
                last.then_inc(f_s, 1)

            def probs(j):
                h, q = fox_jobs[j]
                pe.wait_ge(f_p, j + 1)
                if j >= 1:
                    pe.wait_ge(f_pts, j)
                for t in range(q + 1):
                    last = pe.transpose(ps[:, 4 + t // 4, (t % 4) * P:(t % 4 + 1) * P], PR[j % 2][:, t * P:(t + 1) * P], ident)
                last.then_inc(f_pt, 1)

            def values(j):
                h, q = fox_jobs[j]
                pe.wait_ge(f_pts, j + 1)
                if j >= 2:
                    pe.wait_ge(f_oev, j - 1)
                for t in range(q + 1):
                    last = pe.matmul(ps[:, 6 + j % 2, 0:FD], PTS[j % 2][:, t * P:(t + 1) * P], FV[:, t, h * FD:(h + 1) * FD],
                                     start=(t == 0), stop=(t == q))
                last.then_inc(f_o, 1)

            scores(0)
            for j in range(NJ):
                if j + 1 < NJ:
                    scores(j + 1)
                probs(j)
                if j >= 1:
                    values(j - 1)
            values(NJ - 1)
            pe.wait_ge(f_oev, NJ)
            for n in range(PT):
                for c in range(4):
                    last = pe.transpose(ps[:, n, c * P:(c + 1) * P], otok[:, n, c * P:(c + 1) * P], ident)
                last.then_inc(f_ot, 1)
            leave(pe, pe_stage)

            enter(pe, S_FOXS)
            pe.wait_ge(later_in, 16)

            def seq_out(b):
                pe.wait_ge(s_pn, b + 1)
                for t in range(3):
                    last = pe.transpose(ps[:, 4, t * P:(t + 1) * P], SP[:, t * P:(t + 1) * P], ident)
                last.then_inc(s_pt, 1)
                pe.wait_ge(s_pts, b + 1)
                if b >= 1:
                    pe.wait_ge(s_oev, b)
                for c in range(4):
                    for t in range(3):
                        v = VIN[b % 4][:, t, c * P:(c + 1) * P] if t < 2 else FV[:, PT, c * P:(c + 1) * P]
                        last = pe.matmul(ps[:, 6, c * 32:(c + 1) * 32], v, SPT[:, t, c * 32:(c + 1) * 32],
                                         start=(t == 0), stop=(t == 2))
                last.then_inc(s_o, 1)

            def seq_keys(b):
                pe.wait_ge(cache_in[b % 4], 32 * (b // 4 + 1))
                if b >= 1:
                    pe.wait_ge(s_kts, b)
                for j in range(2):
                    for c in range(4):
                        at = c * 256 + j * P
                        last = pe.transpose(ps[:, at // 512, at % 512:at % 512 + P], KIN[b % 4][:, j, c * P:(c + 1) * P], ident)
                last.then_inc(s_kt, 1)

            def seq_scores(b):
                pe.wait_ge(s_kts, b + 1)
                pe.wait_ge(s_q, b + 2)
                if b >= 2:
                    pe.wait_ge(s_p, b - 1)
                out = ps[:, 2 + b % 2, 0:384]
                for c in range(4):
                    pe.matmul(out, QB[b % 2][:, c * P:(c + 1) * P], KT[:, c, :], start=(c == 0), stop=False)
                for t in range(3):
                    pe.matmul(out, LOG_F[b % 2][:, t, :], LATER[:, t, :], start=False, stop=False)
                pe.matmul(out[:, 256:384], ident, mask(C_MW + 112 - STEP * b), start=False, stop=True).then_inc(s_s, 1)

            seq_keys(0)
            seq_scores(0)
            seq_keys(1)
            for b in range(NSEQ):
                if b + 1 < NSEQ:
                    seq_scores(b + 1)
                if b + 2 < NSEQ:
                    seq_keys(b + 2)
                seq_out(b)
            leave(pe, pe_stage)

            enter(pe, S_ML)
            pe.wait_ge(mv_back, 16 * NT)

            def ml_inputs(n):
                t = slice(n * P, (n + 1) * P)
                for h in range(MH):
                    last = pe.matmul(ps[:, 0, h * P:(h + 1) * P], sel[:, h, :], BM[:, t], start=True, stop=True)
                last.then_inc(m_b, 1)
                for h in range(MH):
                    pe.matmul(ps[:, 1, h * P:(h + 1) * P], sel[:, h, :], GL[:, t], start=True, stop=True)
                    pe.matmul(ps[:, 2, h * P:(h + 1) * P], MK[:, h, t], MQ[:, h, t], start=True, stop=True)
                    last = pe.transpose(ps[:, 3, h * P:(h + 1) * P], MK[:, h, t], ident)
                last.then_inc(m_in, 1)

            for n in range(PT):
                if n >= 1:
                    pe.wait_ge(m_kw, n)
                    pe.wait_ge(m_g, n)
                ml_inputs(n)
                pe.wait_ge(m_a, n + 1)
                pe.wait_ge(m_cn, n + 1)
                if n >= 1:
                    pe.wait_ge(m_num, n)
                for h in range(MH):
                    out = ps[:, 4 + h // 2, (h % 2) * 129:(h % 2 + 1) * 129]
                    pe.matmul(out, AT[:, h], MV[:, n, h], start=True, stop=False)
                    last = pe.matmul(out, QG[:, h], CN[:, h], start=False, stop=True)
                last.then_inc(m_o, 1)
                pe.wait_ge(m_kw, n + 1)
                for h in range(MH):
                    last = pe.matmul(ps[:, 6 + h // 2, (h % 2) * 129:(h % 2 + 1) * 129], KW[:, h], MV[:, n, h],
                                     start=True, stop=True)
                last.then_inc(m_u, 1)
            pe.wait_ge(m_cn, PT + 1)
            pe.wait_ge(m_kw, PT)
            for h in range(MH):
                last = pe.transpose(ps[:, 0, h * P:(h + 1) * P], CN[:, h, 0:128], ident)
            pe.wait_ge(n_in, 16)
            pe.transpose(ps[0:4, 1, 0:P], NNEW[:, 32:36], ident)
            pe.transpose(ps[:, 2, 0:32], NROW[0:32, :], ident[0:32, 0:32]).then_inc(c_ct, 1)
            leave(pe, pe_stage)

            enter(pe, S_MLS)
            ml_inputs(PT)
            pe.wait_ge(m_a, PT + 1)
            pe.wait_ge(m_kw, PT + 1)
            pe.wait_ge(c_in, 16 * MH)
            for h in range(MH):
                for b in range(NSEQ):
                    last = pe.transpose(ps[:, b // 4, (b % 4) * P:(b % 4 + 1) * P], CRAW[h][:, b], ident)
                last.then_inc(c_tr, 1)
                pe.wait_ge(c_ev, h + 1)
                pe.wait_ge(c_qg, h + 1)
                out = ps[:, 4, 0:129]
                pe.matmul(out, AT[:, h], MV[:, PT, h], start=True, stop=False)
                for b in range(NSEQ):
                    last = pe.matmul(out, QGB[:, b * P:(b + 1) * P], CNS[:, b], start=False, stop=(b == NSEQ - 1))
                last.then_inc(m_o, 1)
                pe.wait_ge(c_kw, h + 1)
                for b in range(NSEQ):
                    last = pe.matmul(ps[:, 5 + b // 3, (b % 3) * 129:(b % 3 + 1) * 129], KWB[:, b], MV[:, PT, h],
                                     start=True, stop=True)
                last.then_inc(c_u, 1)
                pe.wait_ge(c_cn, h + 1)
                for b in range(NSEQ):
                    last = pe.transpose(ps[:, b // 4, (b % 4) * P:(b % 4 + 1) * P], CNS[:, b, 0:128], ident)
                last.then_inc(c_ct, 1)
                pe.wait_ge(c_ctev, h + 1)
            pe.transpose(ps[0:32, 2, 0:P], NNEW[:, 0:32], ident)
            for c in range(KC):
                last = pe.transpose(ps[0:27, 5 + c // 4, (c % 4) * P:(c % 4 + 1) * P], convstate[:, c], ident)
            last.then_inc(c_ct, 1)
            leave(pe, pe_stage)

            enter(pe, S_MLH)
            for n in range(NT):
                pe.wait_ge(h_hs, n + 1)
                if n >= 4:
                    pe.wait_ge(h_mix, n - 3)
                for h in range(MH):
                    last = pe.transpose(ps[:, n % 4, h * P:(h + 1) * P], HST[:, n % 2, h * P:(h + 1) * P], ident)
                last.then_inc(h_tr, 1)
            leave(pe, pe_stage)

            enter(pe, S_OUT0)
            out_pe(pe, 0)
            leave(pe, pe_stage)
            enter(pe, S_NORM1)
            norm_pe(pe, 1)
            leave(pe, pe_stage)
            enter(pe, S_FF0)
            mlp_pe(pe, 0, MLP0, (part(0), part(4)), HID0)
            leave(pe, pe_stage)
            enter(pe, S_NORM2)
            norm_pe(pe, 2)
            leave(pe, pe_stage)

            enter(pe, S_PROJ1)
            h = part(0), part(4)
            fm_jobs(16, ODD, 20)
            tm_jobs(4, ODD + 8, 4 * NT)
            pe.wait_ge(lo_ready, GATES1 + 1)
            pe.wait_ge(fm_taken, 36)
            proj_fm(pe, 0, GATES1, 0, h).then_inc(gate_ready, 1)
            pe.wait_ge(tmj_taken, 8 * NT)
            leave(pe, pe_stage)

            enter(pe, S_CB)
            pe.wait_ge(ga_in, 16)
            for m in range(4):
                if m >= 2:
                    pe.wait_ge(a_e, m - 1)
                for n in range(3):
                    last = pe.matmul(ps[:, 3 * (m % 2) + n, 0:GN], WA2[0:16, m * P:(m + 1) * P],
                                     GAT[0:16, n * GN:(n + 1) * GN], start=True, stop=True)
                last.then_inc(a_l, 1)
            leave(pe, pe_stage)

            enter(pe, S_GLA)
            pe.wait_ge(level_in, 16)
            pe.wait_ge(gv_back, 16)

            def level_pair(q):
                return 2 * (q % 2)

            def gla_scaled_keys(n):
                pe.wait_ge(l_ks, n + 1)
                if n >= 1:
                    pe.wait_ge(l_sn, 1 + 4 * n)
                for h in range(GH):
                    last = pe.transpose(ps[:, 6, h * P:(h + 1) * P], KS[:, h], ident)
                last.then_inc(l_kt, 1)

            def gla_levels_of(n, h):
                t = slice(n * P, (n + 1) * P)
                q = levels_turn(n, h)
                pe.wait_ge(l_m, n + 1)
                if q >= 2:
                    pe.wait_ge(l_free, q - 1)
                for l in range(8):
                    out = ps[:, level_pair(q) + l // 4, (l % 4) * P:(l % 4 + 1) * P]
                    if l == 7:
                        last = pe.matmul(out, GKT[:, h, t], GQ[:, h, t], start=True, stop=True)
                    elif n < PT or LEVELS[l] <= 8:
                        pe.matmul(out, EL[n % 2][:, l, h], EL[n % 2][:, l, h], start=True, stop=True)
                last.then_inc(l_a, 1)

            def gla_turn(n):
                q = output_turn(n)
                pe.wait_ge(l_osc, n + 1)
                pe.wait_ge(l_free, q - 1)
                for c in range(8):
                    last = pe.transpose(ps[:, level_pair(q) + c // 4, (c % 4) * P:(c % 4 + 1) * P],
                                        OO[:, c // 2, (c % 2) * P:(c % 2 + 1) * P], ident)
                last.then_inc(l_otr, 1)

            gla_levels_of(0, 0)
            for n in range(PT):
                gla_levels_of(n, 1)
                gla_levels_of(n, 2)
                gla_scaled_keys(n)
                gla_levels_of(n, 3)
                pe.wait_ge(l_qe, n + 1)
                pe.wait_ge(l_sn, 1 + 4 * n)
                if n >= 1:
                    pe.wait_ge(l_osc, n)
                for h in range(GH):
                    pe.wait_ge(l_at, 4 * n + h + 1)
                    out = ps[:, 4 + h // 2, (h % 2) * GV:(h % 2 + 1) * GV]
                    pe.matmul(out, LA[:, h], GVT[:, n, h * GV:(h + 1) * GV], start=True, stop=False)
                    last = pe.matmul(out, QE[:, h], SS[:, h], start=False, stop=True)
                last.then_inc(l_o, 1)
                pe.wait_ge(l_ktev, n + 1)
                for h in range(GH):
                    last = pe.matmul(ps[:, 6 + h // 2, (h % 2) * GV:(h % 2 + 1) * GV], KST[:, h],
                                     GVT[:, n, h * GV:(h + 1) * GV], start=True, stop=True)
                last.then_inc(l_u, 1)
                if n + 1 < PT:
                    gla_levels_of(n + 1, 0)
                gla_turn(n)
            leave(pe, pe_stage)

            enter(pe, S_GLAS)
            gla_scaled_keys(PT)
            for h in range(GH):
                gla_levels_of(PT, h)
            for h in range(GH):
                pe.wait_ge(l_at, 4 * PT + h + 1)
                pe.wait_ge(l_qe, PT + h + 1)
                pe.wait_ge(st_in[h % 2], 32 * (h // 2 + 1))
                out = ps[:, 4 + h // 2, (h % 2) * GV:(h % 2 + 1) * GV]
                pe.matmul(out, LA[:, h], GVT[:, PT, h * GV:(h + 1) * GV], start=True, stop=False)
                for b in range(NSEQ):
                    last = pe.matmul(out, QEB[:, b * P:(b + 1) * P], SIN[h % 2][:, b // 4, b % 4], start=False,
                                     stop=(b == NSEQ - 1))
                last.then_inc(l_o, 1)
                pe.wait_ge(l_keb, h + 1)
                for b in range(NSEQ):
                    g = NSEQ * h + b
                    if g >= 2:
                        pe.wait_ge(l_sn, 1 + 4 * PT + g - 1)
                    pe.matmul(state_bank(g), KEB[:, b], GVT[:, PT, h * GV:(h + 1) * GV],
                              start=True, stop=True).then_inc(l_u, 1)
            gla_turn(PT)
            leave(pe, pe_stage)

            enter(pe, S_OUT1)
            out_pe(pe, 1)
            leave(pe, pe_stage)
            enter(pe, S_NORM3)
            norm_pe(pe, 3)
            leave(pe, pe_stage)
            enter(pe, S_FF1)
            mlp_pe(pe, 1, MLP1, (part(0), part(4)), HID1)
            leave(pe, pe_stage)

        @block.scalar
        def _(act):
            own = [0]
            rows = unit(0, P)
            for r, src in ((0, i["conv_w_ml"][0].rearrange("j (c p) -> (j c) p", p=P)),
                           (32, i["conv_b_ml"][0].rearrange("(c p) -> c p", p=P)),
                           (40, i["g_ml"][0].rearrange("(c p) -> c p", p=P)),
                           (44, i["b_gla_a"][0].rearrange("(c p) -> c p", p=P)),
                           (48, i["g_gla"][0].rearrange("(c p) -> c p", p=P))):
                act.dma_start(rows[r:r + src.shape[0], :], src).then_inc(param_in, 16)
            act.dma_start(unit(0, D, P)[0:24, :], i["state_mlstm_conv"][0].rearrange("b j f -> (b j) f")).then_inc(param_in, 16)
            leave(act, act_stage)

            def parameters():
                act.wait_ge(par_tr, 2)
                act.activation(params, ps[:, 0, 0:56], ACT.Copy)
                act.activation(history.rearrange("p c n -> p (c n)"), ps[:, 1, 0:192], ACT.Copy).then_inc(par_ev, 1)

            act.wait_ge(dve_stage, 1)
            norm_act(act, 0, own, parameters)
            leave(act, act_stage)

            enter(act, S_PROJ0)

            def silu(j):
                act.wait_ge(conv_done, j + 1)
                one = act.activation(conv_out(j), conv_out(j), ACT.Silu)
                if j >= 4:
                    link(act, act_own, own, one)
                    act.activation(conv_out(j), conv_out(j), ACT.Copy, scale=MD ** -0.5)

            act.wait_ge(conv_ready, 1)
            for j in range(20):
                if j % 2 == 0 and j >= 2:
                    hi_of(act, j // 2 + 1)
                act.wait_ge(fm_ready, j + 1)
                g = 3 * (j % 2)
                if j < KC:
                    if j >= 3:
                        act.wait_ge(conv_done, j - 2)
                    u = conv_in(j)
                    act.activation(conv_seq(j)[:, :, 0:3], history[:, j].rearrange("p (b t) -> p b t", b=NSEQ), ACT.Copy)
                    act.activation(u[:, 3:3 + 2 * GN].rearrange("p (g t) -> p g t", g=2), ps[:, g:g + 2, 0:GN], ACT.Copy)
                    act.activation(u[:, 3 + 2 * GN:3 + SEQ], ps[:, g + 2, 0:256], ACT.Copy)
                    link(act, act_own, own, act.activation(
                        conv_seq(j)[:, :, 3:], ps[:, g + 2, 256:384].rearrange("p (b t) -> p b t", b=NSEQ), ACT.Copy))
                    act.activation(conv_out(j)[:, 0:SEQ], u[:, 0:SEQ], ACT.Identity, scale=conv_w[:, 0, j:j + 1],
                                   bias=conv_b[:, j:j + 1])
                    act.activation(sample(conv_out(j)), conv_seq(j)[:, :, 0:STEP], ACT.Identity,
                                   scale=conv_w[:, 0, j:j + 1], bias=conv_b[:, j:j + 1]).then_inc(fm_taken, 1)
                elif j < 12:
                    act.activation(as_groups(FQ[:, j - 8]), group(j), ACT.Copy, scale=FD ** -0.5).then_inc(fm_taken, 1)
                elif j < 16:
                    act.activation(as_groups(FK[:, j - 12]), group(j), ACT.Copy).then_inc(fm_taken, 1)
                else:
                    if j >= 18:
                        act.wait_ge(gate_out[j % 2], 16)
                    act.activation(as_groups(GATE_ST[j % 2]), group(j), ACT.Sigmoid).then_inc(fm_taken, 1)
                if 1 <= j <= KC:
                    silu(j - 1)
            for m in range(10, GATES0):
                hi_of(act, m + 1)
            act.wait_ge(gate_ready, 1)
            act.wait_ge(gate_in, 64)
            for g, (row, m) in enumerate(((RF, 8), (RI, 4), (RM, 4))):
                act.activation(as_groups(row)[0:m], ps[32 * g:32 * g + m, 0:3, 0:GN], ACT.Identity, bias=gbias[0:m, g:g + 1])
            leave(act, act_stage)

            enter(act, S_GATES)

            def keys_out(n):
                act.wait_ge(fkT_ready, n + 1)
                if n >= 2:
                    act.wait_ge(fk_out[n % 2], 16 * (n // 2))
                act.activation(FKST[n % 2], ps[:, 4 + n % 2, :], ACT.Copy).then_inc(fkT_taken, 1)

            def high_parts(h):
                r, row = head_rows(h)
                if h >= 2:
                    act.wait_ge(f_s, PT * (h - 1))
                act.activation(KP[h % 2][0][r], FK[r, h // 2, 0:SEQ], ACT.Copy)
                act.activation(QP[h % 2][0][r], FQ[r, h // 2, 0:SEQ], ACT.Copy).then_inc(f_kh, 1)

            def high_sums(h):
                row = head_rows(h)[1]
                act.wait_ge(fn_in[h % 2], 16 * (h // 2 + 1))
                act.activation(KP[h % 2][0][row], FNROW[row], ACT.Copy).then_inc(f_nh, 1)

            keys_out(0)
            keys_out(1)
            act.wait_ge(g_a, 1)
            act.activation(TF[0:8, :], TF[0:8, :], ACT.Exp)
            link(act, act_own, own, act.activation(TM_[0:4, :], TM_[0:4, :], ACT.Exp))
            act.activation(TF[0:8, :], TF[0:8, :], ACT.Ln, bias=1.0)
            act.activation(TM_[0:4, :], TM_[0:4, :], ACT.Ln, bias=1.0).then_inc(g_b, 1)
            high_parts(0)
            high_parts(1)
            for n in range(2, NT):
                keys_out(n)
            act.wait_ge(g_tr, 1)
            act.activation(lfT.rearrange("p n h -> p (n h)"), ps[:, 0, 0:72], ACT.Copy)
            act.activation(ibT.rearrange("p n h -> p (n h)"), ps[:, 0, 72:108], ACT.Copy)
            act.activation(enmT.rearrange("p n h -> p (n h)"), ps[:, 0, 108:144], ACT.Exp, scale=-1.0).then_inc(g_cols, 1)
            leave(act, act_stage)

            enter(act, S_FOX)
            act.activation(ident_r, ident, ACT.Copy)
            act.activation(mask_r, mask(C_MQ), ACT.Copy)
            high_sums(0)
            high_sums(1)
            for j, (h, q) in enumerate(fox_jobs):
                if q == 2 and 1 <= h < FH - 1:
                    high_parts(h + 1)
                    high_sums(h + 1)
                act.wait_ge(f_mx, j + 1)
                if j >= 2:
                    act.wait_ge(f_pt, j - 1)
                w = (q + 1) * P
                src = ps[:, 2 * (j % 2):2 * (j % 2) + 2, :].rearrange("p b k -> p (b k)")[:, 0:w]
                act.activation(PR[j % 2][:, 0:w], src, ACT.Exp, bias=stat[:, 4 + j % 4:5 + j % 4],
                               accum_out=stat[:, 8 + j % 4:9 + j % 4]).then_inc(f_p, 1)
            for n in range(PT):
                act.wait_ge(f_ot, n + 1)
                act.activation(FQ[:, :, n * P:(n + 1) * P], ps[:, n, :].rearrange("p (c t) -> p c t", c=4), ACT.Copy)
            leave(act, act_stage)

            enter(act, S_FOXS)
            def seq_keys(b):
                act.wait_ge(s_kt, b + 1)
                if b >= 1:
                    act.wait_ge(s_s, b)
                act.activation(KT[:, :, 0:256], ps[:, 0:2, :].rearrange("p b (c k) -> p (b c) k", c=2), ACT.Copy).then_inc(s_kts, 1)

            def seq_exp(b):
                act.wait_ge(s_mx, b + 1)
                act.activation(SP, ps[:, 2 + b % 2, 0:384], ACT.Exp, bias=stat[:, 1:2], accum_out=stat[:, 2:3]).then_inc(s_p, 1)

            seq_keys(0)
            seq_exp(0)
            seq_keys(1)
            for b in range(NSEQ):
                act.wait_ge(s_pt, b + 1)
                if b >= 1:
                    act.wait_ge(s_o, b)
                act.activation(SPT_, ps[:, 4, 0:384], ACT.Copy).then_inc(s_pts, 1)
                if b + 1 < NSEQ:
                    seq_exp(b + 1)
                if b + 2 < NSEQ:
                    seq_keys(b + 2)
            leave(act, act_stage)

            enter(act, S_ML)

            def ml_act(n):
                act.wait_ge(m_dm, n + 1)
                for h in range(MH):
                    last = act.activation(WT[:, h], WT[:, h], ACT.Exp, bias=ibT[:, n, h:h + 1])
                last.then_inc(m_w, 1)
                if n >= 1:
                    act.wait_ge(m_cn, n + 1)
                act.wait_ge(m_in, n + 1)
                act.activation(GB.rearrange("p h t -> p (h t)"), ps[:, 1, :], ACT.Exp).then_inc(m_g, 1)

            def square(n, h):
                link(act, act_own, own, act.activation(HJUNK, NUM[:, n, h, 0:128], ACT.Square,
                                                       accum_out=SSQ[:, n * MH + h:n * MH + h + 1]))

            for n in range(PT):
                ml_act(n)
                if n >= 1:
                    act.wait_ge(m_num, n)
                    for h in range(MH):
                        square(n - 1, h)
                act.wait_ge(m_o, n + 1)
                act.activation(NUM[:, n].rearrange("p (b h) d -> p b (h d)", b=2), ps[:, 4:6, 0:258], ACT.Copy).then_inc(m_num, 1)
            act.wait_ge(m_num, PT)
            for h in range(MH):
                square(PT - 1, h)
            act.wait_ge(c_ct, 1)
            act.activation(QG.rearrange("p h t -> p (h t)"), ps[:, 0, :], ACT.Copy)
            act.activation(NOUT[0:4, :], ps[0:4, 1, 0:P], ACT.Copy)
            act.activation(NCOL, ps[:, 2, 0:32], ACT.Copy)
            leave(act, act_stage)

            enter(act, S_MLS)
            ml_act(PT)
            for h in range(MH):
                act.wait_ge(c_tr, h + 1)
                act.activation(CNS[:, :, 0:128], ps[:, 0:2, :].rearrange("p b (s d) -> p (b s) d", s=4), ACT.Copy)
                act.activation(CNS[:, :, 128:129], NCOL.rearrange("p (b h) -> p b h", h=MH)[:, :, h:h + 1], ACT.Copy).then_inc(c_ev, 1)
                act.wait_ge(m_o, PT + h + 1)
                act.activation(NUM[:, PT, h], ps[:, 4, 0:129], ACT.Copy).then_inc(m_num, 1)
                act.wait_ge(m_num, PT + h + 1)
                square(PT, h)
                act.wait_ge(c_ct, h + 2)
                act.activation(CRAW[h].rearrange("p (a b) d -> p a (b d)", a=2), ps[:, 0:2, :], ACT.Copy).then_inc(c_ctev, 1)
            act.wait_ge(c_ct, MH + 2)
            act.activation(NROW[0:32, :], ps[0:32, 2, 0:P], ACT.Copy)
            act.activation(KWB.rearrange("p (a b) d -> p a (b d)", a=2)[0:27], ps[0:27, 5:7, :], ACT.Copy).then_inc(c_o, 1)
            leave(act, act_stage)

            enter(act, S_MLH)
            hi_of(act, OUT0, free=True)
            hi_of(act, OUT0 + 1, free=True)
            act.wait_ge(h_mean, 1)
            act.activation(RD, SSQ, ACT.Sqrt).then_inc(h_root, 1)
            leave(act, act_stage)

            enter(act, S_OUT0)
            out_act(act, 0, (FQ, MO))
            leave(act, act_stage)
            enter(act, S_NORM1)
            norm_act(act, 1, own)
            leave(act, act_stage)
            enter(act, S_FF0)
            mlp_act(act, 0, MLP0, HID0)
            leave(act, act_stage)
            enter(act, S_NORM2)
            norm_act(act, 2, own)
            leave(act, act_stage)

            enter(act, S_PROJ1)
            for j in range(16):
                if j % 2 == 0:
                    hi_of(act, ODD + j // 2 + 1)
                act.wait_ge(fm_ready, 20 + j + 1)
                if j < 4:
                    act.activation(as_groups(GQ[:, j]), group(j), ACT.Copy, scale=GK ** -0.5).then_inc(fm_taken, 1)
                elif j < 8:
                    act.activation(as_groups(GKT[:, j - 4]), group(j), ACT.Copy).then_inc(fm_taken, 1)
                else:
                    act.activation(as_groups(GG[:, j - 8]), group(j), ACT.Silu).then_inc(fm_taken, 1)
            for m in range(ODD + 8, GATES1):
                hi_of(act, m + 1)
            act.wait_ge(gate_ready, 2)
            act.activation(as_groups(GAT)[0:16], ps[0:16, 0:3, 0:GN], ACT.Copy)
            leave(act, act_stage)

            enter(act, S_CB)
            tmp = fm(5)
            for m in range(4):
                act.wait_ge(a_l, m + 1)
                act.activation(as_groups(CB[:, m]), group(m), ACT.Identity, bias=b_gla[:, m:m + 1]).then_inc(a_e, 1)
            for m in range(4):
                act.wait_ge(a_cb, m + 1)
                link(act, act_own, own, act.activation(tmp[:, m], tmp[:, m], ACT.Exp))
                act.activation(tmp[:, m], tmp[:, m], ACT.Ln, bias=1.0).then_inc(a_e, 1)
            leave(act, act_stage)

            enter(act, S_GLA)

            def gla_exp(n):
                act.wait_ge(l_d, 2 * n + 1)
                first = 0 if n < PT else 3
                act.activation(EL[n % 2][:, first:].rearrange("p l h t -> p (l h t)"),
                               EL[n % 2][:, first:].rearrange("p l h t -> p (l h t)"), ACT.Exp).then_inc(l_e, 1)

            def gla_exp_state(n):
                act.wait_ge(l_d, 2 * n + 2)
                act.activation(KS.rearrange("p h t -> p (h t)"), KS.rearrange("p h t -> p (h t)"), ACT.Exp).then_inc(l_eb, 1)
                if n >= 1:
                    act.wait_ge(l_o, n)
                cb = CB[:, :, n * P:(n + 1) * P]
                act.activation(QE, cb, ACT.Exp)
                if n < PT:
                    act.activation(ecl[:, n % 2, :, 0:1], cb[:, :, P - 1:P], ACT.Exp).then_inc(l_eb, 1)
                else:
                    act.activation(ecl[:, n % 2], cb[:, :, STEP - 1:P:STEP], ACT.Exp).then_inc(l_eb, 1)

            def gla_norm(n):
                act.wait_ge(l_o, n + 1 if n < PT else PT + GH)
                for h in range(GH):
                    link(act, act_own, own, act.activation(junk256, ps[:, 4 + h // 2, (h % 2) * GV:(h % 2 + 1) * GV], ACT.Square,
                                                           scale=GV ** -0.5, accum_out=osum[:, h:h + 1]))
                link(act, act_own, own, act.activation(osum[:, 4:8], osum[:, 0:4], ACT.Ln, bias=eps))
                link(act, act_own, own, act.activation(osum[:, 4:8], osum[:, 4:8], ACT.Exp, scale=-0.5))
                if n >= 1:
                    act.wait_ge(l_otr, n)
                for h in range(GH):
                    last = act.activation(OO[:, h], ps[:, 4 + h // 2, (h % 2) * GV:(h % 2 + 1) * GV], ACT.Copy,
                                          scale=osum[:, 4 + h:5 + h])
                last.then_inc(l_osc, 1)

            def gla_keys(n):
                act.wait_ge(l_kt, n + 1)
                act.activation(KST.rearrange("p h t -> p (h t)"), ps[:, 6, :], ACT.Copy).then_inc(l_ktev, 1)

            gla_exp(0)
            for n in range(PT):
                gla_exp_state(n)
                if n >= 1:
                    act.wait_ge(l_u, n)
                gla_keys(n)
                if n + 1 < PT:
                    gla_exp(n + 1)
                gla_norm(n)
            leave(act, act_stage)

            enter(act, S_GLAS)
            gla_exp(PT)
            gla_exp_state(PT)
            gla_keys(PT)
            gla_norm(PT)
            leave(act, act_stage)

            enter(act, S_OUT1)
            out_act(act, 1, (GG[:, 0:4], GG[:, 4:8]))
            leave(act, act_stage)
            enter(act, S_NORM3)
            norm_act(act, 3, own)
            leave(act, act_stage)
            enter(act, S_FF1)
            mlp_act(act, 1, MLP1, HID1)
            leave(act, act_stage)

            enter(act, S_FINAL)
            for n in range(NT):
                root_mean_square(act, own, unit(2, D, D), tokens(6)[:, n], n)

        @block.vector
        def _(dve):
            own = [0]

            def after(ins):
                link(dve, dve_own, own, ins)

            dve.memset(eps, EPS)
            leave(dve, dve_stage)
            norm_dve(dve, 0)
            leave(dve, dve_stage)

            enter(dve, S_PROJ0)

            def conv(j):
                dve.wait_ge(fm_taken, j + 1)
                u, v = conv_in(j), conv_out(j)
                for tap in range(1, TAPS):
                    w = conv_w[:, tap, j:j + 1]
                    first = dve.scalar_tensor_tensor(out=v[:, 0:SEQ], in0=u[:, tap:tap + SEQ], scalar=w, in1=v[:, 0:SEQ],
                                                     op0=ALU.mult, op1=ALU.add)
                    second = dve.scalar_tensor_tensor(out=sample(v), in0=conv_seq(j)[:, :, tap:tap + STEP], scalar=w,
                                                      in1=sample(v), op0=ALU.mult, op1=ALU.add)
                    if tap < TAPS - 1:
                        after(second)
                dve.tensor_copy(convstate[:, j, 0:3], u[:, SEQ:SEQ + 3])
                dve.tensor_copy(convstate[:, j, 3:27].rearrange("p (b t) -> p b t", b=NSEQ),
                                conv_seq(j)[:, :, STEP:STEP + 3]).then_inc(conv_done, 1)

            for j in range(KC):
                conv(j)

            def pieces(first):
                for j in range(first, first + 4 * NT):
                    dve.wait_ge(tmj_ready, j + 1)
                    if j >= 3:
                        dve.wait_ge(piece_out[j % 3], 16 * (j // 3))
                    dve.tensor_copy(PIECE_ST[j % 3], ps[:, 6 + j % 2, 0:COLS]).then_inc(tmj_taken, 1)

            pieces(0)
            leave(dve, dve_stage)

            enter(dve, S_GATES)
            dve.scalar_tensor_tensor(out=TF[0:8, :], in0=RF[0:8, :], scalar=-1.0, in1=RF[0:8, :], op0=ALU.mult, op1=ALU.min)
            dve.scalar_tensor_tensor(out=TM_[0:4, :], in0=RM[0:4, :], scalar=-1.0, in1=RM[0:4, :], op0=ALU.mult,
                                     op1=ALU.min).then_inc(g_a, 1)
            for row in (FN, BM, IB, MM):
                dve.memset(row, 0.0)
            dve.memset(ONES, 1.0)
            after(dve.memset(RESET, 1.0))
            dve.memset(RESET[:, starts(0)], 0.0)
            after(dve.memset(RESET[:, starts(1)], 0.0))
            dve.wait_ge(gate_in, 64)
            dve.wait_ge(g_b, 1)
            dve.scalar_tensor_tensor(out=LF[0:8, :], in0=RF[0:8, :], scalar=0.0, in1=TF[0:8, :], op0=ALU.min, op1=ALU.subtract)
            after(dve.scalar_tensor_tensor(out=LM[0:4, :], in0=RM[0:4, :], scalar=0.0, in1=TM_[0:4, :], op0=ALU.min,
                                           op1=ALU.subtract))
            dve.tensor_tensor_scan(FN[0:8, 0:SEQ], ONES[0:8, :], LF[0:8, 0:SEQ], 0.0, ALU.mult, ALU.subtract)
            B_ = TF
            after(dve.tensor_tensor_scan(B_[0:4, :], RESET[0:4, :], LM[0:4, :], 0.0, ALU.mult, ALU.add))
            after(dve.tensor_copy(TM_[0:4, :], RI[0:4, :]))
            after(dve.tensor_tensor(IB[0:4, :], RI[0:4, :], B_[0:4, :], ALU.subtract))
            for cols, m0 in ((slice(0, 1), mbefore[0:4, 0:1]), (slice(SEQ, T, STEP), mbefore[0:4, 1:9])):
                after(dve.tensor_tensor(RM[0:4, cols], LM[0:4, cols], m0, ALU.add))
                after(dve.tensor_tensor(TM_[0:4, cols], RM[0:4, cols], RI[0:4, cols], ALU.max))
                after(dve.memset(LM[0:4, cols], -BIG))
            after(dve.tensor_tensor_scan(MM[0:4, :], LM[0:4, :], TM_[0:4, :], 0.0, ALU.add, ALU.max))
            after(dve.tensor_tensor(BM[0:4, :], B_[0:4, :], MM[0:4, :], ALU.subtract))
            after(dve.memset(GL, 0.0))
            after(dve.tensor_copy(GL[0:4, 0:P], BM[0:4, 0:P]))
            dve.tensor_tensor(GL[0:4, P:SEQ].rearrange("p (n t) -> p n t", t=P), BM[0:4, P:SEQ].rearrange("p (n t) -> p n t", t=P),
                              MM[0:4, P - 1:SEQ - 1:P].unsqueeze(2).broadcast_to([4, PT - 1, P]), ALU.add)
            dve.tensor_tensor(sample(GL)[0:4], sample(BM)[0:4],
                              mbefore[0:4, 1:9].unsqueeze(2).broadcast_to([4, NSEQ, STEP]), ALU.add).then_inc(g_rows, 1)
            leave(dve, dve_stage)

            enter(dve, S_FOX)

            def row_of(j):
                return (stat[:, c + j % 4:c + 1 + j % 4] for c in (16, 4, 8, 12))

            def biggest(j, inverse_too):
                h, q = fox_jobs[j] if j < NJ else (0, 0)
                if j < NJ:
                    dve.wait_ge(f_s, j + 1)
                    top, negative = list(row_of(j))[:2]
                    src = ps[:, 2 * (j % 2):2 * (j % 2) + 2, :].rearrange("p b k -> p (b k)")[:, 0:(q + 1) * P]
                    own[0] += 1
                    dve.tensor_reduce(top, src, AX.X, ALU.max).then_inc(dve_own, 1)
                    found = own[0]
                if inverse_too:
                    total, inverse_ = list(row_of(j - 2))[2:]
                    own[0] += 1
                    dve.reciprocal(inverse_, total).then_inc(dve_own, 1)
                if j < NJ:
                    dve.wait_ge(dve_own, found)
                    dve.tensor_scalar(negative, top, -1.0, None, ALU.mult).then_inc(f_mx, 1)
                return own[0]

            def probs_out(j):
                h, q = fox_jobs[j]
                w = (q + 1) * P
                dve.wait_ge(f_pt, j + 1)
                if j >= 2:
                    dve.wait_ge(f_o, j - 1)
                dve.tensor_copy(PTS[j % 2][:, 0:w], ps[:, 4:6, :].rearrange("p b k -> p (b k)")[:, 0:w]).then_inc(f_pts, 1)

            def output(j, inverted):
                h, q = fox_jobs[j]
                dve.wait_ge(f_o, j + 1)
                dve.wait_ge(dve_own, inverted)
                dve.tensor_scalar(otok[:, q, h * FD:(h + 1) * FD], ps[:, 6 + j % 2, 0:FD], list(row_of(j))[3], None,
                                  ALU.mult).then_inc(f_oev, 1)

            dve.wait_ge(fk_out[0], 16 * 5)
            dve.wait_ge(fk_out[1], 16 * 4)
            biggest(0, False)
            for j in range(NJ):
                inverted = biggest(j + 1, j >= 1)
                probs_out(j)
                if j >= 1:
                    output(j - 1, inverted)
            output(NJ - 1, biggest(NJ + 1, True))
            leave(dve, dve_stage)

            enter(dve, S_FOXS)
            dve.tensor_copy(KT[:, :, 256:384], FK[:, :, SEQ:T])
            dve.wait_ge(pastlf_in, 32)
            dve.wait_ge(s_q, 1)
            plf = PLF.rearrange("p (b j h) -> p b j h", b=NSEQ, j=2)
            after(dve.tensor_tensor(LNEW.rearrange("p (h q) -> p h q", q=STEP), lfT[:, PT].unsqueeze(2).broadcast_to([P, FH, STEP]),
                                    mask(C_C16, 16).unsqueeze(1).broadcast_to([P, FH, STEP]), ALU.mult))

            def seq_queries(b):
                LP = LOG_F[b % 2]
                if b >= 2:
                    dve.wait_ge(s_s, b - 1)
                t = slice(SEQ + b * STEP, SEQ + (b + 1) * STEP)
                for r in range(2):
                    dve.tensor_copy(QB[b % 2][64 * r:64 * r + 64].rearrange("p (c x) -> p c x", x=160)[:, :, r * 16:r * 16 + 16],
                                    FQ[64 * r:64 * r + 64, :, t])
                for jt in range(2):
                    dve.tensor_copy(LP[:, jt].rearrange("p (h q) -> p h q", q=STEP),
                                    plf[:, b, jt].unsqueeze(2).broadcast_to([P, FH, STEP]))
                dve.tensor_scalar(LP[:, 2], LNEW, mask(C_IND + b, 1), None, ALU.mult).then_inc(s_q, 1)

            def seq_max(b):
                dve.wait_ge(s_s, b + 1)
                after(dve.tensor_reduce(stat[:, 0:1], ps[:, 2 + b % 2, 0:384], AX.X, ALU.max))
                dve.tensor_scalar(stat[:, 1:2], stat[:, 0:1], -1.0, None, ALU.mult).then_inc(s_mx, 1)

            seq_queries(0)
            seq_queries(1)
            seq_max(0)
            for b in range(NSEQ):
                dve.wait_ge(s_p, b + 1)
                after(dve.reciprocal(stat[:, 3:4], stat[:, 2:3]))
                dve.tensor_scalar(SP, SP, stat[:, 3:4], None, ALU.mult).then_inc(s_pn, 1)
                if b + 1 < NSEQ:
                    seq_max(b + 1)
                if b + 2 < NSEQ:
                    seq_queries(b + 2)
                dve.wait_ge(s_o, b + 1)
                t = slice(SEQ + b * STEP, SEQ + (b + 1) * STEP)
                for r in range(2):
                    last = dve.tensor_copy(FQ[64 * r:64 * r + 64, :, t],
                                           ps[64 * r:64 * r + 64, 6, 0:128].rearrange("p (c x) -> p c x", x=32)[:, :, 16 * r:16 * r + 16])
                last.then_inc(s_oev, 1)
            leave(dve, dve_stage)

            enter(dve, S_ML)

            def ml_dve(n, m):
                t = slice(n * P, (n + 1) * P)
                dve.wait_ge(m_b, n + 1)
                dve.tensor_tensor(WT, ps[:, 0, :].rearrange("p (h t) -> p h t", h=MH),
                                  mask(m).unsqueeze(1).broadcast_to([P, MH, P]), ALU.add).then_inc(m_dm, 1)
                dve.wait_ge(m_g, n + 1)
                if n >= 1:
                    dve.wait_ge(m_o, n)
                dve.tensor_tensor(QG, MQ[:, :, t], GB, ALU.mult)
                dve.wait_ge(m_w, n + 1)
                dve.wait_ge(m_in, n + 1)
                dve.tensor_tensor(AT, WT, ps[:, 2, :].rearrange("p (h t) -> p h t", h=MH), ALU.mult).then_inc(m_a, 1)

            for n in range(PT):
                if n >= 1:
                    dve.wait_ge(m_a, n)
                ml_dve(n, C_MC)
                if n >= 1:
                    dve.wait_ge(m_u, n)
                for h in range(MH):
                    last = dve.tensor_scalar(KW[:, h], ps[:, 3, h * P:(h + 1) * P], WT[:, h, P - 1:P], None, ALU.mult)
                last.then_inc(m_kw, 1)
                dve.wait_ge(m_u, n + 1)
                for h in range(MH):
                    last = dve.scalar_tensor_tensor(out=CN[:, h], in0=CN[:, h], scalar=GB[:, h, P - 1:P],
                                                    in1=ps[:, 6 + h // 2, (h % 2) * 129:(h % 2 + 1) * 129],
                                                    op0=ALU.mult, op1=ALU.add)
                if n < PT - 1:
                    last.then_inc(m_cn, 1)
                else:
                    after(last)
            dve.tensor_copy(NNEW[:, 32:36].unsqueeze(2), CN[:, :, 128:129]).then_inc(m_cn, 1)
            leave(dve, dve_stage)

            enter(dve, S_MLS)
            dve.wait_ge(out_done, 16 * 6)
            ml_dve(PT, C_MB)
            dve.tensor_copy(KW.rearrange("p h t -> p (h t)"), ps[:, 3, :]).then_inc(m_kw, 1)
            dve.wait_ge(m_kw, PT + 1)
            for h in range(MH):
                if h >= 1:
                    dve.wait_ge(m_o, PT + h)
                    dve.wait_ge(c_u, h)
                dve.tensor_copy(QGB.rearrange("p (b x) -> p b x", x=144)[:, :, 0:STEP],
                                QG[:, h].rearrange("p (b t) -> p b t", b=NSEQ)).then_inc(c_qg, 1)
                for b in range(NSEQ):
                    e = b * STEP + STEP - 1
                    last = dve.tensor_scalar(KWB[:, b], KW[:, h], WT[:, h, e:e + 1], None, ALU.mult)
                last.then_inc(c_kw, 1)
                dve.wait_ge(c_u, h + 1)
                for b in range(NSEQ):
                    e = b * STEP + STEP - 1
                    last = dve.scalar_tensor_tensor(out=CNS[:, b], in0=CNS[:, b], scalar=GB[:, h, e:e + 1],
                                                    in1=ps[:, 5 + b // 3, (b % 3) * 129:(b % 3 + 1) * 129],
                                                    op0=ALU.mult, op1=ALU.add)
                after(last)
                dve.tensor_copy(NNEW[:, 0:32].rearrange("p (b h) -> p b h", h=MH)[:, :, h:h + 1], CNS[:, :, 128:129]).then_inc(c_cn, 1)
            leave(dve, dve_stage)

            enter(dve, S_MLH)
            dve.wait_ge(mo_back, 16)
            den4 = NUM[:, :, :, 128:129].rearrange("p n h o -> p (n h) o")
            RD3 = RD.unsqueeze(2)
            after(dve.scalar_tensor_tensor(out=RD3, in0=den4, scalar=-1.0, in1=den4, op0=ALU.mult, op1=ALU.max))
            after(dve.tensor_tensor(RD, RD, enmT.rearrange("p n h -> p (n h)"), ALU.max))
            after(dve.reciprocal(HSC, RD))
            after(dve.tensor_tensor(SSQ, SSQ, HSC, ALU.mult))
            after(dve.tensor_tensor(SSQ, SSQ, HSC, ALU.mult))
            dve.tensor_scalar(SSQ, SSQ, 1.0 / MD, EPS, ALU.mult, ALU.add).then_inc(h_mean, 1)
            dve.wait_ge(h_root, 1)
            after(dve.reciprocal(RD, RD))
            after(dve.tensor_tensor(HSC, HSC, RD, ALU.mult))

            def mix(n):
                dve.wait_ge(h_tr, n + 1)
                for h in range(MH):
                    v = MO[:, h, n * P:(n + 1) * P]
                    last = dve.scalar_tensor_tensor(out=v, in0=ps[:, n % 4, h * P:(h + 1) * P], scalar=g_ml[:, h:h + 1], in1=v,
                                                    op0=ALU.mult, op1=ALU.mult)
                last.then_inc(h_mix, 1)

            for n in range(NT):
                if n >= 2:
                    mix(n - 2)
                dve.tensor_tensor(HST[:, n % 2].rearrange("p (h d) -> p h d", h=MH), NUM[:, n, :, 0:128],
                                  HSC[:, n * MH:(n + 1) * MH].unsqueeze(2).broadcast_to([P, MH, MD]), ALU.mult).then_inc(h_hs, 1)
            mix(NT - 2)
            mix(NT - 1)
            leave(dve, dve_stage)

            enter(dve, S_OUT0)
            out_dve(dve, 0, tokens(2), (FQ, MO))
            leave(dve, dve_stage)
            enter(dve, S_NORM1)
            norm_dve(dve, 1)
            leave(dve, dve_stage)
            enter(dve, S_FF0)
            mlp_dve(dve, 0, tokens(2), HID0)
            leave(dve, dve_stage)
            enter(dve, S_NORM2)
            norm_dve(dve, 2)
            leave(dve, dve_stage)

            enter(dve, S_PROJ1)
            pieces(4 * NT)
            leave(dve, dve_stage)

            enter(dve, S_CB)
            tmp = fm(5)
            for m in range(4):
                dve.wait_ge(a_e, m + 1)
                dve.scalar_tensor_tensor(out=tmp[:, m], in0=CB[:, m], scalar=-1.0, in1=CB[:, m], op0=ALU.mult,
                                         op1=ALU.min).then_inc(a_cb, 1)
            dve.wait_ge(a_pre, 1)
            for m in range(4):
                dve.wait_ge(a_e, 4 + m + 1)
                after(dve.scalar_tensor_tensor(out=tmp[:, m], in0=CB[:, m], scalar=0.0, in1=tmp[:, m], op0=ALU.min,
                                               op1=ALU.subtract))
                after(dve.tensor_scalar(tmp[:, m], tmp[:, m], 1.0 / TAU, None, ALU.mult))
                dve.tensor_tensor_scan(CB[:, m], RESET, tmp[:, m], 0.0, ALU.mult, ALU.add)
            leave(dve, dve_stage)

            enter(dve, S_GLA)

            def gla_factors(n):
                t = slice(n * P, (n + 1) * P)
                dve.wait_ge(l_e, n + 1)
                for l, w in enumerate(LEVELS):
                    if n == PT and w > 8:
                        continue
                    e = EL[n % 2][:, l].rearrange("p h (n w) -> p h n w", w=2 * w)
                    k = GKT[:, :, t].rearrange("p h (n w) -> p h n w", w=2 * w)
                    q = GQ[:, :, t].rearrange("p h (n w) -> p h n w", w=2 * w)
                    dve.tensor_tensor(e[:, :, :, 0:w], e[:, :, :, 0:w], k[:, :, :, 0:w], ALU.mult)
                    last = dve.tensor_tensor(e[:, :, :, w:2 * w], e[:, :, :, w:2 * w], q[:, :, :, w:2 * w], ALU.mult)
                last.then_inc(l_m, 1)

            def gla_state_factors(n):
                t = slice(n * P, (n + 1) * P)
                dve.wait_ge(l_eb, 2 * n + 1)
                dve.tensor_tensor(KS, KS, GKT[:, :, t], ALU.mult).then_inc(l_ks, 1)
                dve.wait_ge(l_eb, 2 * n + 2)
                if n < PT:
                    dve.tensor_tensor(QE, QE, GQ[:, :, t], ALU.mult).then_inc(l_qe, 1)
                else:
                    after(dve.tensor_tensor(QE, QE, GQ[:, :, t], ALU.mult))

            def gla_levels(n, h):
                q = levels_turn(n, h)
                first = 0 if n < PT else 3
                dve.wait_ge(l_a, 4 * n + h + 1)
                if n >= 1 and h == 0:
                    dve.wait_ge(l_o, n)
                b = 2 * (q % 2)
                src = ps[:, b:b + 2, :].rearrange("p b (l t) -> p (b l) t", t=P)
                if n or h:
                    dve.wait_ge(l_at, 4 * n + h)
                dve.tensor_tensor(LT[:, first:], src[:, first:], sel[:, first:], ALU.mult).then_inc(l_free, 1)
                dve.wait_ge(l_free, q + 1)
                dve.tensor_reduce(LA[:, h], LT[:, first:].rearrange("p l t -> p t l"), AX.X, ALU.add).then_inc(l_at, 1)

            def gla_mix(n):
                q = output_turn(n)
                dve.wait_ge(l_otr, n + 1)
                for c in range(8):
                    v = GG[:, c, n * P:(n + 1) * P]
                    last = dve.scalar_tensor_tensor(out=v, in0=ps[:, 2 * (q % 2) + c // 4, (c % 4) * P:(c % 4 + 1) * P],
                                                    scalar=g_gla[:, c:c + 1], in1=v, op0=ALU.mult, op1=ALU.mult)
                last.then_inc(l_free, 1)

            gla_factors(0)
            for n in range(PT):
                for h in range(n > 0, 2):
                    gla_levels(n, h)
                gla_state_factors(n)
                for h in range(2, GH):
                    gla_levels(n, h)
                if n + 1 < PT:
                    gla_factors(n + 1)
                dve.wait_ge(l_u, n + 1)
                for h in range(GH):
                    dve.scalar_tensor_tensor(out=SS[:, h], in0=SS[:, h], scalar=ecl[:, n % 2, h, 0:1],
                                             in1=ps[:, 6 + h // 2, (h % 2) * GV:(h % 2 + 1) * GV],
                                             op0=ALU.mult, op1=ALU.add).then_inc(l_sn, 1)
                if n + 1 < PT:
                    gla_levels(n + 1, 0)
                gla_mix(n)
            leave(dve, dve_stage)

            enter(dve, S_GLAS)
            dve.wait_ge(l_v, 1)
            gla_factors(PT)
            gla_state_factors(PT)
            for h in range(GH):
                gla_levels(PT, h)
            dve.wait_ge(l_ktev, PT + 1)
            for h in range(GH):
                if h >= 1:
                    dve.wait_ge(l_o, PT + h)
                    dve.wait_ge(l_u, PT + NSEQ * h)
                dve.tensor_copy(QEB.rearrange("p (b x) -> p b x", x=144)[:, :, 0:STEP],
                                QE[:, h].rearrange("p (b t) -> p b t", b=NSEQ)).then_inc(l_qe, 1)
                for b in range(NSEQ):
                    last = dve.tensor_scalar(KEB[:, b], KST[:, h], mask(C_IND + b, 1), None, ALU.mult)
                last.then_inc(l_keb, 1)
                if h >= 2:
                    dve.wait_ge(st_out[h % 2], 32 * (h // 2))
                for b in range(NSEQ):
                    g = NSEQ * h + b
                    dve.wait_ge(l_u, PT + g + 1)
                    dve.scalar_tensor_tensor(out=SNEW[h % 2][:, b // 4, b % 4], in0=SIN[h % 2][:, b // 4, b % 4],
                                             scalar=ecl[:, PT % 2, h, b:b + 1], in1=state_bank(g),
                                             op0=ALU.mult, op1=ALU.add).then_inc(l_sn, 1)
            gla_mix(PT)
            leave(dve, dve_stage)

            enter(dve, S_OUT1)
            out_dve(dve, 1, tokens(6), (GG[:, 0:4], GG[:, 4:8]))
            leave(dve, dve_stage)
            enter(dve, S_NORM3)
            norm_dve(dve, 3)
            leave(dve, dve_stage)
            enter(dve, S_FF1)
            mlp_dve(dve, 1, tokens(6), HID1)
            leave(dve, dve_stage)

            enter(dve, S_FINAL)
            dve.wait_ge(gain_in, 16 * 5)
            for n in range(NT):
                inverse(dve, NT * 4 + n)
                dve.wait_ge(root_ready, NT * 4 + n + 1)
                if n >= 4:
                    dve.wait_ge(y_out[n % 4], 16 * (n // 4))
                dve.scalar_tensor_tensor(out=unit(0, D, (n % 4) * D), in0=tokens(6)[:, n], scalar=rstd[:, n:n + 1],
                                         in1=unit(2, D), op0=ALU.mult, op1=ALU.mult).then_inc(y_ready, 1)


INPUTS = ["x_prompt", "x_sample", "cache_fox_k", "cache_fox_v", "cache_fox_logf", "state_mlstm_c", "state_mlstm_n",
          "state_mlstm_m", "state_mlstm_conv", "state_gla_s", "norm_mix", "norm_ffn", "norm_final", "w_in_even",
          "b_fox_f", "conv_w_ml", "conv_b_ml", "b_ml_i", "b_ml_f", "g_ml", "w_in_odd", "w_gla_a2", "b_gla_a", "g_gla",
          "w_out", "w_ff1", "w_ff2"]
OUTPUTS = {
    "y_prompt": (1, SEQ, D), "y_sample": (NSEQ, STEP, D),
    "p_fox_k": (1, 1, SEQ, FH, FD), "p_fox_v": (1, 1, SEQ, FH, FD), "p_fox_logf": (1, 1, SEQ, FH),
    "p_mlstm_c": (1, 1, MH, MD, MD), "p_mlstm_n": (1, 1, MH, MD), "p_mlstm_m": (1, 1, MH),
    "p_mlstm_conv": (1, 1, 3, D), "p_gla_s": (1, 1, GH, GK, GV),
    "s_fox_k": (1, NSEQ, STEP, FH, FD), "s_fox_v": (1, NSEQ, STEP, FH, FD), "s_fox_logf": (1, NSEQ, STEP, FH),
    "s_mlstm_c": (1, NSEQ, MH, MD, MD), "s_mlstm_n": (1, NSEQ, MH, MD), "s_mlstm_m": (1, NSEQ, MH),
    "s_mlstm_conv": (1, NSEQ, 3, D), "s_gla_s": (1, NSEQ, GH, GK, GV),
}


def kernel(**inputs):
    import concourse.bacc as bacc
    from concourse.bass_utils import run_bass_kernel_spmd

    nc = bacc.Bacc("TRN2", target_bir_lowering=False, num_devices=1, dynamic_dma_scratch_size=2048)
    arrays, i, o = {}, {}, {}
    for name in INPUTS:
        arrays[name] = np.ascontiguousarray(inputs[name])
    arrays.update(constants())
    for name, a in arrays.items():
        i[name] = nc.dram_tensor(name, a.shape, F32, kind="ExternalInput").ap()
    for name, shape in OUTPUTS.items():
        o[name] = nc.dram_tensor("out_" + name, shape, F32, kind="ExternalOutput").ap()
    scratch = nc.dram_tensor("stream", (P, NT * D), F32, kind="Internal").ap()
    park_mo = nc.dram_tensor("park_mo", (P, 4, T), F32, kind="Internal").ap()
    park_mv = nc.dram_tensor("park_mv", (T, MH * MD), F32, kind="Internal").ap()
    park_gv = nc.dram_tensor("park_gv", (T, GH * GV), F32, kind="Internal").ap()
    streaming_step(nc, i, o, scratch, park_mo, park_mv, park_gv)
    r = run_bass_kernel_spmd(nc, [arrays], core_ids=[0])
    return tuple(r.results[0]["out_" + name] for name in OUTPUTS)
```
